# Optimizing a Trainium2 kernel written in Bass

```python
import math
import jax
import jax.numpy as jnp
from jax import lax
import numpy as np

D_MODEL = 1024
BATCH = 1
SEQ = 512
DEPTH = 2

GRID_W = 64
CTX_LEN = 256
N_MIXERS = 3
N_MOD = 9
EPS = 1e-6
ROPE_BASE = 10000.0
D_FF = 128 * ((8 * D_MODEL + 3 * 128 - 1) // (3 * 128))

MLA_HEADS = D_MODEL // 128
MLA_NOPE = 128
MLA_ROPE = 64
MLA_V = 128
MLA_Q_RANK = 3 * D_MODEL // 8
MLA_KV_RANK = D_MODEL // 4
Q_BLOCK = 128

RET_HEADS = D_MODEL // 256
RET_DK = 256
RET_DV = 512
RET_CHUNK = 128

S5_GROUP = 16
S5_GROUPS = D_MODEL // S5_GROUP
S5_STATE = 64
S5_CHUNK = 128
DT_MIN = 1e-3
DT_MAX = 1e-1

N_MLA = (DEPTH + N_MIXERS - 1) // N_MIXERS
N_RET = (DEPTH + N_MIXERS - 2) // N_MIXERS
N_S5 = (DEPTH + N_MIXERS - 3) // N_MIXERS

kernel_name = 'hybrid_mla_retention_s5_dit'

def rms_norm(x, gain):
    xf = x.astype(jnp.float32)
    y = xf * lax.rsqrt(jnp.mean(xf * xf, axis=-1, keepdims=True) + EPS)
    return (y * gain.astype(jnp.float32)).astype(x.dtype)

def pre_norm(z, gain, mod, k):
    return rms_norm(z, gain) * (1 + mod[:, 3 * k + 1]) + mod[:, 3 * k]

def swiglu(x, w_in, w_out):
    a, b = jnp.split(x @ w_in, 2, axis=-1)
    return (jax.nn.silu(a) * b) @ w_out

def flip(a):
    return jnp.flip(a, axis=1)

def rope_angles(pos, dim):
    inv_freq = ROPE_BASE ** (-jnp.arange(0, dim, 2, dtype=jnp.float32) / dim)
    return pos.astype(jnp.float32)[:, None] * inv_freq[None, :]

def apply_rotary(x, ang):
    cos = jnp.cos(ang)[:, None, :]
    sin = jnp.sin(ang)[:, None, :]
    x1, x2 = jnp.split(x.astype(jnp.float32), 2, axis=-1)
    return jnp.concatenate([x1 * cos - x2 * sin, x2 * cos + x1 * sin], axis=-1).astype(x.dtype)

def grid_angles(n_tok, dim):
    rows = n_tok // GRID_W
    row = jnp.repeat(jnp.arange(rows), GRID_W)
    col = jnp.tile(jnp.arange(GRID_W), rows)
    return rope_angles(row, dim // 2), rope_angles(col, dim // 2)

def axial_rotary(x, angs):
    ang_row, ang_col = angs
    half = x.shape[-1] // 2
    return jnp.concatenate([apply_rotary(x[..., :half], ang_row), apply_rotary(x[..., half:], ang_col)], axis=-1)

def mla_qk_norm(x, gain):
    return jnp.concatenate([rms_norm(x[..., :MLA_NOPE], gain[:MLA_NOPE]),
                            rms_norm(x[..., MLA_NOPE:], gain[MLA_NOPE:])], axis=-1)

def mla_queries(cq, q_norm, w_uq, q_gain, angs):
    b, t, _ = cq.shape
    q = (rms_norm(cq, q_norm) @ w_uq).reshape(b, t, MLA_HEADS, MLA_NOPE + MLA_ROPE)
    q = mla_qk_norm(q, q_gain)
    if angs is None:
        return q
    return jnp.concatenate([q[..., :MLA_NOPE], axial_rotary(q[..., MLA_NOPE:], angs)], axis=-1)

def mla_keys_values(ckv, k_rope, kv_norm, w_ukv, k_gain, angs):
    b, t, _ = ckv.shape
    kv = (rms_norm(ckv, kv_norm) @ w_ukv).reshape(b, t, MLA_HEADS, MLA_NOPE + MLA_V)
    k_nope = rms_norm(kv[..., :MLA_NOPE], k_gain[:MLA_NOPE])
    k_rope = rms_norm(k_rope, k_gain[MLA_NOPE:])[:, :, None, :]
    if angs is not None:
        k_rope = axial_rotary(k_rope, angs)
    k = jnp.concatenate([k_nope, jnp.broadcast_to(k_rope, (b, t, MLA_HEADS, MLA_ROPE))], axis=-1)
    return k, kv[..., MLA_NOPE:]

def attend(q, k, v):
    s = jnp.einsum('bqhd,bkhd->bhqk', q, k, preferred_element_type=jnp.float32) * (q.shape[-1] ** -0.5)
    p = jax.nn.softmax(s, axis=-1).astype(v.dtype)
    return jnp.einsum('bhqk,bkhd->bqhd', p, v)

def blocked_attend(q, k, v):
    b, t, h, dk = q.shape
    nb = t // Q_BLOCK
    qb = q.reshape(b, nb, Q_BLOCK, h, dk).swapaxes(0, 1)
    o = lax.map(lambda qi: attend(qi, k, v), qb)
    return o.swapaxes(0, 1).reshape(b, t, h, v.shape[-1])

def mla_mixer(hn, gn, need_ctx, w_in, q_norm, kv_norm, w_uq, w_ukv, q_gain, k_gain, w_o):
    b, s, _ = hn.shape
    l = gn.shape[1]
    cuts = [MLA_Q_RANK, MLA_Q_RANK + MLA_KV_RANK]
    angs = grid_angles(s, MLA_ROPE)
    cq_l, ckv_l, kr_l = jnp.split(hn @ w_in, cuts, axis=-1)
    q_l = mla_queries(cq_l, q_norm, w_uq, q_gain, angs)
    k_l, v_l = mla_keys_values(ckv_l, kr_l, kv_norm, w_ukv, k_gain, angs)
    if need_ctx:
        cq_c, ckv_c, kr_c = jnp.split(gn @ w_in, cuts, axis=-1)
    else:
        ckv_c, kr_c = jnp.split(gn @ w_in[:, MLA_Q_RANK:], [MLA_KV_RANK], axis=-1)
    k_c, v_c = mla_keys_values(ckv_c, kr_c, kv_norm, w_ukv, k_gain, None)
    k_all = jnp.concatenate([k_c, k_l], axis=1)
    v_all = jnp.concatenate([v_c, v_l], axis=1)
    y_l = blocked_attend(q_l, k_all, v_all).reshape(b, s, MLA_HEADS * MLA_V) @ w_o
    y_c = None
    if need_ctx:
        q_c = mla_queries(cq_c, q_norm, w_uq, q_gain, None)
        y_c = attend(q_c, k_c, v_c).reshape(b, l, MLA_HEADS * MLA_V) @ w_o
    return y_l, y_c

def ret_heads(a, dim):
    return a.reshape(a.shape[0], a.shape[1], RET_HEADS, dim)

def retention_scan(q, k, v, log_g, state0, strict):
    b, t, h, _ = q.shape
    dv = v.shape[-1]
    c = RET_CHUNK
    n = t // c
    idx = jnp.arange(c, dtype=jnp.float32)
    diff = idx[:, None] - idx[None, :]
    lower = diff > 0 if strict else diff >= 0
    intra = jnp.where(lower[None], jnp.exp(log_g[:, None, None] * jnp.maximum(diff, 0.0)[None]), 0.0)
    q_dec = jnp.exp(log_g[None, :] * (idx[:, None] + 1.0))[None, :, :, None]
    k_dec = jnp.exp(log_g[None, :] * (c - 1.0 - idx[:, None]))[None, :, :, None]
    chunk_dec = jnp.exp(log_g * c)[None, :, None, None]

    def chunks(a):
        return a.astype(jnp.float32).reshape(b, n, c, h, a.shape[-1]).swapaxes(0, 1)

    def step(state, inp):
        qc, kc, vc = inp
        scores = jnp.einsum('bihd,bjhd->bhij', qc, kc) * intra[None]
        o = jnp.einsum('bhij,bjhe->bihe', scores, vc) + jnp.einsum('bihd,bhde->bihe', qc * q_dec, state)
        state = state * chunk_dec + jnp.einsum('bjhd,bjhe->bhde', kc * k_dec, vc)
        return state, o

    _, o = lax.scan(step, state0, (chunks(q), chunks(k), chunks(v)))
    return o.swapaxes(0, 1).reshape(b, t, h, dv)

def retention_state(k, v, log_g, expo):
    w = jnp.exp(expo[:, None] * log_g[None, :])
    return jnp.einsum('lh,blhd,blhe->bhde', w, k.astype(jnp.float32), v.astype(jnp.float32))

def retention_out(o, gate, gn_gain, w_o):
    b, t = o.shape[:2]
    mu = jnp.mean(o, axis=-1, keepdims=True)
    var = jnp.mean(jnp.square(o - mu), axis=-1, keepdims=True)
    on = ((o - mu) * lax.rsqrt(var + EPS)).reshape(b, t, RET_HEADS * RET_DV)
    y = on * gn_gain.astype(jnp.float32) * jax.nn.silu(gate.astype(jnp.float32))
    return y.astype(w_o.dtype) @ w_o

def retention_mixer(hn, gn, need_ctx, w_in, log1m_gamma, gn_gain, w_o):
    b, s, _ = hn.shape
    l = gn.shape[1]
    hdk, hdv = RET_HEADS * RET_DK, RET_HEADS * RET_DV
    cuts = [hdk, 2 * hdk, 2 * hdk + hdv]
    log_g = jnp.log1p(-jnp.exp(log1m_gamma.astype(jnp.float32)))
    scale = RET_DK ** -0.5
    q_l, k_l, v_l, gate_l = jnp.split(hn @ w_in, cuts, axis=-1)
    ang = rope_angles(jnp.arange(s), RET_DK)
    q_l = apply_rotary(ret_heads(q_l, RET_DK), ang)
    k_l = apply_rotary(ret_heads(k_l, RET_DK), ang) * scale
    v_l = ret_heads(v_l, RET_DV)
    if need_ctx:
        q_c, k_c, v_c, gate_c = jnp.split(gn @ w_in, cuts, axis=-1)
    else:
        k_c, v_c = jnp.split(gn @ w_in[:, hdk:2 * hdk + hdv], [hdk], axis=-1)
    k_c = ret_heads(k_c, RET_DK) * scale
    v_c = ret_heads(v_c, RET_DV)
    pos_c = jnp.arange(l, dtype=jnp.float32)
    s_fwd = retention_state(k_c, v_c, log_g[0], (l - 1) - pos_c)
    s_bwd = retention_state(k_c, v_c, log_g[1], pos_c)
    o_l = (retention_scan(q_l, k_l, v_l, log_g[0], s_fwd, False)
           + flip(retention_scan(flip(q_l), flip(k_l), flip(v_l), log_g[1], s_bwd, True)))
    y_l = retention_out(o_l, gate_l, gn_gain, w_o)
    y_c = None
    if need_ctx:
        q_c = ret_heads(q_c, RET_DK)
        zero = jnp.zeros_like(s_fwd)
        o_c = (retention_scan(q_c, k_c, v_c, log_g[0], zero, False)
               + flip(retention_scan(flip(q_c), flip(k_c), flip(v_c), log_g[1], zero, True)))
        y_c = retention_out(o_c, gate_c, gn_gain, w_o)
    return y_l, y_c

def s5_discretise(lam_re, lam_im, log_dt, b_re, b_im, c_re, c_im):
    f32 = jnp.float32
    lam = lax.complex(lam_re.astype(f32), lam_im.astype(f32))
    a_log = lam * jnp.exp(log_dt.astype(f32))[:, None]
    b_bar = ((jnp.exp(a_log) - 1.0) / lam)[..., None] * lax.complex(b_re.astype(f32), b_im.astype(f32))
    c_mat = lax.complex(c_re.astype(f32), c_im.astype(f32))
    return a_log, b_bar, c_mat

def ssm_combine(e1, e2):
    a1, b1 = e1
    a2, b2 = e2
    return a1 * a2, a2 * b1 + b2

def s5_state(u, a_log, b_bar, expo):
    pw = jnp.exp(a_log[None] * expo[:, None, None])
    return jnp.einsum('lgp,gpm,blgm->bgp', pw, b_bar, u.astype(jnp.complex64))

def s5_scan(u, a_log, b_bar, c_mat, h0):
    b, t, g, m = u.shape
    n = t // S5_CHUNK
    a_bar = jnp.exp(a_log)

    def step(h_prev, uc):
        bu = jnp.einsum('gpm,bcgm->bcgp', b_bar, uc.astype(jnp.complex64))
        a_cum, h_loc = lax.associative_scan(ssm_combine, (jnp.broadcast_to(a_bar, bu.shape), bu), axis=1)
        hs = h_loc + a_cum * h_prev[:, None]
        y = jnp.einsum('gmp,bcgp->bcgm', c_mat, hs).real
        return hs[:, -1], y

    _, y = lax.scan(step, h0, u.reshape(b, n, S5_CHUNK, g, m).swapaxes(0, 1))
    return y.swapaxes(0, 1).reshape(b, t, g, m)

def s5_out(y, glu_w, glu_b):
    z = jax.nn.gelu(y).astype(glu_w.dtype)
    a, gate = jnp.split(z @ glu_w + glu_b, 2, axis=-1)
    return a * jax.nn.sigmoid(gate)

def s5_mixer(hn, gn, need_ctx, lam_re, lam_im, log_dt, b_re, b_im, c_re, c_im, d_skip, glu_w, glu_b):
    b, s, d = hn.shape
    l = gn.shape[1]
    fwd = s5_discretise(lam_re[0], lam_im[0], log_dt[0], b_re[0], b_im[0], c_re[0], c_im[0])
    bwd = s5_discretise(lam_re[1], lam_im[1], log_dt[1], b_re[1], b_im[1], c_re[1], c_im[1])
    u_l = hn.astype(jnp.float32).reshape(b, s, S5_GROUPS, S5_GROUP)
    u_c = gn.astype(jnp.float32).reshape(b, l, S5_GROUPS, S5_GROUP)
    d_g = d_skip.astype(jnp.float32).reshape(S5_GROUPS, S5_GROUP)
    pos_c = jnp.arange(l, dtype=jnp.float32)
    h_fwd = s5_state(u_c, fwd[0], fwd[1], (l - 1) - pos_c)
    h_bwd = s5_state(u_c, bwd[0], bwd[1], pos_c)
    y_l = s5_scan(u_l, *fwd, h_fwd) + flip(s5_scan(flip(u_l), *bwd, h_bwd)) + d_g * u_l
    out_l = s5_out(y_l.reshape(b, s, d), glu_w, glu_b)
    out_c = None
    if need_ctx:
        zero = jnp.zeros_like(h_fwd)
        y_c = s5_scan(u_c, *fwd, zero) + flip(s5_scan(flip(u_c), *bwd, zero)) + d_g * u_c
        out_c = s5_out(y_c.reshape(b, l, d), glu_w, glu_b)
    return out_l, out_c

def setup_inputs(seed: int = 0) -> dict:
    key = jax.random.key(seed)
    keys = iter(jax.random.split(key, 40))
    f32 = jnp.float32

    def nrm(shape, std):
        return jax.random.normal(next(keys), shape, f32) * std

    def gain(shape):
        return 1.0 + nrm(shape, 0.01)

    d = D_MODEL
    hq = MLA_HEADS * (MLA_NOPE + MLA_ROPE)
    hkv = MLA_HEADS * (MLA_NOPE + MLA_V)
    hdk, hdv = RET_HEADS * RET_DK, RET_HEADS * RET_DV
    gp = (N_S5, 2, S5_GROUPS, S5_STATE)
    decay0 = -(5.0 + jnp.arange(RET_HEADS, dtype=f32)) * math.log(2.0)
    return {
        'x': nrm((BATCH, SEQ, d), 1.0),
        'c': nrm((BATCH, d), 1.0),
        'ctx': nrm((BATCH, CTX_LEN, d), 1.0),
        'c_ctx': nrm((d,), 1.0),
        'ada_w': nrm((DEPTH, d, N_MOD * d), 0.5 * d ** -0.5),
        'ada_b': nrm((DEPTH, N_MOD * d), 0.01),
        'norm_g': gain((DEPTH, 3, d)),
        'ffn_w_in': nrm((DEPTH, 2, d, 2 * D_FF), d ** -0.5),
        'ffn_w_out': nrm((DEPTH, 2, D_FF, d), D_FF ** -0.5),
        'mla_w_in': nrm((N_MLA, d, MLA_Q_RANK + MLA_KV_RANK + MLA_ROPE), d ** -0.5),
        'mla_q_norm': gain((N_MLA, MLA_Q_RANK)),
        'mla_kv_norm': gain((N_MLA, MLA_KV_RANK)),
        'mla_w_uq': nrm((N_MLA, MLA_Q_RANK, hq), MLA_Q_RANK ** -0.5),
        'mla_w_ukv': nrm((N_MLA, MLA_KV_RANK, hkv), MLA_KV_RANK ** -0.5),
        'mla_q_gain': gain((N_MLA, MLA_NOPE + MLA_ROPE)),
        'mla_k_gain': gain((N_MLA, MLA_NOPE + MLA_ROPE)),
        'mla_w_o': nrm((N_MLA, MLA_HEADS * MLA_V, d), (MLA_HEADS * MLA_V) ** -0.5),
        'ret_w_in': nrm((N_RET, d, 2 * hdk + 2 * hdv), d ** -0.5),
        'ret_log1m_gamma': jnp.broadcast_to(decay0, (N_RET, 2, RET_HEADS)) + nrm((N_RET, 2, RET_HEADS), 0.05),
        'ret_gn_gain': gain((N_RET, hdv)),
        'ret_w_o': nrm((N_RET, hdv, d), hdv ** -0.5),
        's5_lam_re': -0.5 + nrm(gp, 0.01),
        's5_lam_im': jnp.pi * jnp.arange(S5_STATE, dtype=f32) + nrm(gp, 0.01),
        's5_log_dt': jax.random.uniform(next(keys), (N_S5, 2, S5_GROUPS), f32, math.log(DT_MIN), math.log(DT_MAX)),
        's5_b_re': nrm(gp + (S5_GROUP,), (2 * S5_GROUP) ** -0.5),
        's5_b_im': nrm(gp + (S5_GROUP,), (2 * S5_GROUP) ** -0.5),
        's5_c_re': nrm((N_S5, 2, S5_GROUPS, S5_GROUP, S5_STATE), S5_STATE ** -0.5),
        's5_c_im': nrm((N_S5, 2, S5_GROUPS, S5_GROUP, S5_STATE), S5_STATE ** -0.5),
        's5_d': nrm((N_S5, d), 1.0),
        's5_glu_w': nrm((N_S5, d, 2 * d), d ** -0.5),
        's5_glu_b': nrm((N_S5, 2 * d), 0.01),
    }

def reference(x, c, ctx, c_ctx, ada_w, ada_b, norm_g, ffn_w_in, ffn_w_out,
              mla_w_in, mla_q_norm, mla_kv_norm, mla_w_uq, mla_w_ukv, mla_q_gain, mla_k_gain, mla_w_o,
              ret_w_in, ret_log1m_gamma, ret_gn_gain, ret_w_o,
              s5_lam_re, s5_lam_im, s5_log_dt, s5_b_re, s5_b_im, s5_c_re, s5_c_im, s5_d, s5_glu_w, s5_glu_b):
    b, s, d = x.shape
    silu_c = jax.nn.silu(c)
    silu_cc = jax.nn.silu(c_ctx)[None, :]
    h, g = x, ctx
    for i in range(DEPTH):
        last = i == DEPTH - 1
        kind, j = i % N_MIXERS, i // N_MIXERS
        mod_l = (silu_c @ ada_w[i] + ada_b[i]).reshape(b, N_MOD, 1, d)
        mod_c = (silu_cc @ ada_w[i] + ada_b[i]).reshape(1, N_MOD, 1, d)
        h = h + 0.5 * mod_l[:, 2] * swiglu(pre_norm(h, norm_g[i, 0], mod_l, 0), ffn_w_in[i, 0], ffn_w_out[i, 0])
        g = g + 0.5 * mod_c[:, 2] * swiglu(pre_norm(g, norm_g[i, 0], mod_c, 0), ffn_w_in[i, 0], ffn_w_out[i, 0])
        hn = pre_norm(h, norm_g[i, 1], mod_l, 1)
        gn = pre_norm(g, norm_g[i, 1], mod_c, 1)
        if kind == 0:
            y_l, y_c = mla_mixer(hn, gn, not last, mla_w_in[j], mla_q_norm[j], mla_kv_norm[j], mla_w_uq[j],
                                 mla_w_ukv[j], mla_q_gain[j], mla_k_gain[j], mla_w_o[j])
        elif kind == 1:
            y_l, y_c = retention_mixer(hn, gn, not last, ret_w_in[j], ret_log1m_gamma[j], ret_gn_gain[j], ret_w_o[j])
        else:
            y_l, y_c = s5_mixer(hn, gn, not last, s5_lam_re[j], s5_lam_im[j], s5_log_dt[j], s5_b_re[j], s5_b_im[j],
                                s5_c_re[j], s5_c_im[j], s5_d[j], s5_glu_w[j], s5_glu_b[j])
        h = h + mod_l[:, 5] * y_l
        h = h + 0.5 * mod_l[:, 8] * swiglu(pre_norm(h, norm_g[i, 2], mod_l, 2), ffn_w_in[i, 1], ffn_w_out[i, 1])
        if not last:
            g = g + mod_c[:, 5] * y_c
            g = g + 0.5 * mod_c[:, 8] * swiglu(pre_norm(g, norm_g[i, 2], mod_c, 2), ffn_w_in[i, 1], ffn_w_out[i, 1])
    return h


_drawn_inputs = setup_inputs


def setup_inputs(seed=0):
    import zlib

    import numpy as np

    out = dict(_drawn_inputs(seed))
    spreads = {}
    factors = {'ada_b': 4.193,
     'norm_g': 8.0,
     'mla_q_norm': 8.0,
     'mla_kv_norm': 8.0,
     'mla_q_gain': 8.0,
     'mla_k_gain': 8.0,
     'ret_gn_gain': 8.0}
    for name, (base, spread) in spreads.items():
        noise = np.random.default_rng([zlib.crc32(name.encode()), seed]).standard_normal(out[name].shape)
        drawn = base * np.exp(spread * noise) if base else spread * noise
        out[name] = jnp.asarray(drawn.astype(out[name].dtype))
    for name, factor in factors.items():
        out[name] = (out[name] * factor).astype(out[name].dtype)
    return out
```

```python
from contextlib import ExitStack, contextmanager

import numpy as np
import concourse.bass as bass
from concourse import mybir

F32 = mybir.dt.float32
F32R = mybir.dt.float32r
ACT = mybir.ActivationFunctionType
ALU = mybir.AluOpType
AX_X = mybir.AxisListType.X

P = 128
D = 1024
KD = D // P
S, L = 512, 256
T = S + L
D_FF = P * ((8 * D + 3 * P - 1) // (3 * P))
BLOCKS = D_FF // (2 * P)
UNIT = 2048
N_MOD = 9
EPS = 1e-6
HEADS, NOPE, ROPE, DV = 8, 128, 64, 128
Q_RANK, KV_RANK = 384, 256
PAIRS = HEADS // 2
RET_HEADS, RET_DK, RET_DV = 4, 256, 512
FFN_UNITS = 3 * BLOCKS
MLA_PRE_UNITS, MLA_PAIR_UNITS, RET_UNITS = 3, 4, 8
N_UNITS = 4 * FFN_UNITS + MLA_PRE_UNITS + MLA_PAIR_UNITS * PAIRS + RET_UNITS * RET_HEADS
ADA_UNITS = 2 * N_MOD * D // 256
ADA_FIRST = 3 * D // 256
ADA_A, ADA_B = 3, 2
ADA_MID = ADA_UNITS - ADA_FIRST - (ADA_A + ADA_B) * BLOCKS
STREAMS = ((0, S), (S, L))

_cols = {}
_at = 0
for _name, _n in (("c", KD * 2), ("ada_b", 2 * N_MOD * KD * 2), ("norm_g", 6 * KD * 2), ("q_norm", 3), ("kv_norm", 2),
                  ("qg_nope", 1), ("qg_rope", 1), ("kg_nope", 1), ("kg_rope", 1), ("gn", 16), ("log1m", 8)):
    _cols[_name] = (_at, _at + _n)
    _at += _n
N_VEC = _at
DIST_W = 896


class Count:

    def __init__(self):
        self.n, self.i, self.per = {}, None, {}

    def ahead(self, sem, n):
        k = self.n.get(sem.name, 0) + n
        if self.i is None or not self.per.get(sem.name):
            return k
        return self.i * self.per[sem.name] + k

    def next(self, sem, n=1):
        v = self.ahead(sem, n)
        self.n[sem.name] = self.n.get(sem.name, 0) + n
        return v

    @contextmanager
    def loop(self, eng, times, per):
        before = dict(self.n)
        self.per = {s.name: v for s, v in per.items()}
        with eng.Fori(0, times) as i:
            self.i = i
            yield i
        took = {k: v - before.get(k, 0) for k, v in self.n.items() if v != before.get(k, 0)}
        assert took == self.per, f"an iteration takes {took}"
        for k, v in took.items():
            self.n[k] = before.get(k, 0) + v * times
        self.i, self.per = None, {}


def build(nc, weights, ada, vecs, consts, x_in, rope_mla, rope_ret, dist_in, out):
    with ExitStack() as ctx:
        def sb(name, shape, dt=F32, where=ctx):
            return where.enter_context(nc.sbuf_tensor(name, shape, dt))

        def sem(name):
            return ctx.enter_context(nc.semaphore(name))

        ps = ctx.enter_context(nc.psum_tensor("ps", [P, 8, 512], F32))

        h = sb("h", [P, KD, T])
        xnh = sb("xnh", [P, KD, T], F32R)
        xnl = sb("xnl", [P, KD, T], F32R)
        raw = sb("raw", [P, 2, UNIT])
        wh = sb("wh", [P, 2, UNIT], F32R)
        wl = sb("wl", [P, 2, UNIT], F32R)
        mats = sb("mats", [P, 4, P])
        ones, ones64, swap, ident = (mats[:, i, :] for i in range(4))
        vec = sb("vec", [P, N_VEC])
        mods = sb("mods", [P, 2 * N_MOD * KD, 2])
        coef = sb("coef", [P, 2, KD, 2])
        c_act = sb("c_act", [P, KD, 2])
        lg = sb("lg", [P, 5, 8])
        row = sb("row", [P, 4, 2])
        eps = sb("eps", [P, 1])

        def v(name):
            a, b = _cols[name]
            return vec[:, a:b]

        ffn_mem = ExitStack()
        hidh = sb("hidh", [P, 2, 2, T], F32R, ffn_mem)
        hidl = sb("hidl", [P, 2, 2, T], F32R, ffn_mem)
        act_buf = sb("act_buf", [P, 2, T], F32, ffn_mem)
        ssum = sb("ssum", [P, T], F32, ffn_mem)
        rstd = sb("rstd", [P, T], F32, ffn_mem)
        adaw = sb("adaw", [P, 2, UNIT], F32, ffn_mem)
        ffn_mem.close()
        mla_mem = ExitStack()
        cqn = sb("cqn", [P, 2, 3, T], F32R, mla_mem)
        ckvn = sb("ckvn", [P, 2, 2, T], F32R, mla_mem)
        krr = sb("krr", [P, 2, T], F32R, mla_mem)
        qrr = sb("qrr", [P, 2, T], F32R, mla_mem)
        qn = sb("qn", [P, 2, 2, T], F32R, mla_mem)
        kn = sb("kn", [P, 2, 2, T], F32R, mla_mem)
        cs = sb("cs", [P, 2, S], F32, mla_mem)
        sqb = sb("sqb", [P, T], F32, mla_mem)
        nrm = sb("nrm", [P, 3, T], F32, mla_mem)
        mla_mem.close()
        ret_mem = ExitStack()
        rq = sb("rq", [P, 2, 2, S], F32R, ret_mem)
        rk = sb("rk", [P, 2, 2, T], F32R, ret_mem)
        rv = sb("rv", [P, 2, 6, 256], F32R, ret_mem)
        st = sb("st", [P, 2, 6, S], F32R, ret_mem)
        cr = sb("cr", [P, 2, S], F32, ret_mem)
        dist = sb("dist", [P, DIST_W], F32, ret_mem)
        dec = sb("dec", [P, 4, S], F32, ret_mem)
        rt = sb("rt", [P, 3, S], F32, ret_mem)
        rrs = sb("rrs", [P, S], F32, ret_mem)
        ret_mem.close()
        dec_flat = dec[:].rearrange("p a t -> p (a t)")
        rt_flat = rt[:].rearrange("p a t -> p (a t)")
        dec_lat, dec_ctx = dec_flat[:, 0:DIST_W], dec_flat[:, DIST_W:DIST_W + 640]
        xf = [t[:].rearrange("p k t -> p (k t)") for t in (xnh, xnl)]
        pt = [t[:, 0:3072].rearrange("p (k q) -> p k q", k=6) for t in xf]
        vv = [t[:, 3072:4608].rearrange("p (k e) -> p k e", k=6) for t in xf]
        oo = [t[:, 4608:6144].rearrange("p (j t) -> p j t", j=2) for t in xf]

        loaded = sem("loaded")
        raw_full = [sem(f"raw_full{s}") for s in range(2)]
        w_hi = [sem(f"w_hi{s}") for s in range(2)]
        w_ready = [sem(f"w_ready{s}") for s in range(2)]
        ada_full = [sem(f"ada_full{s}") for s in range(2)]
        ada_psum, ada_evac = sem("ada_psum"), sem("ada_evac")
        tab_full = sem("tab_full")
        dve_step = sem("dve_step")
        setup_done = sem("setup_done")
        sq_done, sq_added, ms_full, std_done = sem("sq_done"), sem("sq_added"), sem("ms_full"), sem("std_done")
        prod_done, xn_hi, xn_ready = sem("prod_done"), sem("xn_hi"), sem("xn_ready")
        glu_full, silu_done, hid_done = sem("glu_full"), sem("silu_done"), sem("hid_done")
        hid_hi, hid_ready = sem("hid_hi"), sem("hid_ready")
        y_full, y_added = sem("y_full"), sem("y_added")
        item_full, item_sq, item_ms, item_std = sem("item_full"), sem("item_sq"), sem("item_ms"), sem("item_std")
        item_v, item_swapped, item_rot = sem("item_v"), sem("item_swapped"), sem("item_rot")
        item_hi, item_ready = sem("item_hi"), sem("item_ready")
        v_full, v_hi, v_ready = sem("v_full"), sem("v_hi"), sem("v_ready")
        s_full, max_done, exp_done, p_done = sem("s_full"), sem("max_done"), sem("exp_done"), sem("p_done")
        pt_full, pt_hi, pt_ready = sem("pt_full"), sem("pt_hi"), sem("pt_ready")
        o_full, o_hi, o_ready = sem("o_full"), sem("o_hi"), sem("o_ready")
        lg_ready, lg_step = sem("lg_ready"), sem("lg_step")
        dec_exp, dec_done = sem("dec_exp"), sem("dec_done")
        qk_full, qk_val, qk_hi, qk_ready = sem("qk_full"), sem("qk_val"), sem("qk_hi"), sem("qk_ready")
        sc_full, sc_val, sc_hi, sc_ready = sem("sc_full"), sem("sc_val"), sem("sc_hi"), sem("sc_ready")
        osum_ready, mu_full, cen_done = sem("osum_ready"), sem("mu_full"), sem("cen_done")
        vsq_done, vsq_added, var_full, rstd_done = sem("vsq_done"), sem("vsq_added"), sem("var_full"), sem("rstd_done")
        g_full, g_silu, g_val, g_hi, g_ready = sem("g_full"), sem("g_silu"), sem("g_val"), sem("g_hi"), sem("g_ready")
        stored = sem("stored")

        def mod_col(layer, which):
            a = (layer * N_MOD + which) * KD
            return mods[:, a:a + KD, :]

        block = ctx.enter_context(nc.Block())

        @block.sync
        def _(sp):
            c = Count()
            sp.dma_start(vec[:], vecs).then_inc(loaded, 16)
            sp.dma_start(mats[:], consts).then_inc(loaded, 16)
            sp.dma_start(h[:], x_in).then_inc(loaded, 16)
            for s in range(2):
                sp.dma_start(raw[:, s, :], weights[s]).then_inc(raw_full[s], 16)
            with c.loop(sp, (N_UNITS - 2) // 2, {w_ready[0]: 1, w_ready[1]: 1}) as i:
                for s in range(2):
                    sp.wait_ge(w_ready[s], c.next(w_ready[s]))
                    sp.dma_start(raw[:, s, :], weights[bass.ds(i * 2 + (2 + s), 1)].rearrange("u p e -> (u p) e")
                                 ).then_inc(raw_full[s], 16)
            if N_UNITS % 2:
                sp.wait_ge(w_ready[0], c.next(w_ready[0]))
                sp.dma_start(raw[:, 0, :], weights[N_UNITS - 1]).then_inc(raw_full[0], 16)
            c.next(y_added, KD * (3 * BLOCKS + PAIRS + RET_HEADS + BLOCKS - 1))
            for m in range(KD):
                sp.wait_ge(y_added, c.next(y_added))
                sp.dma_start(out[m], h[:, m, 0:S]).then_inc(stored, 16)
            sp.wait_ge(stored, 16 * KD)

        @block.gpsimd
        def _(pool):
            c = Count()
            for s in range(2):
                pool.dma_start(adaw[:, s, :], ada[s]).then_inc(ada_full[s], 16)

            def ada_loop(first, times):
                with c.loop(pool, times, {ada_psum: 2}) as i:
                    for j in range(2):
                        s = (first + j) % 2
                        pool.wait_ge(ada_psum, c.next(ada_psum))
                        pool.dma_start(adaw[:, s, :], ada[bass.ds(i * 2 + (first + j), 1)].rearrange("u p e -> (u p) e")
                                       ).then_inc(ada_full[s], 16)
            mid = ADA_FIRST + ADA_A * BLOCKS + ADA_MID
            assert mid % 2 == 0 and ADA_UNITS % 2 == 0
            ada_loop(2, (mid - 2) // 2)
            c.next(ada_psum, 2)
            c.next(xn_ready, KD)
            pool.wait_ge(xn_ready, c.next(xn_ready, KD))
            pool.dma_start(cs[:], rope_mla).then_inc(tab_full, 16)
            pool.wait_ge(xn_ready, c.next(xn_ready, KD))
            for s in range(2):
                pool.dma_start(adaw[:, s, :], ada[mid + s]).then_inc(ada_full[s], 16)
            ada_loop(mid + 2, (ADA_UNITS - mid - 2) // 2)
            pool.wait_ge(xn_ready, c.next(xn_ready, 2 * KD))
            pool.dma_start(cr[:], rope_ret).then_inc(tab_full, 16)
            pool.dma_start(dist[:], dist_in).then_inc(tab_full, 16)

        @block.tensor
        def _(pe):
            c = Count()
            mm = nc.tensor.matmul

            def three(dst, lhs, rhs, first, last, rows=slice(0, P)):
                mm(dst, lhs[1][rows], rhs[0][rows], start=first, stop=False)
                mm(dst, lhs[0][rows], rhs[1][rows], start=False, stop=False)
                return mm(dst, lhs[0][rows], rhs[0][rows], start=False, stop=last)

            def w(s, a, n=P):
                return wh[:, s, a:a + n], wl[:, s, a:a + n]

            def xn(k, a, n):
                return xnh[:, k, a:a + n], xnl[:, k, a:a + n]

            def ada_units(first, n):
                for u in range(n):
                    s = (first + u) % 2
                    pe.wait_ge(ada_full[s], c.next(ada_full[s], 16))
                    for j in range(2):
                        for k in range(KD):
                            a = k * 256 + j * P
                            ins = mm(ps[:, 5, 4 * u + 2 * j:4 * u + 2 * j + 2], adaw[:, s, a:a + P], c_act[:, k, :],
                                     start=(k == 0), stop=(k == KD - 1))
                    ins.then_inc(ada_psum, 1)

            def mean_square():
                pe.wait_ge(sq_added, c.next(sq_added, KD))
                mm(ps[:, 6, :], ones, ssum[:, 0:S], start=True, stop=True)
                mm(ps[:, 7, 0:L], ones, ssum[:, S:T], start=True, stop=True).then_inc(ms_full, 1)

            def ffn(n_streams, ada_per, ada_first, slot):
                streams = STREAMS[:n_streams]

                def up(j, s, first=False, wait_hid=True, wait_y=False, wait_ada=False):
                    pe.wait_ge(w_ready[s], c.next(w_ready[s]))
                    if wait_hid:
                        pe.wait_ge(hid_done, c.next(hid_done))
                    if wait_ada:
                        pe.wait_ge(ada_evac, c.next(ada_evac))
                    for g, (half, bank, col, (t0, n)) in enumerate(
                            [(1, 3 * j + 1, 0, STREAMS[0]), (0, 3 * j, 0, STREAMS[0])] +
                            [(0, 3 * j + 2, 0, STREAMS[1]), (1, 3 * j + 2, L, STREAMS[1])] * (n_streams - 1)):
                        if g == 1 and wait_y:
                            pe.wait_ge(y_added, c.next(y_added, 2))
                        for k in range(KD):
                            if first and g == 0:
                                pe.wait_ge(xn_ready, c.next(xn_ready))
                            ins = three(ps[:, bank, col:col + n], w(s, k * 256 + half * P), xn(k, t0, n),
                                        k == 0, k == KD - 1)
                    ins.then_inc(glu_full, 1)

                def down(par, s, after=2):
                    pe.wait_ge(w_ready[s], c.next(w_ready[s]))
                    pe.wait_ge(hid_ready, c.next(hid_ready, 2))
                    for m in range(KD):
                        if m == 1:
                            pe.wait_ge(hid_done, c.ahead(hid_done, min(after, 1)))
                        if m >= 2:
                            pe.wait_ge(y_added, c.next(y_added))
                        for i, (t0, n) in enumerate(streams):
                            bank = (0, 2)[i] if m % 2 else 6 + i
                            for kk in range(2):
                                ins = three(ps[:, bank, 0:n], w(s, kk * D + m * P),
                                            (hidh[:, par, kk, t0:t0 + n], hidl[:, par, kk, t0:t0 + n]), kk == 0, kk == 1)
                        ins.then_inc(y_full, 1)

                s0, s1 = slot, 1 - slot
                up(0, s0, first=True, wait_hid=False)
                up(1, s1, wait_hid=False)
                pre = 0
                if ada_per:
                    pe.wait_ge(hid_done, c.ahead(hid_done, 2))
                    ada_units(ada_first, ada_per)
                    pre = ada_per

                per = {w_ready[0]: 3, w_ready[1]: 3, hid_done: 4, y_added: 16, hid_ready: 4}
                if ada_per:
                    per.update({ada_full[0]: 16 * ada_per, ada_full[1]: 16 * ada_per, ada_evac: 2})
                with c.loop(pe, BLOCKS // 2, per):
                    up(0, s0)
                    up(1, s1, wait_ada=bool(ada_per))
                    down(0, s0)
                    if ada_per:
                        pe.wait_ge(hid_done, c.ahead(hid_done, 2))
                        ada_units(ada_first + pre, ada_per)
                    up(0, s1, wait_y=True)
                    up(1, s0, wait_ada=bool(ada_per))
                    down(1, s1)
                    if ada_per:
                        pe.wait_ge(hid_done, c.ahead(hid_done, 2))
                        ada_units(ada_first + pre + ada_per, ada_per)
                    pe.wait_ge(y_added, c.next(y_added, 2))
                down(0, s0)
                pe.wait_ge(y_added, c.next(y_added, 2))
                c.next(hid_done, 2)
                if ada_per:
                    pe.wait_ge(ada_evac, c.next(ada_evac))
                return 1 - slot

            pe.wait_ge(loaded, 48)
            pe.wait_ge(setup_done, c.next(setup_done))
            ada_units(0, ADA_FIRST)
            pe.wait_ge(ada_evac, c.next(ada_evac))
            mean_square()
            slot = ffn(2, ADA_A, ADA_FIRST, 0)
            ada_units(ADA_FIRST + ADA_A * BLOCKS, ADA_MID)
            c.next(ada_evac)
            mean_square()

            sets = ((0, 1), (2, 3), (4, 5))

            def project(n_item, lhs, rhs, ks, s=None, first=False):
                if n_item >= 3:
                    pe.wait_ge(item_v, c.next(item_v))
                for i, (t0, n) in enumerate(STREAMS):
                    for k in range(ks):
                        if first and i == 0:
                            pe.wait_ge(xn_ready, c.next(xn_ready))
                        ins = three(ps[:, sets[n_item % 3][i], 0:n], lhs(k), rhs(k, t0, n), k == 0, k == ks - 1)
                ins.then_inc(item_full, 1)

            def w_in(s, j):
                return lambda k: w(s, k * 256 + j * P)

            s0, s1 = slot, 1 - slot
            pe.wait_ge(w_ready[s0], c.next(w_ready[s0]))
            for n_item in range(6):
                s = (s0, s1, s0)[n_item // 2]
                if n_item in (2, 4):
                    pe.wait_ge(w_ready[s], c.next(w_ready[s]))
                project(n_item, w_in(s, n_item % 2), xn, KD, first=(n_item == 0))
                if n_item in (0, 1, 2):
                    pe.wait_ge(item_sq, c.next(item_sq))
                    mm(ps[:, 6, :], ones, sqb[:, 0:S], start=(n_item == 0), stop=(n_item == 2))
                    mm(ps[:, 7, 0:L], ones, sqb[:, S:T], start=(n_item == 0), stop=(n_item == 2)).then_inc(item_ms, 1)
                if n_item in (3, 4, 5):
                    pe.wait_ge(item_sq, c.next(item_sq))
                    if n_item in (3, 5):
                        pe.wait_ge(item_std, c.next(item_std))
                    mat = ones64 if n_item == 5 else ones
                    mm(ps[:, 6, :], mat, sqb[:, 0:S], start=(n_item != 4), stop=(n_item != 3))
                    mm(ps[:, 7, 0:L], mat, sqb[:, S:T], start=(n_item != 4), stop=(n_item != 3)).then_inc(item_ms, 1)
            pe.wait_ge(item_std, c.next(item_std))
            pe.wait_ge(item_v, c.next(item_v, 3))
            mm(ps[:, 6, :], swap, nrm[:, 2, 0:S], start=True, stop=True).then_inc(item_swapped, 1)
            pe.wait_ge(item_ready, c.next(item_ready, 6))
            c.next(item_rot)
            slot = s1

            tiles = [(hh, q) for hh in range(2) for q in (4, 5, 0, 1, 2, 3)]

            def scores(n, hh, q):
                if n >= 2:
                    pe.wait_ge(exp_done, c.next(exp_done))
                b = 2 * (n % 2)
                qs = slice(q * P, q * P + P)
                for t0, n_key in (STREAMS if q < 4 else STREAMS[1:]):
                    bank = ps[:, b + (t0 > 0), 0:n_key]
                    ks = slice(t0, t0 + n_key)
                    half = slice(ROPE * hh, ROPE * hh + ROPE)
                    three(bank, (qn[:, 0, hh, qs], qn[:, 1, hh, qs]), (kn[:, 0, hh, ks], kn[:, 1, hh, ks]), True, False)
                    ins = three(bank, (qrr[:, 0, qs], qrr[:, 1, qs]), (krr[:, 0, ks], krr[:, 1, ks]), False, True, half)
                ins.then_inc(s_full, 1)

            def turn(n, hh, q):
                pe.wait_ge(p_done, c.next(p_done))
                if n >= 1:
                    pe.wait_ge(pt_ready, c.next(pt_ready))
                for kc in (range(6) if q < 4 else (4, 5)):
                    ins = nc.tensor.transpose(ps[:, 4 + kc // 4, (kc % 4) * P:(kc % 4) * P + P],
                                              nrm[:, n % 2, kc * P:kc * P + P], ident)
                ins.then_inc(pt_full, 1)

            def weigh(hh, context):
                keys, q0, n, bank = ((4, 5), L, L, 7) if context else (range(6), 0, S, 6)
                for kc in keys:
                    ins = three(ps[:, bank, 0:n], (vv[0][:, kc, hh * DV:hh * DV + DV], vv[1][:, kc, hh * DV:hh * DV + DV]),
                                (pt[0][:, kc, q0:q0 + n], pt[1][:, kc, q0:q0 + n]), kc == keys[0], kc == keys[-1])
                ins.then_inc(o_full, 1)

            s0, s1 = slot, 1 - slot
            with c.loop(pe, PAIRS, {w_ready[0]: 2, w_ready[1]: 2, item_v: 5, item_sq: 5, item_std: 5,
                                    item_ready: 5, item_rot: 1, v_ready: 6, exp_done: 12, p_done: 12, pt_ready: 12, o_ready: 4,
                                    y_added: 8}):
                pe.wait_ge(w_ready[s0], c.next(w_ready[s0]))
                cq = lambda k, t0, n: (cqn[:, 0, k, t0:t0 + n], cqn[:, 1, k, t0:t0 + n])
                ckv = lambda k, t0, n: (ckvn[:, 0, k, t0:t0 + n], ckvn[:, 1, k, t0:t0 + n])

                def head_sum(mat):
                    pe.wait_ge(item_sq, c.next(item_sq))
                    mm(ps[:, 6, :], mat, sqb[:, 0:S], start=True, stop=True)
                    mm(ps[:, 7, 0:L], mat, sqb[:, S:T], start=True, stop=True).then_inc(item_ms, 1)
                    pe.wait_ge(item_std, c.next(item_std))

                project(0, lambda k: w(s0, k * 384 + 256), cq, 3)
                project(1, lambda k: w(s0, k * 384), cq, 3)
                head_sum(ones64)
                project(2, lambda k: w(s0, k * 384 + 128), cq, 3)
                pe.wait_ge(item_v, c.next(item_v))
                mm(ps[:, 6, :], swap, nrm[:, 0, 0:S], start=True, stop=True).then_inc(item_swapped, 1)
                pe.wait_ge(item_rot, c.next(item_rot))
                head_sum(ones)
                pe.wait_ge(w_ready[s1], c.next(w_ready[s1]))
                for i, (t0, n) in enumerate(STREAMS):
                    for k in range(2):
                        ins = three(ps[:, sets[0][i], 0:n], w(s1, k * 512), ckv(k, t0, n), k == 0, k == 1)
                ins.then_inc(item_full, 1)
                head_sum(ones)
                pe.wait_ge(item_v, c.next(item_v))
                for i, (t0, n) in enumerate(STREAMS):
                    for k in range(2):
                        ins = three(ps[:, sets[1][i], 0:n], w(s1, k * 512 + P), ckv(k, t0, n), k == 0, k == 1)
                ins.then_inc(item_full, 1)
                head_sum(ones)
                pe.wait_ge(item_v, c.next(item_v))
                for tc in range(6):
                    if tc == 3:
                        head_sum(ones)
                    if tc >= 2:
                        pe.wait_ge(v_ready, c.next(v_ready))
                    for k in range(2):
                        ins = three(ps[:, 4 + tc % 2, 0:256], ckv(k, tc * P, P), w(s1, k * 512 + 256, 256),
                                    k == 0, k == 1)
                    ins.then_inc(v_full, 1)
                c.next(item_v, 2)
                pe.wait_ge(item_ready, c.next(item_ready, 5))
                pe.wait_ge(v_ready, c.next(v_ready, 2))
                scores(0, *tiles[0])
                for n, (hh, q) in enumerate(tiles):
                    if n + 1 < len(tiles):
                        scores(n + 1, *tiles[n + 1])
                    if q == 1:
                        weigh(hh, True)
                    if q == 4 and hh == 1:
                        pe.wait_ge(pt_ready, c.ahead(pt_ready, 1))
                        weigh(0, False)
                    turn(n, hh, q)
                    if q == 0 and hh == 1:
                        pe.wait_ge(o_ready, c.next(o_ready, 2))
                pe.wait_ge(pt_ready, c.next(pt_ready))
                weigh(1, False)
                c.next(exp_done, 2)
                pe.wait_ge(o_ready, c.next(o_ready, 2))
                pe.wait_ge(w_ready[s0], c.next(w_ready[s0]))
                pe.wait_ge(w_ready[s1], c.next(w_ready[s1]))
                for m in range(KD):
                    if m >= 2:
                        pe.wait_ge(y_added, c.next(y_added))
                    for i, (t0, n) in enumerate(STREAMS):
                        for kk, s in enumerate((s0, s1)):
                            ins = three(ps[:, (0, 2)[i] if m % 2 else 6 + i, 0:n], w(s, m * P),
                                        (oo[0][:, kk, t0:t0 + n], oo[1][:, kk, t0:t0 + n]), kk == 0, kk == 1)
                    ins.then_inc(y_full, 1)
                pe.wait_ge(y_added, c.next(y_added, 2))
            mean_square()
            slot = ffn(2, ADA_B, ADA_FIRST + ADA_A * BLOCKS + ADA_MID, slot)
            mean_square()
            slot = ffn(2, 0, 0, slot)
            mean_square()

            s0, s1 = slot, 1 - slot

            def values(s, banks, first):
                pe.wait_ge(w_ready[s], c.next(w_ready[s]))
                for tc in range(6):
                    if tc >= 2:
                        pe.wait_ge(v_ready, c.next(v_ready))
                    for k in range(KD):
                        ins = three(ps[:, banks[tc % 2], 0:256], xn(k, tc * P, P), w(s, k * 256, 256),
                                    k == 0, k == KD - 1)
                    ins.then_inc(v_full, 1)
                pe.wait_ge(v_ready, c.next(v_ready, 2))

            def outputs(half):
                for j in range(2):
                    for jc in range(6):
                        ins = three(ps[:, 4 + 2 * half + j, :], (rv[:, 0, jc, j * P:j * P + P], rv[:, 1, jc, j * P:j * P + P]),
                                    (st[:, 0, jc, :], st[:, 1, jc, :]), jc == 0, jc == 5)
                    ins.then_inc(o_full, 1)

            pe.wait_ge(xn_ready, c.next(xn_ready, KD))
            with c.loop(pe, RET_HEADS, {w_ready[0]: 4, w_ready[1]: 4, v_ready: 12, qk_ready: 2, sc_ready: 6,
                                        osum_ready: 1, cen_done: 1, vsq_added: 4, g_ready: 4, y_added: 8}):
                pe.wait_ge(w_ready[s0], c.next(w_ready[s0]))
                for j in range(2):
                    for k in range(KD):
                        ins = three(ps[:, j, :], w(s0, k * 256 + j * P), xn(k, 0, S), k == 0, k == KD - 1)
                ins.then_inc(qk_full, 1)
                pe.wait_ge(w_ready[s1], c.next(w_ready[s1]))
                for i, (t0, n) in enumerate(STREAMS):
                    for j in range(2):
                        for k in range(KD):
                            ins = three(ps[:, 2 + 2 * i + j, 0:n], w(s1, k * 256 + j * P), xn(k, t0, n), k == 0, k == KD - 1)
                ins.then_inc(qk_full, 1)
                values(s0, (6, 7), True)
                pe.wait_ge(qk_ready, c.next(qk_ready, 2))
                for jc in range(6):
                    if jc >= 4:
                        pe.wait_ge(sc_ready, c.next(sc_ready))
                    for k in range(2):
                        ins = three(ps[:, jc % 4, :], (rk[:, 0, k, jc * P:jc * P + P], rk[:, 1, k, jc * P:jc * P + P]),
                                    (rq[:, 0, k, :], rq[:, 1, k, :]), k == 0, k == 1)
                    ins.then_inc(sc_full, 1)
                pe.wait_ge(sc_ready, c.next(sc_ready, 4))
                outputs(0)
                values(s1, (0, 1), False)
                outputs(1)
                pe.wait_ge(w_ready[s0], c.next(w_ready[s0]))

                def gate(j, s, bank):
                    for k in range(KD):
                        ins = three(ps[:, bank, :], w(s, k * 256 + (j % 2) * P), xn(k, 0, S), k == 0, k == KD - 1)
                    ins.then_inc(g_full, 1)
                gate(0, s0, 2)
                pe.wait_ge(osum_ready, c.next(osum_ready))
                mm(ps[:, 0, :], ones, rrs[:], start=True, stop=True).then_inc(mu_full, 1)
                gate(1, s0, 3)
                pe.wait_ge(vsq_added, c.next(vsq_added, 4))
                mm(ps[:, 1, :], ones, rrs[:], start=True, stop=True).then_inc(var_full, 1)
                pe.wait_ge(w_ready[s1], c.next(w_ready[s1]))
                pe.wait_ge(cen_done, c.next(cen_done))
                gate(2, s1, 4)
                gate(3, s1, 5)
                pe.wait_ge(g_ready, c.next(g_ready, 4))
                pe.wait_ge(w_ready[s0], c.next(w_ready[s0]))
                pe.wait_ge(w_ready[s1], c.next(w_ready[s1]))
                for m in range(KD):
                    if m >= 2:
                        pe.wait_ge(y_added, c.next(y_added))
                    for kk in range(4):
                        ins = three(ps[:, 0 if m % 2 else 6, :], w((s0, s1)[kk // 2], (kk % 2) * D + m * P),
                                    (st[:, 0, kk, :], st[:, 1, kk, :]), kk == 0, kk == 3)
                    ins.then_inc(y_full, 1)
                pe.wait_ge(y_added, c.next(y_added, 2))
            mean_square()
            ffn(1, 0, 0, slot)

        @block.scalar
        def _(act):
            c = Count()
            fn = nc.scalar.activation

            def split_hi(s):
                act.wait_ge(raw_full[s], c.next(raw_full[s], 16))
                fn(wh[:, s, :], raw[:, s, :], ACT.Copy).then_inc(w_hi[s], 1)

            def norm(layer, k, n_y):
                if n_y:
                    act.wait_ge(y_added, c.next(y_added, n_y))
                for m in range(KD):
                    if m >= 2:
                        act.wait_ge(sq_added, c.next(sq_added))
                    fn(act_buf[:, m % 2, :], h[:, m, :], ACT.Square).then_inc(sq_done, 1)
                c.next(sq_added, 2)
                act.wait_ge(ms_full, c.next(ms_full))
                fn(rstd[:, 0:S], ps[:, 6, :], ACT.Sqrt, bias=eps[:, 0:1], scale=1.0 / D)
                fn(rstd[:, S:T], ps[:, 7, 0:L], ACT.Sqrt, bias=eps[:, 0:1], scale=1.0 / D).then_inc(std_done, 1)
                shift = mod_col(layer, 3 * k)
                for m in range(KD):
                    act.wait_ge(prod_done, c.next(prod_done))
                    for i, (t0, n) in enumerate(STREAMS):
                        ins = fn(xnh[:, m, t0:t0 + n], act_buf[:, m % 2, t0:t0 + n], ACT.Identity, bias=shift[:, m, i:i + 1])
                    ins.then_inc(xn_hi, 1)

            def ffn(n_streams, slot, last=False):
                n_tok = (S, T)[n_streams - 1]

                def up(j, par, s, wait_buf=True, refill=True):
                    act.wait_ge(glu_full, c.next(glu_full))
                    if wait_buf:
                        act.wait_ge(hid_ready, c.next(hid_ready))
                    ins = fn(act_buf[:, j, 0:S], ps[:, 3 * j, :], ACT.Silu)
                    if n_streams == 2:
                        ins = fn(act_buf[:, j, S:T], ps[:, 3 * j + 2, 0:L], ACT.Silu)
                    ins.then_inc(silu_done, 1)
                    act.wait_ge(hid_done, c.next(hid_done))
                    fn(hidh[:, par, j, 0:n_tok], act_buf[:, j, 0:n_tok], ACT.Copy).then_inc(hid_hi, 1)
                    if refill:
                        split_hi(s)

                def down(s, refill=True):
                    act.wait_ge(y_full, c.next(y_full, KD))
                    if refill:
                        split_hi(s)

                s0, s1 = slot, 1 - slot
                up(0, 0, s0, wait_buf=False)
                up(1, 0, s1, wait_buf=False)
                loops = BLOCKS // 2 - (1 if last else 0)

                def body(refill=True):
                    up(0, 1, s0)
                    up(1, 1, s1)
                    down(s0)
                    up(0, 0, s1)
                    up(1, 0, s0, refill=refill)
                    down(s1, refill=refill)
                with c.loop(act, loops, {glu_full: 4, hid_ready: 4, hid_done: 4, y_full: 16,
                                         raw_full[0]: 48, raw_full[1]: 48}):
                    body()
                if last:
                    up(0, 1, s0)
                    up(1, 1, s1)
                    down(s0)
                    up(0, 0, s1)
                    up(1, 0, s0)
                    down(s1, refill=False)
                c.next(hid_ready, 2)
                down(s0, refill=not last)
                return 1 - slot

            split_hi(0)
            split_hi(1)
            act.wait_ge(loaded, 48)
            act.wait_ge(dve_step, c.next(dve_step))
            fn(c_act[:].rearrange("p k j -> p (k j)"), v("c"), ACT.Silu).then_inc(setup_done, 1)
            fn(lg[:, 0, :], v("log1m"), ACT.Exp).then_inc(lg_step, 1)
            act.wait_ge(lg_step, c.next(lg_step, 2))
            fn(lg[:, 2, :], lg[:, 1, :], ACT.Ln).then_inc(lg_step, 1)
            c.next(lg_step)
            norm(0, 0, 0)
            slot = ffn(2, 0)
            norm(0, 1, KD * BLOCKS)

            s0, s1 = slot, 1 - slot
            sets = ((0, 1), (2, 3), (4, 5))

            def square(n_item, wait_sq=True):
                act.wait_ge(item_full, c.next(item_full))
                if wait_sq:
                    act.wait_ge(item_ms, c.ahead(item_ms, 0))
                fn(sqb[:, 0:S], ps[:, sets[n_item % 3][0], :], ACT.Square)
                fn(sqb[:, S:T], ps[:, sets[n_item % 3][1], 0:L], ACT.Square).then_inc(item_sq, 1)

            def root(i, dim, n_ms=1):
                act.wait_ge(item_ms, c.next(item_ms, n_ms))
                fn(nrm[:, i, 0:S], ps[:, 6, :], ACT.Sqrt, bias=eps[:, 0:1], scale=1.0 / dim)
                fn(nrm[:, i, S:T], ps[:, 7, 0:L], ACT.Sqrt, bias=eps[:, 0:1], scale=1.0 / dim).then_inc(item_std, 1)

            def hi(dst, src, wait=item_v, rot=False):
                act.wait_ge(wait, c.next(wait))
                fn(dst, src, ACT.Copy).then_inc(item_hi, 1)

            square(0, False)
            c.next(item_ms)
            act.wait_ge(item_ms, c.ahead(item_ms, 0))
            square(1, False)
            split_hi(s0)
            c.next(item_ms)
            act.wait_ge(item_ms, c.ahead(item_ms, 0))
            square(2, False)
            root(0, Q_RANK)
            for k in range(3):
                hi(cqn[:, 0, k, :], nrm[:, (1, 2, 0)[k], :])
                if k == 0:
                    square(3, False)
                    split_hi(s1)
                if k == 1:
                    c.next(item_ms)
                    act.wait_ge(item_ms, c.ahead(item_ms, 0))
                    square(4, False)
            root(1, KV_RANK)
            hi(ckvn[:, 0, 0, :], nrm[:, 2, :])
            square(5, False)
            split_hi(s0)
            hi(ckvn[:, 0, 1, :], nrm[:, 1, :])
            root(2, ROPE)
            c.next(item_v)
            hi(krr[:, 0, :], nrm[:, 2, :], item_rot)
            slot = s1

            tiles = [(hh, q) for hh in range(2) for q in (4, 5, 0, 1, 2, 3)]
            scale = (NOPE + ROPE) ** -0.5

            def exponent(n, hh, q):
                act.wait_ge(max_done, c.next(max_done))
                b, e = n % 2, n % 2
                cols = (0, T) if q < 4 else (S, T)
                flat = ps[:, 2 * b:2 * b + 2, :].rearrange("p b t -> p (b t)")
                fn(nrm[:, e, cols[0]:cols[1]], flat[:, cols[0]:cols[1]], ACT.Exp, bias=row[:, 0, b:b + 1], scale=scale,
                   accum_out=row[:, 1, b:b + 1]).then_inc(exp_done, 1)

            def turned(n, hh, q):
                act.wait_ge(pt_full, c.next(pt_full))
                if q < 4:
                    fn(pt[0][:, 0:4, q * P:q * P + P], ps[:, 4, :].rearrange("p (k q) -> p k q", k=4), ACT.Copy)
                q0 = q * P if q < 4 else L + (q - 4) * P
                fn(pt[0][:, 4:6, q0:q0 + P], ps[:, 5, 0:256].rearrange("p (k q) -> p k q", k=2), ACT.Copy
                   ).then_inc(pt_hi, 1)

            def attended(hh, context):
                act.wait_ge(o_full, c.next(o_full))
                t0, n = STREAMS[context]
                fn(oo[0][:, hh, t0:t0 + n], ps[:, 6 + context, 0:n], ACT.Copy).then_inc(o_hi, 1)

            s0, s1 = slot, 1 - slot
            with c.loop(act, PAIRS, {item_full: 5, item_ms: 5, item_v: 5, item_rot: 1, v_full: 6, max_done: 12,
                                     pt_full: 12, o_full: 4, y_full: 8, raw_full[0]: 32, raw_full[1]: 32}):
                square(0)
                root(0, ROPE)
                square(1, False)
                c.next(item_v)
                hi(qrr[:, 0, :], nrm[:, 0, :], item_rot)
                root(1, NOPE)
                square(2, False)
                split_hi(s0)
                hi(qn[:, 0, 0, :], nrm[:, 1, :])
                root(2, NOPE)
                square(3, False)
                hi(qn[:, 0, 1, :], nrm[:, 2, :])
                root(0, NOPE)
                square(4, False)
                hi(kn[:, 0, 0, :], nrm[:, 0, :])

                def value(tc):
                    act.wait_ge(v_full, c.next(v_full))
                    fn(vv[0][:, tc, :], ps[:, 4 + tc % 2, 0:256], ACT.Copy).then_inc(v_hi, 1)
                value(0)
                value(1)
                value(2)
                root(1, NOPE)
                hi(kn[:, 0, 1, :], nrm[:, 1, :])
                for tc in range(3, 6):
                    value(tc)
                split_hi(s1)
                exponent(0, *tiles[0])
                for n, (hh, q) in enumerate(tiles):
                    if n + 1 < len(tiles):
                        exponent(n + 1, *tiles[n + 1])
                    if q == 1:
                        attended(hh, 1)
                    if q == 4 and hh == 1:
                        attended(0, 0)
                    turned(n, hh, q)
                attended(1, 0)
                act.wait_ge(y_full, c.next(y_full, KD))
                split_hi(s0)
                split_hi(s1)
            norm(0, 2, KD * PAIRS)
            slot = ffn(2, slot)
            norm(1, 0, KD * BLOCKS)
            slot = ffn(2, slot)
            norm(1, 1, KD * BLOCKS)

            s0, s1 = slot, 1 - slot

            def part(wait, done, dst, src):
                act.wait_ge(wait, c.next(wait))
                fn(dst, src, ACT.Copy).then_inc(done, 1)

            with c.loop(act, RET_HEADS, {dec_done: 1, qk_full: 2, qk_val: 4, v_full: 12, sc_val: 6, o_full: 4, cen_done: 1,
                                         vsq_added: 4, var_full: 1, g_full: 4, g_val: 4, y_full: 8,
                                         raw_full[0]: 64, raw_full[1]: 64}):
                act.wait_ge(dec_done, c.next(dec_done))
                fn(dec_lat, dec_lat, ACT.Exp)
                fn(dec_ctx, dec_ctx, ACT.Exp)
                fn(rt_flat[:, 0:640], rt_flat[:, 0:640], ACT.Exp).then_inc(dec_exp, 1)
                act.wait_ge(qk_full, c.next(qk_full))
                split_hi(s0)
                for j in range(2):
                    part(qk_val, qk_hi, rq[:, 0, j, :], rt[:, j, :])
                act.wait_ge(qk_full, c.next(qk_full))
                split_hi(s1)
                fn(rk[:, 0, 0, S:T], ps[:, 4, 0:L], ACT.Copy)
                fn(rk[:, 0, 1, S:T], ps[:, 5, 0:L], ACT.Copy).then_inc(qk_hi, 1)
                for j in range(2):
                    part(qk_val, qk_hi, rk[:, 0, j, 0:S], rt[:, j, :])
                for tc in range(6):
                    part(v_full, v_hi, rv[:, 0, tc, :], ps[:, 6 + tc % 2, 0:256])
                split_hi(s0)
                for jc in range(6):
                    part(sc_val, sc_hi, st[:, 0, jc, :], rt[:, jc % 2, :])
                act.wait_ge(o_full, c.next(o_full, 2))
                for tc in range(6):
                    part(v_full, v_hi, rv[:, 0, tc, :], ps[:, tc % 2, 0:256])
                split_hi(s1)
                c.next(o_full, 2)
                act.wait_ge(cen_done, c.next(cen_done))
                for j in range(4):
                    if j >= 2:
                        act.wait_ge(vsq_added, c.next(vsq_added))
                    fn(rt[:, j % 2, :], dec[:, j, :], ACT.Square).then_inc(vsq_done, 1)
                c.next(vsq_added, 2)
                act.wait_ge(var_full, c.next(var_full))
                fn(rrs[:], ps[:, 1, :], ACT.Sqrt, bias=eps[:, 0:1], scale=1.0 / RET_DV).then_inc(rstd_done, 1)
                for j in range(4):
                    act.wait_ge(g_full, c.next(g_full))
                    fn(rt[:, 2, :], ps[:, 2 + j, :], ACT.Silu).then_inc(g_silu, 1)
                    if j in (1, 3):
                        split_hi((s0, s1)[j // 2])
                    part(g_val, g_hi, st[:, 0, j, :], dec[:, j, :])
                act.wait_ge(y_full, c.next(y_full, KD))
                split_hi(s0)
                split_hi(s1)
            norm(1, 2, KD * RET_HEADS)
            ffn(1, slot, last=True)

        @block.vector
        def _(dve):
            c = Count()
            tt, ts, stt = nc.vector.tensor_tensor, nc.vector.tensor_scalar, nc.vector.scalar_tensor_tensor

            def split_lo(s):
                dve.wait_ge(w_hi[s], c.next(w_hi[s]))
                tt(wl[:, s, :], raw[:, s, :], wh[:, s, :].bitcast(F32), ALU.subtract).then_inc(w_ready[s], 1)

            def step(ins):
                ins.then_inc(dve_step, 1)
                dve.wait_ge(dve_step, c.next(dve_step))

            def ada_out(chunk, n):
                dve.wait_ge(ada_psum, c.next(ada_psum, n))
                b0 = _cols["ada_b"][0]
                o = mods[:].rearrange("p k j -> p (k j)")
                if isinstance(chunk, int):
                    dst, bias = o[:, 2 * chunk:2 * chunk + 4 * n], vec[:, b0 + 2 * chunk:b0 + 2 * chunk + 4 * n]
                else:
                    dst, bias = o[:, bass.ds(chunk * 2, 4 * n)], vec[:, bass.ds(chunk * 2 + b0, 4 * n)]
                tt(dst, ps[:, 5, 0:4 * n], bias, ALU.add).then_inc(ada_evac, 1)

            def coefs(layer, k):
                g0 = _cols["norm_g"][0] + (layer * 3 + k) * 2 * KD
                gain = vec[:, g0:g0 + 2 * KD].rearrange("p (k j) -> p k j", j=2)
                stt(out=coef[:, 0, :, :], in0=mod_col(layer, 3 * k + 1), scalar=1.0, in1=gain, op0=ALU.add, op1=ALU.mult)
                step(ts(coef[:, 1, :, :], mod_col(layer, 3 * k + 2), 0.5 if k != 1 else 1.0, None, ALU.mult))

            def norm(layer, k):
                for m in range(KD):
                    dve.wait_ge(sq_done, c.next(sq_done))
                    if m == 0:
                        nc.vector.tensor_copy(ssum[:], act_buf[:, 0, :]).then_inc(sq_added, 1)
                    else:
                        dve.wait_ge(sq_added, c.next(sq_added))
                        tt(ssum[:], ssum[:], act_buf[:, m % 2, :], ALU.add).then_inc(sq_added, 1)
                c.next(sq_added)
                coefs(layer, k)
                dve.wait_ge(std_done, c.next(std_done))
                step(nc.vector.reciprocal(rstd[:], rstd[:]))
                shift = mod_col(layer, 3 * k)
                for m in range(KD + 1):
                    if m < KD:
                        if m >= 2:
                            dve.wait_ge(xn_ready, c.next(xn_ready))
                        for i, (t0, n) in enumerate(STREAMS):
                            ins = stt(out=act_buf[:, m % 2, t0:t0 + n], in0=h[:, m, t0:t0 + n], scalar=coef[:, 0, m, i:i + 1],
                                      in1=rstd[:, t0:t0 + n], op0=ALU.mult, op1=ALU.mult)
                        ins.then_inc(prod_done, 1)
                    if m >= 1:
                        dve.wait_ge(xn_hi, c.next(xn_hi))
                        for i, (t0, n) in enumerate(STREAMS):
                            ins = stt(out=xnl[:, m - 1, t0:t0 + n], in0=act_buf[:, (m - 1) % 2, t0:t0 + n],
                                      scalar=shift[:, m - 1, i:i + 1], in1=xnh[:, m - 1, t0:t0 + n].bitcast(F32),
                                      op0=ALU.add, op1=ALU.subtract)
                        ins.then_inc(xn_ready, 1)
                c.next(xn_ready, 2)

            def add_y(m, n_streams):
                dve.wait_ge(y_full, c.next(y_full))
                for i, (t0, n) in enumerate(STREAMS[:n_streams]):
                    bank = (0, 2)[i] if m % 2 else 6 + i
                    ins = stt(out=h[:, m, t0:t0 + n], in0=ps[:, bank, 0:n], scalar=coef[:, 1, m, i:i + 1],
                              in1=h[:, m, t0:t0 + n], op0=ALU.mult, op1=ALU.add)
                ins.then_inc(y_added, 1)

            def ffn(n_streams, slot, ada_per, ada_first, last=False):
                n_tok = (S, T)[n_streams - 1]

                def up(j, par, s=None):
                    dve.wait_ge(silu_done, c.next(silu_done))
                    ins = tt(act_buf[:, j, 0:S], act_buf[:, j, 0:S], ps[:, 3 * j + 1, :], ALU.mult)
                    if n_streams == 2:
                        ins = tt(act_buf[:, j, S:T], act_buf[:, j, S:T], ps[:, 3 * j + 2, L:2 * L], ALU.mult)
                    ins.then_inc(hid_done, 1)
                    dve.wait_ge(hid_hi, c.next(hid_hi))
                    tt(hidl[:, par, j, 0:n_tok], act_buf[:, j, 0:n_tok], hidh[:, par, j, 0:n_tok].bitcast(F32),
                       ALU.subtract).then_inc(hid_ready, 1)
                    if s is not None:
                        split_lo(s)

                def down(s, s_mid=None):
                    for m in range(KD):
                        add_y(m, n_streams)
                        if m == 3 and s_mid is not None:
                            split_lo(s_mid)
                    if s is not None:
                        split_lo(s)

                s0, s1 = slot, 1 - slot
                up(0, 0, s0)
                up(1, 0, s1)
                if ada_per:
                    ada_out(2 * ada_first, ada_per)
                per = {silu_done: 4, hid_hi: 4, w_hi[0]: 3, w_hi[1]: 3, y_full: 16}
                if ada_per:
                    per[ada_psum] = 2 * ada_per
                with c.loop(dve, BLOCKS // 2 - (1 if last else 0), per) as i:
                    up(0, 1, s0)
                    up(1, 1)
                    down(s0, s1)
                    if ada_per:
                        ada_out(i * (4 * ada_per) + 2 * (ada_first + ada_per), ada_per)
                    up(0, 0, s1)
                    up(1, 0)
                    down(s1, s0)
                    if ada_per:
                        ada_out(i * (4 * ada_per) + 2 * (ada_first + 2 * ada_per), ada_per)
                if last:
                    up(0, 1, s0)
                    up(1, 1)
                    down(s0, s1)
                    up(0, 0, s1)
                    up(1, 0)
                    down(None, s0)
                down(None if last else s0)
                return 1 - slot

            step(nc.vector.memset(eps[:], EPS))
            split_lo(0)
            split_lo(1)
            dve.wait_ge(loaded, 48)
            dve.wait_ge(lg_step, c.next(lg_step))
            ts(lg[:, 1, :], lg[:, 0, :], -1.0, 1.0, ALU.mult, ALU.add).then_inc(lg_step, 1)
            dve.wait_ge(lg_step, c.next(lg_step, 2))
            step(ts(lg[:, 3, :], lg[:, 1, :], 1.0, None, ALU.is_equal))
            stt(out=lg[:, 4, :], in0=lg[:, 1, :], scalar=-1.0, in1=lg[:, 3, :], op0=ALU.add, op1=ALU.add)
            step(tt(lg[:, 2, :], lg[:, 2, :], lg[:, 3, :], ALU.add))
            step(nc.vector.reciprocal(lg[:, 4, :], lg[:, 4, :]))
            step(tt(lg[:, 2, :], lg[:, 2, :], lg[:, 4, :], ALU.mult))
            step(tt(lg[:, 2, :], lg[:, 2, :], lg[:, 0, :], ALU.mult))
            step(ts(lg[:, 1, :], lg[:, 2, :], -1.0, None, ALU.mult))
            ada_out(0, ADA_FIRST)
            dve.wait_ge(ada_evac, c.next(ada_evac))
            norm(0, 0)
            slot = ffn(2, 0, ADA_A, ADA_FIRST)
            ada_out(2 * (ADA_FIRST + ADA_A * BLOCKS), ADA_MID)
            c.next(ada_evac, BLOCKS)
            dve.wait_ge(ada_evac, c.next(ada_evac))
            norm(0, 1)

            s0, s1 = slot, 1 - slot
            sets = ((0, 1), (2, 3), (4, 5))
            gate_cols = {n: v(n) for n in ("q_norm", "kv_norm", "qg_nope", "qg_rope", "kg_nope", "kg_rope")}

            def inverse(i):
                dve.wait_ge(item_std, c.next(item_std))
                step(nc.vector.reciprocal(nrm[:, i, :], nrm[:, i, :]))

            def scaled(n_item, i_rms, i_out, gain):
                for i, (t0, n) in enumerate(STREAMS):
                    ins = stt(out=nrm[:, i_out, t0:t0 + n], in0=ps[:, sets[n_item % 3][i], 0:n], scalar=gain,
                              in1=nrm[:, i_rms, t0:t0 + n], op0=ALU.mult, op1=ALU.mult)
                ins.then_inc(item_v, 1)

            def lo(dst, hi_part, src):
                dve.wait_ge(item_hi, c.next(item_hi))
                tt(dst, src, hi_part.bitcast(F32), ALU.subtract).then_inc(item_ready, 1)

            def rotated(i):
                dve.wait_ge(item_swapped, c.next(item_swapped))
                tt(nrm[:, i, 0:S], nrm[:, i, 0:S], cs[:, 0, :], ALU.mult)
                step(tt(ps[:, 6, :], ps[:, 6, :], cs[:, 1, :], ALU.mult))
                tt(nrm[:, i, 0:S], nrm[:, i, 0:S], ps[:, 6, :], ALU.add).then_inc(item_rot, 1)

            inverse(0)
            g = gate_cols["q_norm"]
            for k, i_out in enumerate((1, 2, 0)):
                scaled(k, 0, i_out, g[:, k:k + 1])
                lo(cqn[:, 1, k, :], cqn[:, 0, k, :], nrm[:, i_out, :])
                if k == 1:
                    split_lo(s0)
            split_lo(s1)
            inverse(1)
            g = gate_cols["kv_norm"]
            for k, i_out in enumerate((2, 1)):
                scaled(3 + k, 1, i_out, g[:, k:k + 1])
                lo(ckvn[:, 1, k, :], ckvn[:, 0, k, :], nrm[:, i_out, :])
            split_lo(s0)
            inverse(2)
            scaled(5, 2, 2, gate_cols["kg_rope"])
            dve.wait_ge(tab_full, 16)
            rotated(2)
            lo(krr[:, 1, :], krr[:, 0, :], nrm[:, 2, :])
            slot = s1

            tiles = [(hh, q) for hh in range(2) for q in (4, 5, 0, 1, 2, 3)]
            scale = (NOPE + ROPE) ** -0.5

            def maximum(n, hh, q):
                dve.wait_ge(s_full, c.next(s_full))
                b = n % 2
                cols = (0, T) if q < 4 else (S, T)
                flat = ps[:, 2 * b:2 * b + 2, :].rearrange("p b t -> p (b t)")
                step(nc.vector.reduce_max(row[:, 3, b:b + 1], flat[:, cols[0]:cols[1]], AX_X))
                ts(row[:, 0, b:b + 1], row[:, 3, b:b + 1], -scale, None, ALU.mult).then_inc(max_done, 1)

            def probabilities(n, hh, q):
                dve.wait_ge(exp_done, c.next(exp_done))
                b = n % 2
                cols = (0, T) if q < 4 else (S, T)
                step(nc.vector.reciprocal(row[:, 2, b:b + 1], row[:, 1, b:b + 1]))
                ts(nrm[:, b, cols[0]:cols[1]], nrm[:, b, cols[0]:cols[1]], row[:, 2, b:b + 1], None, ALU.mult
                   ).then_inc(p_done, 1)

            def turned(n, hh, q):
                dve.wait_ge(pt_hi, c.next(pt_hi))
                if q < 4:
                    tt(pt[1][:, 0:4, q * P:q * P + P], ps[:, 4, :].rearrange("p (k q) -> p k q", k=4),
                       pt[0][:, 0:4, q * P:q * P + P].bitcast(F32), ALU.subtract)
                q0 = q * P if q < 4 else L + (q - 4) * P
                tt(pt[1][:, 4:6, q0:q0 + P], ps[:, 5, 0:256].rearrange("p (k q) -> p k q", k=2),
                   pt[0][:, 4:6, q0:q0 + P].bitcast(F32), ALU.subtract).then_inc(pt_ready, 1)

            def attended(hh, context):
                dve.wait_ge(o_hi, c.next(o_hi))
                t0, n = STREAMS[context]
                tt(oo[1][:, hh, t0:t0 + n], ps[:, 6 + context, 0:n], oo[0][:, hh, t0:t0 + n].bitcast(F32),
                   ALU.subtract).then_inc(o_ready, 1)

            s0, s1 = slot, 1 - slot
            with c.loop(dve, PAIRS, {item_std: 5, item_hi: 5, item_swapped: 1, v_hi: 6, s_full: 12, exp_done: 12,
                                     pt_hi: 12, o_hi: 4, y_full: 8, w_hi[0]: 2, w_hi[1]: 2, dve_step: 5 + 1 + 24}):
                inverse(0)
                scaled(0, 0, 0, gate_cols["qg_rope"])
                rotated(0)
                lo(qrr[:, 1, :], qrr[:, 0, :], nrm[:, 0, :])
                inverse(1)
                scaled(1, 1, 1, gate_cols["qg_nope"])
                lo(qn[:, 1, 0, :], qn[:, 0, 0, :], nrm[:, 1, :])
                inverse(2)
                scaled(2, 2, 2, gate_cols["qg_nope"])
                split_lo(s0)
                lo(qn[:, 1, 1, :], qn[:, 0, 1, :], nrm[:, 2, :])
                inverse(0)
                scaled(3, 0, 0, gate_cols["kg_nope"])
                lo(kn[:, 1, 0, :], kn[:, 0, 0, :], nrm[:, 0, :])

                def value(tc):
                    dve.wait_ge(v_hi, c.next(v_hi))
                    tt(vv[1][:, tc, :], ps[:, 4 + tc % 2, 0:256], vv[0][:, tc, :].bitcast(F32), ALU.subtract
                       ).then_inc(v_ready, 1)
                for tc in range(3):
                    value(tc)
                inverse(1)
                scaled(4, 1, 1, gate_cols["kg_nope"])
                lo(kn[:, 1, 1, :], kn[:, 0, 1, :], nrm[:, 1, :])
                for tc in range(3, 6):
                    value(tc)
                split_lo(s1)
                maximum(0, *tiles[0])
                for n, (hh, q) in enumerate(tiles):
                    if n + 1 < len(tiles):
                        maximum(n + 1, *tiles[n + 1])
                    probabilities(n, hh, q)
                    if q == 1:
                        attended(hh, 1)
                    if q == 4 and hh == 1:
                        attended(0, 0)
                    turned(n, hh, q)
                attended(1, 0)
                for m in range(KD):
                    add_y(m, 2)
                split_lo(s0)
                split_lo(s1)
            norm(0, 2)
            slot = ffn(2, slot, ADA_B, ADA_FIRST + ADA_A * BLOCKS + ADA_MID)
            dve.wait_ge(ada_evac, c.next(ada_evac, BLOCKS))
            norm(1, 0)
            slot = ffn(2, slot, 0, 0)
            norm(1, 1)

            s0, s1 = slot, 1 - slot
            dve.wait_ge(tab_full, 48)
            c.next(o_full, 4 * PAIRS)
            gn0 = _cols["gn"][0]
            with c.loop(dve, RET_HEADS, {dec_exp: 1, qk_full: 2, qk_hi: 5, v_hi: 12, qk_ready: 2, sc_ready: 6, sc_full: 6, sc_hi: 6, o_full: 4,
                                         mu_full: 1, vsq_done: 4, vsq_added: 4, rstd_done: 1, g_silu: 4, g_hi: 4, y_full: 8,
                                         w_hi[0]: 4, w_hi[1]: 4, dve_step: 18}) as i:
                lgf, nlgb = lg[:, 1, bass.ds(i, 1)], lg[:, 2, bass.ds(i + RET_HEADS, 1)]
                ts(dec_lat, dist[:], 0.0, lgf, ALU.max, ALU.mult)
                step(ts(rt_flat[:, 0:DIST_W], dist[:], 0.0, nlgb, ALU.min, ALU.mult))
                step(tt(dec_lat, dec_lat, rt_flat[:, 0:DIST_W], ALU.add))
                ts(dec_ctx, dist[:, 256:DIST_W], float(L), lgf, ALU.add, ALU.mult)
                ts(rt_flat[:, 0:640], dist[:, 256:DIST_W], -float(S), nlgb, ALU.add, ALU.mult).then_inc(dec_done, 1)
                dve.wait_ge(dec_exp, c.next(dec_exp))
                step(tt(dec_ctx, dec_ctx, rt_flat[:, 0:640], ALU.add))

                def rotate(b):
                    cos, sin = cr[:, 0, :], cr[:, 1, :]
                    tt(rt[:, 0, :], ps[:, b, :], cos, ALU.mult)
                    step(tt(rt[:, 2, :], ps[:, b + 1, :], sin, ALU.mult))
                    tt(rt[:, 0, :], rt[:, 0, :], rt[:, 2, :], ALU.subtract).then_inc(qk_val, 1)
                    step(tt(rt[:, 1, :], ps[:, b + 1, :], cos, ALU.mult))
                    step(tt(rt[:, 2, :], ps[:, b, :], sin, ALU.mult))
                    tt(rt[:, 1, :], rt[:, 1, :], rt[:, 2, :], ALU.add).then_inc(qk_val, 1)

                dve.wait_ge(qk_full, c.next(qk_full))
                rotate(0)
                for j in range(2):
                    dve.wait_ge(qk_hi, c.next(qk_hi))
                    ins = tt(rq[:, 1, j, :], rt[:, j, :], rq[:, 0, j, :].bitcast(F32), ALU.subtract)
                ins.then_inc(qk_ready, 1)
                split_lo(s0)
                dve.wait_ge(qk_full, c.next(qk_full))
                dve.wait_ge(qk_hi, c.next(qk_hi))
                for j in range(2):
                    tt(rk[:, 1, j, S:T], ps[:, 4 + j, 0:L], rk[:, 0, j, S:T].bitcast(F32), ALU.subtract)
                dve.wait_ge(qk_ready, c.next(qk_ready))
                rotate(2)
                for j in range(2):
                    dve.wait_ge(qk_hi, c.next(qk_hi))
                    ins = tt(rk[:, 1, j, 0:S], rt[:, j, :], rk[:, 0, j, 0:S].bitcast(F32), ALU.subtract)
                ins.then_inc(qk_ready, 1)
                split_lo(s1)

                def value(tc, bank):
                    dve.wait_ge(v_hi, c.next(v_hi))
                    tt(rv[:, 1, tc, :], ps[:, bank, 0:256], rv[:, 0, tc, :].bitcast(F32), ALU.subtract
                       ).then_inc(v_ready, 1)
                for tc in range(6):
                    value(tc, 6 + tc % 2)
                split_lo(s0)
                dve.wait_ge(qk_ready, c.next(qk_ready))
                for jc in range(7):
                    if jc < 6:
                        if jc >= 2:
                            dve.wait_ge(sc_ready, c.next(sc_ready))
                        dve.wait_ge(sc_full, c.next(sc_full))
                        table = dec_flat[:, 384 - P * jc:384 - P * jc + S] if jc < 4 else \
                            dec_ctx[:, P * (5 - jc):P * (5 - jc) + S]
                        stt(out=rt[:, jc % 2, :], in0=ps[:, jc % 4, :], scalar=RET_DK ** -0.5, in1=table,
                            op0=ALU.mult, op1=ALU.mult).then_inc(sc_val, 1)
                    if jc >= 1:
                        dve.wait_ge(sc_hi, c.next(sc_hi))
                        tt(st[:, 1, jc - 1, :], rt[:, (jc - 1) % 2, :], st[:, 0, jc - 1, :].bitcast(F32),
                           ALU.subtract).then_inc(sc_ready, 1)
                for tc in range(6):
                    value(tc, tc % 2)
                split_lo(s1)
                c.next(sc_ready, 2)
                dve.wait_ge(o_full, c.next(o_full, 4))
                step(nc.vector.tensor_copy(rrs[:], ps[:, 4, :]))
                step(tt(rrs[:], rrs[:], ps[:, 5, :], ALU.add))
                step(tt(rrs[:], rrs[:], ps[:, 6, :], ALU.add))
                tt(rrs[:], rrs[:], ps[:, 7, :], ALU.add).then_inc(osum_ready, 1)
                dve.wait_ge(mu_full, c.next(mu_full))
                step(ts(rt[:, 2, :], ps[:, 0, :], -1.0 / RET_DV, None, ALU.mult))
                for j in range(4):
                    ins = tt(dec[:, j, :], ps[:, 4 + j, :], rt[:, 2, :], ALU.add)
                ins.then_inc(cen_done, 1)
                for j in range(4):
                    dve.wait_ge(vsq_done, c.next(vsq_done))
                    if j == 0:
                        nc.vector.tensor_copy(rrs[:], rt[:, 0, :]).then_inc(vsq_added, 1)
                    else:
                        dve.wait_ge(vsq_added, c.next(vsq_added))
                        tt(rrs[:], rrs[:], rt[:, j % 2, :], ALU.add).then_inc(vsq_added, 1)
                c.next(vsq_added)
                dve.wait_ge(rstd_done, c.next(rstd_done))
                step(nc.vector.reciprocal(rrs[:], rrs[:]))
                for j in range(4):
                    step(stt(out=dec[:, j, :], in0=dec[:, j, :], scalar=vec[:, bass.ds(i * 4 + (gn0 + j), 1)],
                             in1=rrs[:], op0=ALU.mult, op1=ALU.mult))
                    dve.wait_ge(g_silu, c.next(g_silu))
                    tt(dec[:, j, :], dec[:, j, :], rt[:, 2, :], ALU.mult).then_inc(g_val, 1)
                    if j in (1, 3):
                        split_lo((s0, s1)[j // 2])
                    dve.wait_ge(g_hi, c.next(g_hi))
                    tt(st[:, 1, j, :], dec[:, j, :], st[:, 0, j, :].bitcast(F32), ALU.subtract).then_inc(g_ready, 1)
                for m in range(KD):
                    add_y(m, 1)
                split_lo(s0)
                split_lo(s1)
            norm(1, 2)
            ffn(1, slot, 0, 0, last=True)


def _chunks(w, n_out):
    i, o = w.shape
    return w.reshape(i // P, P, o // n_out, n_out).transpose(2, 1, 0, 3).reshape(o // n_out, P, -1)


def _rows(w, n_in):
    i, o = w.shape
    return w.reshape(i // (P * n_in), n_in, P, o).transpose(0, 2, 1, 3).reshape(i // (P * n_in), P, -1)


def _pad(u):
    full = np.zeros((u.shape[0], UNIT), u.dtype)
    full[:, :u.shape[1]] = u
    return full


def _ffn_units(w_in, w_out):
    a, b = _chunks(w_in[:, :D_FF], P), _chunks(w_in[:, D_FF:], P)
    up = np.concatenate([a.reshape(-1, P, KD, P), b.reshape(-1, P, KD, P)], 3).reshape(-1, P, UNIT)
    down = _rows(w_out, 2)
    order = [up[0], up[1]]
    for blk in range(1, BLOCKS):
        order += [up[2 * blk], up[2 * blk + 1], down[blk - 1]]
    return order + [down[BLOCKS - 1]]


def _mla_units(w_in, w_uq, w_ukv, w_o):
    w_in = np.concatenate([w_in, w_in[:, Q_RANK + KV_RANK:]], 1)
    order = list(_chunks(w_in, 256))
    uq = w_uq.reshape(Q_RANK, HEADS, NOPE + ROPE)
    ukv = w_ukv.reshape(KV_RANK, HEADS, NOPE + DV)
    for p in range(PAIRS):
        a, b = 2 * p, 2 * p + 1
        q = np.concatenate([uq[:, a, :NOPE], uq[:, b, :NOPE], uq[:, a, NOPE:], uq[:, b, NOPE:]], 1)
        kv = np.concatenate([ukv[:, a, :NOPE], ukv[:, b, :NOPE], ukv[:, a, NOPE:], ukv[:, b, NOPE:]], 1)
        order += [_pad(_rows(q, 3)[0]), _pad(_rows(kv, 2)[0])]
        order += [_pad(w_o[a * P:a * P + P]), _pad(w_o[b * P:b * P + P])]
    return order


def _ret_units(w_in, w_o):
    hdk, hdv = RET_HEADS * RET_DK, RET_HEADS * RET_DV
    u = _chunks(w_in, 256)
    q, k, val, gate = u[:4], u[4:8], u[8:16], u[16:24]
    o = _rows(w_o, 2)
    order = []
    for n in range(RET_HEADS):
        order += [q[n], k[n], val[2 * n], val[2 * n + 1], gate[2 * n], gate[2 * n + 1], o[2 * n], o[2 * n + 1]]
    return order


def _angles(pos, dim):
    inv = (np.float32(10000.0) ** (-np.arange(0, dim, 2, dtype=np.float32) / np.float32(dim))).astype(np.float32)
    return pos.astype(np.float32)[:, None] * inv[None, :]


def _tables():
    mats = np.zeros((P, 4, P), np.float32)
    mats[:, 0] = 1.0
    mats[:64, 1, :64] = mats[64:, 1, 64:] = 1.0
    for p in range(P):
        mats[p ^ 16, 2, p] = 1.0
        mats[p, 3, p] = 1.0
    pos = np.arange(S)
    a_row, a_col = _angles(pos // 64, 32), _angles(pos % 64, 32)
    ang = np.concatenate([a_row, a_row, a_col, a_col], 1).T
    sign = np.where((np.arange(64) & 16) == 0, -1.0, 1.0).astype(np.float32)[:, None]
    rope = np.stack([np.cos(ang), np.sin(ang) * sign], 1)
    rope = np.concatenate([rope, rope], 0).astype(np.float32)
    ang = _angles(pos, RET_DK).T
    ret = np.stack([np.cos(ang), np.sin(ang)], 1).astype(np.float32)
    dist = (np.arange(DIST_W)[None, :] - 384 - np.arange(P)[:, None]).astype(np.float32)
    return mats, rope, ret, dist


def kernel(**inputs):
    import concourse.bacc as _bacc
    from concourse.bass_utils import run_bass_kernel_spmd as _run

    a = {k: np.asarray(t) for k, t in inputs.items()}
    units = []
    fi, fo = a["ffn_w_in"], a["ffn_w_out"]
    units += _ffn_units(fi[0, 0], fo[0, 0])
    units += _mla_units(a["mla_w_in"][0], a["mla_w_uq"][0], a["mla_w_ukv"][0], a["mla_w_o"][0])
    units += _ffn_units(fi[0, 1], fo[0, 1]) + _ffn_units(fi[1, 0], fo[1, 0])
    units += _ret_units(a["ret_w_in"][0], a["ret_w_o"][0])
    units += _ffn_units(fi[1, 1], fo[1, 1])
    weights = np.stack(units)
    assert weights.shape == (N_UNITS, P, UNIT)
    ada = np.concatenate([_chunks(a["ada_w"][i], 256) for i in range(2)])

    def col(x):
        return x.reshape(-1, P).T

    def twice(x):
        return np.repeat(col(x), 2, axis=1)
    c2 = np.stack([col(a["c"][0]), col(a["c_ctx"])], 2).reshape(P, -1)
    qg, kg = a["mla_q_gain"][0], a["mla_k_gain"][0]
    vecs = np.concatenate([
        c2, twice(a["ada_b"]), twice(a["norm_g"]), col(a["mla_q_norm"][0]), col(a["mla_kv_norm"][0]),
        col(qg[:NOPE]), col(np.concatenate([qg[NOPE:]] * 2)), col(kg[:NOPE]), col(np.concatenate([kg[NOPE:]] * 2)),
        col(a["ret_gn_gain"][0]), np.broadcast_to(a["ret_log1m_gamma"][0].reshape(1, 8), (P, 8))], 1)
    assert vecs.shape == (P, N_VEC)
    x = np.concatenate([a["x"][0], a["ctx"][0]], 0).T.reshape(KD, P, T).transpose(1, 0, 2)
    mats, rope, ret, dist = _tables()
    arrays = {"weights": weights, "ada": ada, "vecs": vecs, "consts": mats, "x_in": x, "rope_mla": rope,
              "rope_ret": ret, "dist_in": dist}
    arrays = {k: np.ascontiguousarray(t) for k, t in arrays.items()}
    nc = _bacc.Bacc("TRN2", target_bir_lowering=False, num_devices=1)
    args = [nc.dram_tensor(k, t.shape, F32, kind="ExternalInput").ap() for k, t in arrays.items()]
    out = nc.dram_tensor("out", (KD, P, S), F32, kind="ExternalOutput").ap()
    build(nc, *args, out)
    r = _run(nc, [arrays], core_ids=[0])
    return np.ascontiguousarray(r.results[0]["out"].reshape(D, S).T)[None]
```

```python
from contextlib import ExitStack, contextmanager

import numpy as np
import concourse.bass as bass
from concourse import mybir

F32 = mybir.dt.float32
F32R = mybir.dt.float32r
ACT = mybir.ActivationFunctionType
ALU = mybir.AluOpType
AX_X = mybir.AxisListType.X

P = 128
D = 1024
KD = D // P
S, L = 512, 256
T = S + L
D_FF = P * ((8 * D + 3 * P - 1) // (3 * P))
BLOCKS = D_FF // (2 * P)
UNIT = 2048
N_MOD = 9
EPS = 1e-6
HEADS, NOPE, ROPE, DV = 8, 128, 64, 128
Q_RANK, KV_RANK = 384, 256
PAIRS = HEADS // 2
RET_HEADS, RET_DK, RET_DV = 4, 256, 512
FFN_UNITS = 3 * BLOCKS
MLA_PRE_UNITS, MLA_PAIR_UNITS, RET_UNITS = 3, 4, 8
N_UNITS = 4 * FFN_UNITS + MLA_PRE_UNITS + MLA_PAIR_UNITS * PAIRS + RET_UNITS * RET_HEADS
ADA_UNITS = 2 * N_MOD * D // 256
ADA_FIRST = 3 * D // 256
ADA_A, ADA_B = 3, 2
ADA_MID = ADA_UNITS - ADA_FIRST - (ADA_A + ADA_B) * BLOCKS
ADA_GATE = 4
Y_SETS = ((6, 7), (0, 2), (3, 5))
STREAMS = ((0, S), (S, L))

_cols = {}
_at = 0
for _name, _n in (("c", KD * 2), ("ada_b", 2 * N_MOD * KD), ("norm_g", 6 * KD * 2), ("q_norm", 3), ("kv_norm", 2),
                  ("qg_nope", 1), ("qg_rope", 1), ("kg_nope", 1), ("kg_rope", 1), ("gn", 16), ("log1m", 8)):
    _cols[_name] = (_at, _at + _n)
    _at += _n
N_VEC = _at
DIST_W = 896


class Count:

    def __init__(self):
        self.n, self.i, self.per = {}, None, {}

    def ahead(self, sem, n):
        k = self.n.get(sem.name, 0) + n
        if self.i is None or not self.per.get(sem.name):
            return k
        return self.i * self.per[sem.name] + k

    def next(self, sem, n=1):
        v = self.ahead(sem, n)
        self.n[sem.name] = self.n.get(sem.name, 0) + n
        return v

    @contextmanager
    def loop(self, eng, times, per):
        before = dict(self.n)
        self.per = {s.name: v for s, v in per.items()}
        with eng.Fori(0, times) as i:
            self.i = i
            yield i
        took = {k: v - before.get(k, 0) for k, v in self.n.items() if v != before.get(k, 0)}
        assert took == self.per, f"an iteration takes {took}"
        for k, v in took.items():
            self.n[k] = before.get(k, 0) + v * times
        self.i, self.per = None, {}


def build(nc, weights, ada, vecs, consts, x_in, rope_mla, rope_ret, dist_in, out):
    with ExitStack() as ctx:
        def sb(name, shape, dt=F32, where=ctx):
            return where.enter_context(nc.sbuf_tensor(name, shape, dt))

        def sem(name):
            return ctx.enter_context(nc.semaphore(name))

        ps = ctx.enter_context(nc.psum_tensor("ps", [P, 8, 512], F32))

        h = sb("h", [P, KD, T])
        xnh = sb("xnh", [P, KD, T], F32R)
        xnl = sb("xnl", [P, KD, T], F32R)
        raw = sb("raw", [P, 2, UNIT])
        wh = sb("wh", [P, 2, UNIT], F32R)
        wl = sb("wl", [P, 2, UNIT], F32R)
        mats = sb("mats", [P, 4 * P + 2])
        ones, ones64, swap, ident = (mats[:, i * P:i * P + P] for i in range(4))
        pick = mats[:, 4 * P:4 * P + 2]
        vec = sb("vec", [P, N_VEC])
        mods = sb("mods", [P, 2 * N_MOD * KD, 2])
        coef = sb("coef", [P, 2, KD, 2])
        c_act = sb("c_act", [P, KD, 32])
        lg = sb("lg", [P, 5, 8])
        row = sb("row", [P, 4, 2])
        eps = sb("eps", [P, 1])

        def v(name):
            a, b = _cols[name]
            return vec[:, a:b]

        ffn_mem = ExitStack()
        hidh = sb("hidh", [P, 2, 2, T], F32R, ffn_mem)
        hidl = sb("hidl", [P, 2, 2, T], F32R, ffn_mem)
        act_buf = sb("act_buf", [P, 2, T], F32, ffn_mem)
        ssum = sb("ssum", [P, T], F32, ffn_mem)
        rstd = sb("rstd", [P, T], F32, ffn_mem)
        adaw = sb("adaw", [P, 2, UNIT], F32, ffn_mem)
        ada_rows = sb("ada_rows", [P, 3, 256], F32, ffn_mem)
        ffn_mem.close()
        mla_mem = ExitStack()
        cqn = sb("cqn", [P, 2, 3, T], F32R, mla_mem)
        ckvn = sb("ckvn", [P, 2, 2, T], F32R, mla_mem)
        krr = sb("krr", [P, 2, T], F32R, mla_mem)
        qrr = sb("qrr", [P, 2, T], F32R, mla_mem)
        qn = sb("qn", [P, 2, 2, T], F32R, mla_mem)
        kn = sb("kn", [P, 2, 2, T], F32R, mla_mem)
        cs = sb("cs", [P, 2, S], F32, mla_mem)
        sqb = sb("sqb", [P, T], F32, mla_mem)
        nrm = sb("nrm", [P, 3, T], F32, mla_mem)
        mla_mem.close()
        ret_mem = ExitStack()
        rq = sb("rq", [P, 2, 2, S], F32R, ret_mem)
        rk = sb("rk", [P, 2, 2, T], F32R, ret_mem)
        rv = sb("rv", [P, 2, 6, 256], F32R, ret_mem)
        st = sb("st", [P, 2, 6, S], F32R, ret_mem)
        cr = sb("cr", [P, 2, S], F32, ret_mem)
        dist = sb("dist", [P, DIST_W], F32, ret_mem)
        dec = sb("dec", [P, 4, S], F32, ret_mem)
        rt = sb("rt", [P, 3, S], F32, ret_mem)
        rrs = sb("rrs", [P, S], F32, ret_mem)
        ret_mem.close()
        dec_flat = dec[:].rearrange("p a t -> p (a t)")
        rt_flat = rt[:].rearrange("p a t -> p (a t)")
        dec_lat, dec_ctx = dec_flat[:, 0:DIST_W], dec_flat[:, DIST_W:DIST_W + 640]
        xf = [t[:].rearrange("p k t -> p (k t)") for t in (xnh, xnl)]
        pt = [t[:, 0:3072].rearrange("p (k q) -> p k q", k=6) for t in xf]
        vv = [t[:, 3072:4608].rearrange("p (k e) -> p k e", k=6) for t in xf]
        oo = [t[:, 4608:6144].rearrange("p (j t) -> p j t", j=2) for t in xf]

        loaded = sem("loaded")
        raw_full = [sem(f"raw_full{s}") for s in range(2)]
        w_hi = [sem(f"w_hi{s}") for s in range(2)]
        w_ready = [sem(f"w_ready{s}") for s in range(2)]
        ada_full = [sem(f"ada_full{s}") for s in range(2)]
        ada_used, ada_part, ada_row = sem("ada_used"), sem("ada_part"), sem("ada_row")
        ada_psum, ada_evac = sem("ada_psum"), sem("ada_evac")
        tab_full = sem("tab_full")
        dve_step = sem("dve_step")
        setup_done = sem("setup_done")
        sq_done, sq_added, ms_full, std_done = sem("sq_done"), sem("sq_added"), sem("ms_full"), sem("std_done")
        prod_done, xn_hi, xn_ready = sem("prod_done"), sem("xn_hi"), sem("xn_ready")
        glu_full, silu_done, hid_done = sem("glu_full"), sem("silu_done"), sem("hid_done")
        hid_hi, hid_ready = sem("hid_hi"), sem("hid_ready")
        y_full, y_added = sem("y_full"), sem("y_added")
        item_full, item_sq, item_ms, item_std = sem("item_full"), sem("item_sq"), sem("item_ms"), sem("item_std")
        item_v, item_swapped, item_rot = sem("item_v"), sem("item_swapped"), sem("item_rot")
        item_hi, item_ready = sem("item_hi"), sem("item_ready")
        v_full, v_hi, v_ready = sem("v_full"), sem("v_hi"), sem("v_ready")
        s_full, max_done, exp_done, p_done = sem("s_full"), sem("max_done"), sem("exp_done"), sem("p_done")
        pt_full, pt_hi, pt_ready = sem("pt_full"), sem("pt_hi"), sem("pt_ready")
        o_full, o_hi, o_ready = sem("o_full"), sem("o_hi"), sem("o_ready")
        lg_ready, lg_step = sem("lg_ready"), sem("lg_step")
        dec_exp, dec_done = sem("dec_exp"), sem("dec_done")
        qk_full, qk_val, qk_hi, qk_ready = sem("qk_full"), sem("qk_val"), sem("qk_hi"), sem("qk_ready")
        sc_full, sc_val, sc_hi, sc_ready = sem("sc_full"), sem("sc_val"), sem("sc_hi"), sem("sc_ready")
        osum_ready, mu_full, cen_done = sem("osum_ready"), sem("mu_full"), sem("cen_done")
        vsq_done, vsq_added, var_full, rstd_done = sem("vsq_done"), sem("vsq_added"), sem("var_full"), sem("rstd_done")
        g_full, g_silu, g_val, g_hi, g_ready = sem("g_full"), sem("g_silu"), sem("g_val"), sem("g_hi"), sem("g_ready")
        stored = sem("stored")

        def mod_col(layer, which):
            a = (layer * N_MOD + which) * KD
            return mods[:, a:a + KD, :]

        block = ctx.enter_context(nc.Block())

        @block.sync
        def _(sp):
            c = Count()
            sp.dma_start(vec[:], vecs).then_inc(loaded, 16)
            sp.dma_start(mats[:], consts).then_inc(loaded, 16)
            sp.dma_start(h[:], x_in).then_inc(loaded, 16)
            for s in range(2):
                sp.dma_start(raw[:, s, :], weights[s]).then_inc(raw_full[s], 16)
            with c.loop(sp, (N_UNITS - 2) // 2, {w_ready[0]: 1, w_ready[1]: 1}) as i:
                for s in range(2):
                    sp.wait_ge(w_ready[s], c.next(w_ready[s]))
                    sp.dma_start(raw[:, s, :], weights[bass.ds(i * 2 + (2 + s), 1)].rearrange("u p e -> (u p) e")
                                 ).then_inc(raw_full[s], 16)
            if N_UNITS % 2:
                sp.wait_ge(w_ready[0], c.next(w_ready[0]))
                sp.dma_start(raw[:, 0, :], weights[N_UNITS - 1]).then_inc(raw_full[0], 16)
            c.next(y_added, KD * (3 * BLOCKS + 2 * PAIRS + 2 * RET_HEADS + BLOCKS - 1))
            for m in range(KD):
                sp.wait_ge(y_added, c.next(y_added))
                sp.dma_start(out[m], h[:, m, 0:S]).then_inc(stored, 16)
            sp.wait_ge(stored, 16 * KD)

        @block.gpsimd
        def _(pool):
            c = Count()
            for s in range(2):
                pool.dma_start(adaw[:, s, :], ada[s]).then_inc(ada_full[s], 16)

            def ada_loop(first, times):
                with c.loop(pool, times, {ada_used: 2}) as i:
                    for j in range(2):
                        s = (first + j) % 2
                        pool.wait_ge(ada_used, c.next(ada_used))
                        pool.dma_start(adaw[:, s, :], ada[bass.ds(i * 2 + (first + j), 1)].rearrange("u p e -> (u p) e")
                                       ).then_inc(ada_full[s], 16)
            mid = ADA_FIRST + ADA_A * BLOCKS + ADA_MID
            assert mid % 2 == 0 and ADA_UNITS % 2 == 0
            ada_loop(2, (mid - 2) // 2)
            c.next(ada_used, 2)
            c.next(xn_ready, KD)
            pool.wait_ge(xn_ready, c.next(xn_ready, KD))
            pool.dma_start(cs[:], rope_mla).then_inc(tab_full, 16)
            pool.wait_ge(xn_ready, c.next(xn_ready, KD))
            for s in range(2):
                pool.dma_start(adaw[:, s, :], ada[mid + s]).then_inc(ada_full[s], 16)
            ada_loop(mid + 2, (ADA_UNITS - mid - 2) // 2)
            pool.wait_ge(xn_ready, c.next(xn_ready, 2 * KD))
            pool.dma_start(cr[:], rope_ret).then_inc(tab_full, 16)
            pool.dma_start(dist[:], dist_in).then_inc(tab_full, 16)

        @block.tensor
        def _(pe):
            c = Count()
            mm = nc.tensor.matmul

            def three(dst, lhs, rhs, first, last, rows=slice(0, P)):
                mm(dst, lhs[1][rows], rhs[0][rows], start=first, stop=False)
                mm(dst, lhs[0][rows], rhs[1][rows], start=False, stop=False)
                return mm(dst, lhs[0][rows], rhs[0][rows], start=False, stop=last)

            def w(s, a, n=P):
                return wh[:, s, a:a + n], wl[:, s, a:a + n]

            def xn(k, a, n):
                return xnh[:, k, a:a + n], xnl[:, k, a:a + n]

            def ada_sums(first, n):
                for u in range(n):
                    s = (first + u) % 2
                    pe.wait_ge(ada_full[s], c.next(ada_full[s], 16))
                    col = 256 * (u % 2)
                    for k in range(KD):
                        j = 32 * (k % 4)
                        ins = mm(ps[j:j + 32, (1, 4)[u // 2], col:col + 256], c_act[:, k, :],
                                 adaw[:, s, k * 256:k * 256 + 256], start=(k < 4), stop=(k >= 4))
                    ins.then_inc(ada_used, 1)

            def ada_turn(n):
                pe.wait_ge(ada_row, c.next(ada_row))
                for u in range(n):
                    for j in range(2):
                        at = 256 + 4 * u + 2 * j
                        ins = mm(ps[:, 4, at:at + 2], ada_rows[:, u, j * P:j * P + P], pick, start=True, stop=True)
                ins.then_inc(ada_psum, 1)

            def mean_square():
                pe.wait_ge(sq_added, c.next(sq_added, KD))
                mm(ps[:, 6, :], ones, ssum[:, 0:S], start=True, stop=True)
                mm(ps[:, 7, 0:L], ones, ssum[:, S:T], start=True, stop=True).then_inc(ms_full, 1)

            def ffn(n_streams, ada_per, ada_first, slot, gate_units=0):
                streams = STREAMS[:n_streams]

                def up(j, s, first=False, wait_hid=True, y_left=0, wait_ada=False):
                    pe.wait_ge(w_ready[s], c.next(w_ready[s]))
                    if wait_hid:
                        pe.wait_ge(hid_done, c.next(hid_done))
                    if wait_ada:
                        pe.wait_ge(ada_evac, c.next(ada_evac))
                    for g, (half, bank, col, (t0, n)) in enumerate(
                            [(1, 3 * j + 1, 0, STREAMS[0]), (0, 3 * j, 0, STREAMS[0])] +
                            [(0, 3 * j + 2, 0, STREAMS[1]), (1, 3 * j + 2, L, STREAMS[1])] * (n_streams - 1)):
                        if g == 1 and y_left:
                            pe.wait_ge(y_added, c.next(y_added, y_left))
                        for k in range(KD):
                            if first and g == 0:
                                pe.wait_ge(xn_ready, c.next(xn_ready))
                            ins = three(ps[:, bank, col:col + n], w(s, k * 256 + half * P), xn(k, t0, n),
                                        k == 0, k == KD - 1)
                    ins.then_inc(glu_full, 1)

                def down(par, s, tail=False, ada_at=None):
                    pe.wait_ge(w_ready[s], c.next(w_ready[s]))
                    pe.wait_ge(hid_ready, c.next(hid_ready, 2))
                    for m in range(KD):
                        if m in (1, 2) and not tail:
                            pe.wait_ge(hid_done, c.ahead(hid_done, m))
                        if m >= 3:
                            pe.wait_ge(y_added, c.next(y_added))
                        for i, (t0, n) in enumerate(streams):
                            for kk in range(2):
                                ins = three(ps[:, Y_SETS[m % 3][i], 0:n], w(s, kk * D + m * P),
                                            (hidh[:, par, kk, t0:t0 + n], hidl[:, par, kk, t0:t0 + n]), kk == 0, kk == 1)
                        ins.then_inc(y_full, 1)
                        if m == 3 and ada_at is not None:
                            ada_sums(ada_at, ada_per)
                    if ada_at is not None:
                        ada_turn(ada_per)

                s0, s1 = slot, 1 - slot
                up(0, s0, first=True, wait_hid=False)
                up(1, s1, wait_hid=False)
                if gate_units:
                    pe.wait_ge(hid_done, c.ahead(hid_done, 2))
                    for g in range(0, gate_units, 2):
                        ada_sums(ada_first - gate_units + g, 2)
                        ada_turn(2)
                        pe.wait_ge(ada_evac, c.next(ada_evac))
                pre = 0
                if ada_per:
                    pe.wait_ge(hid_done, c.ahead(hid_done, 2))
                    ada_sums(ada_first, ada_per)
                    ada_turn(ada_per)
                    pre = ada_per

                per = {w_ready[0]: 3, w_ready[1]: 3, hid_done: 4, y_added: 16, hid_ready: 4}
                if ada_per:
                    per.update({ada_full[0]: 16 * ada_per, ada_full[1]: 16 * ada_per, ada_row: 2, ada_evac: 2})
                with c.loop(pe, BLOCKS // 2, per):
                    up(0, s0)
                    up(1, s1, wait_ada=bool(ada_per))
                    down(0, s0, ada_at=ada_first + pre if ada_per else None)
                    up(0, s1, y_left=3)
                    up(1, s0, wait_ada=bool(ada_per))
                    down(1, s1, ada_at=ada_first + pre + ada_per if ada_per else None)
                    pe.wait_ge(y_added, c.next(y_added, 3))
                down(0, s0, tail=True)
                pe.wait_ge(y_added, c.next(y_added, 3))
                c.next(hid_done, 2)
                if ada_per:
                    pe.wait_ge(ada_evac, c.next(ada_evac))
                return 1 - slot

            pe.wait_ge(loaded, 48)
            pe.wait_ge(setup_done, c.next(setup_done))
            for g in range(0, ADA_FIRST - ADA_GATE, 2):
                ada_sums(g, 2)
                ada_turn(2)
                pe.wait_ge(ada_evac, c.next(ada_evac))
            mean_square()
            slot = ffn(2, ADA_A, ADA_FIRST, 0, ADA_GATE)
            for g in range(0, ADA_MID, 3):
                n = min(3, ADA_MID - g)
                ada_sums(ADA_FIRST + ADA_A * BLOCKS + g, n)
                ada_turn(n)
                pe.wait_ge(ada_evac, c.next(ada_evac))
            mean_square()

            sets = ((0, 1), (2, 3), (4, 5))

            def project(n_item, lhs, rhs, ks, s=None, first=False):
                if n_item >= 3:
                    pe.wait_ge(item_v, c.next(item_v))
                for i, (t0, n) in enumerate(STREAMS):
                    for k in range(ks):
                        if first and i == 0:
                            pe.wait_ge(xn_ready, c.next(xn_ready))
                        ins = three(ps[:, sets[n_item % 3][i], 0:n], lhs(k), rhs(k, t0, n), k == 0, k == ks - 1)
                ins.then_inc(item_full, 1)

            def w_in(s, j):
                return lambda k: w(s, k * 256 + j * P)

            s0, s1 = slot, 1 - slot
            pe.wait_ge(w_ready[s0], c.next(w_ready[s0]))
            for n_item in range(6):
                s = (s0, s1, s0)[n_item // 2]
                if n_item in (2, 4):
                    pe.wait_ge(w_ready[s], c.next(w_ready[s]))
                project(n_item, w_in(s, n_item % 2), xn, KD, first=(n_item == 0))
                if n_item in (0, 1, 2):
                    pe.wait_ge(item_sq, c.next(item_sq))
                    mm(ps[:, 6, :], ones, sqb[:, 0:S], start=(n_item == 0), stop=(n_item == 2))
                    mm(ps[:, 7, 0:L], ones, sqb[:, S:T], start=(n_item == 0), stop=(n_item == 2)).then_inc(item_ms, 1)
                if n_item in (3, 4, 5):
                    pe.wait_ge(item_sq, c.next(item_sq))
                    if n_item in (3, 5):
                        pe.wait_ge(item_std, c.next(item_std))
                    mat = ones64 if n_item == 5 else ones
                    mm(ps[:, 6, :], mat, sqb[:, 0:S], start=(n_item != 4), stop=(n_item != 3))
                    mm(ps[:, 7, 0:L], mat, sqb[:, S:T], start=(n_item != 4), stop=(n_item != 3)).then_inc(item_ms, 1)
            pe.wait_ge(item_std, c.next(item_std))
            pe.wait_ge(item_v, c.next(item_v, 3))
            mm(ps[:, 6, :], swap, nrm[:, 2, 0:S], start=True, stop=True).then_inc(item_swapped, 1)
            pe.wait_ge(item_ready, c.next(item_ready, 6))
            c.next(item_rot)
            slot = s1

            tiles = [(hh, q) for hh in range(2) for q in (4, 5, 0, 1, 2, 3)]

            def scores(n, hh, q):
                if n >= 2:
                    pe.wait_ge(exp_done, c.next(exp_done))
                b = 2 * (n % 2)
                qs = slice(q * P, q * P + P)
                for t0, n_key in (STREAMS if q < 4 else STREAMS[1:]):
                    bank = ps[:, b + (t0 > 0), 0:n_key]
                    ks = slice(t0, t0 + n_key)
                    half = slice(ROPE * hh, ROPE * hh + ROPE)
                    three(bank, (qn[:, 0, hh, qs], qn[:, 1, hh, qs]), (kn[:, 0, hh, ks], kn[:, 1, hh, ks]), True, False)
                    ins = three(bank, (qrr[:, 0, qs], qrr[:, 1, qs]), (krr[:, 0, ks], krr[:, 1, ks]), False, True, half)
                ins.then_inc(s_full, 1)

            def turn(n, hh, q):
                pe.wait_ge(p_done, c.next(p_done))
                if n >= 1:
                    pe.wait_ge(pt_ready, c.next(pt_ready))
                for kc in (range(6) if q < 4 else (4, 5)):
                    ins = nc.tensor.transpose(ps[:, 4 + kc // 4, (kc % 4) * P:(kc % 4) * P + P],
                                              nrm[:, n % 2, kc * P:kc * P + P], ident)
                ins.then_inc(pt_full, 1)

            def weigh(hh, context):
                keys, q0, n, bank = ((4, 5), L, L, 7) if context else (range(6), 0, S, 6)
                for kc in keys:
                    ins = three(ps[:, bank, 0:n], (vv[0][:, kc, hh * DV:hh * DV + DV], vv[1][:, kc, hh * DV:hh * DV + DV]),
                                (pt[0][:, kc, q0:q0 + n], pt[1][:, kc, q0:q0 + n]), kc == keys[0], kc == keys[-1])
                ins.then_inc(o_full, 1)

            s0, s1 = slot, 1 - slot
            with c.loop(pe, PAIRS, {w_ready[0]: 2, w_ready[1]: 2, item_v: 5, item_sq: 5, item_std: 5,
                                    item_ready: 5, item_rot: 1, v_ready: 6, exp_done: 12, p_done: 12, pt_ready: 12, o_ready: 4,
                                    y_added: 16}):
                pe.wait_ge(w_ready[s0], c.next(w_ready[s0]))
                cq = lambda k, t0, n: (cqn[:, 0, k, t0:t0 + n], cqn[:, 1, k, t0:t0 + n])
                ckv = lambda k, t0, n: (ckvn[:, 0, k, t0:t0 + n], ckvn[:, 1, k, t0:t0 + n])

                def head_sum(mat):
                    pe.wait_ge(item_sq, c.next(item_sq))
                    mm(ps[:, 6, :], mat, sqb[:, 0:S], start=True, stop=True)
                    mm(ps[:, 7, 0:L], mat, sqb[:, S:T], start=True, stop=True).then_inc(item_ms, 1)
                    pe.wait_ge(item_std, c.next(item_std))

                project(0, lambda k: w(s0, k * 384 + 256), cq, 3)
                project(1, lambda k: w(s0, k * 384), cq, 3)
                head_sum(ones64)
                project(2, lambda k: w(s0, k * 384 + 128), cq, 3)
                pe.wait_ge(item_v, c.next(item_v))
                mm(ps[:, 6, :], swap, nrm[:, 0, 0:S], start=True, stop=True).then_inc(item_swapped, 1)
                pe.wait_ge(item_rot, c.next(item_rot))
                head_sum(ones)
                pe.wait_ge(w_ready[s1], c.next(w_ready[s1]))
                for i, (t0, n) in enumerate(STREAMS):
                    for k in range(2):
                        ins = three(ps[:, sets[0][i], 0:n], w(s1, k * 512), ckv(k, t0, n), k == 0, k == 1)
                ins.then_inc(item_full, 1)
                head_sum(ones)
                pe.wait_ge(item_v, c.next(item_v))
                for i, (t0, n) in enumerate(STREAMS):
                    for k in range(2):
                        ins = three(ps[:, sets[1][i], 0:n], w(s1, k * 512 + P), ckv(k, t0, n), k == 0, k == 1)
                ins.then_inc(item_full, 1)
                head_sum(ones)
                pe.wait_ge(item_v, c.next(item_v))
                for tc in range(6):
                    if tc == 3:
                        head_sum(ones)
                    if tc >= 2:
                        pe.wait_ge(v_ready, c.next(v_ready))
                    for k in range(2):
                        ins = three(ps[:, 4 + tc % 2, 0:256], ckv(k, tc * P, P), w(s1, k * 512 + 256, 256),
                                    k == 0, k == 1)
                    ins.then_inc(v_full, 1)
                c.next(item_v, 2)
                pe.wait_ge(item_ready, c.next(item_ready, 5))
                pe.wait_ge(v_ready, c.next(v_ready, 2))
                scores(0, *tiles[0])
                for n, (hh, q) in enumerate(tiles):
                    if n + 1 < len(tiles):
                        scores(n + 1, *tiles[n + 1])
                    if q == 1:
                        weigh(hh, True)
                    if q == 4 and hh == 1:
                        pe.wait_ge(pt_ready, c.ahead(pt_ready, 1))
                        weigh(0, False)
                    turn(n, hh, q)
                    if q == 0 and hh == 1:
                        pe.wait_ge(o_ready, c.next(o_ready, 2))
                pe.wait_ge(pt_ready, c.next(pt_ready))
                weigh(1, False)
                c.next(exp_done, 2)
                pe.wait_ge(o_ready, c.next(o_ready, 2))
                for kk, s in enumerate((s0, s1)):
                    pe.wait_ge(w_ready[s], c.next(w_ready[s]))
                    for n_y in range(KD * kk, KD * kk + KD):
                        if n_y >= 3:
                            pe.wait_ge(y_added, c.next(y_added))
                        for i, (t0, n) in enumerate(STREAMS):
                            ins = three(ps[:, Y_SETS[n_y % 3][i], 0:n], w(s, (n_y % KD) * P),
                                        (oo[0][:, kk, t0:t0 + n], oo[1][:, kk, t0:t0 + n]), True, True)
                        ins.then_inc(y_full, 1)
                pe.wait_ge(y_added, c.next(y_added, 3))
            mean_square()
            slot = ffn(2, ADA_B, ADA_FIRST + ADA_A * BLOCKS + ADA_MID, slot)
            mean_square()
            slot = ffn(2, 0, 0, slot)
            mean_square()

            s0, s1 = slot, 1 - slot

            def values(s, banks, first):
                pe.wait_ge(w_ready[s], c.next(w_ready[s]))
                for tc in range(6):
                    if tc >= 2:
                        pe.wait_ge(v_ready, c.next(v_ready))
                    for k in range(KD):
                        ins = three(ps[:, banks[tc % 2], 0:256], xn(k, tc * P, P), w(s, k * 256, 256),
                                    k == 0, k == KD - 1)
                    ins.then_inc(v_full, 1)
                pe.wait_ge(v_ready, c.next(v_ready, 2))

            def outputs(half):
                for j in range(2):
                    for jc in range(6):
                        ins = three(ps[:, 4 + 2 * half + j, :], (rv[:, 0, jc, j * P:j * P + P], rv[:, 1, jc, j * P:j * P + P]),
                                    (st[:, 0, jc, :], st[:, 1, jc, :]), jc == 0, jc == 5)
                    ins.then_inc(o_full, 1)

            pe.wait_ge(xn_ready, c.next(xn_ready, KD))
            with c.loop(pe, RET_HEADS, {w_ready[0]: 4, w_ready[1]: 4, v_ready: 12, qk_ready: 2, sc_ready: 6,
                                        osum_ready: 1, cen_done: 1, vsq_added: 4, g_ready: 4, y_added: 16}):
                pe.wait_ge(w_ready[s0], c.next(w_ready[s0]))
                for j in range(2):
                    for k in range(KD):
                        ins = three(ps[:, j, :], w(s0, k * 256 + j * P), xn(k, 0, S), k == 0, k == KD - 1)
                ins.then_inc(qk_full, 1)
                pe.wait_ge(w_ready[s1], c.next(w_ready[s1]))
                for i, (t0, n) in enumerate(STREAMS):
                    for j in range(2):
                        for k in range(KD):
                            ins = three(ps[:, 2 + 2 * i + j, 0:n], w(s1, k * 256 + j * P), xn(k, t0, n), k == 0, k == KD - 1)
                ins.then_inc(qk_full, 1)
                values(s0, (6, 7), True)
                pe.wait_ge(qk_ready, c.next(qk_ready, 2))
                for jc in range(6):
                    if jc >= 4:
                        pe.wait_ge(sc_ready, c.next(sc_ready))
                    for k in range(2):
                        ins = three(ps[:, jc % 4, :], (rk[:, 0, k, jc * P:jc * P + P], rk[:, 1, k, jc * P:jc * P + P]),
                                    (rq[:, 0, k, :], rq[:, 1, k, :]), k == 0, k == 1)
                    ins.then_inc(sc_full, 1)
                pe.wait_ge(sc_ready, c.next(sc_ready, 4))
                outputs(0)
                values(s1, (0, 1), False)
                outputs(1)
                pe.wait_ge(w_ready[s0], c.next(w_ready[s0]))

                def gate(j, s, bank):
                    for k in range(KD):
                        ins = three(ps[:, bank, :], w(s, k * 256 + (j % 2) * P), xn(k, 0, S), k == 0, k == KD - 1)
                    ins.then_inc(g_full, 1)
                gate(0, s0, 2)
                pe.wait_ge(osum_ready, c.next(osum_ready))
                mm(ps[:, 0, :], ones, rrs[:], start=True, stop=True).then_inc(mu_full, 1)
                gate(1, s0, 3)
                pe.wait_ge(vsq_added, c.next(vsq_added, 4))
                mm(ps[:, 1, :], ones, rrs[:], start=True, stop=True).then_inc(var_full, 1)
                pe.wait_ge(w_ready[s1], c.next(w_ready[s1]))
                pe.wait_ge(cen_done, c.next(cen_done))
                gate(2, s1, 4)
                gate(3, s1, 5)
                for half, s in enumerate((s0, s1)):
                    pe.wait_ge(g_ready, c.next(g_ready, 2))
                    pe.wait_ge(w_ready[s], c.next(w_ready[s]))
                    for n_y in range(KD * half, KD * half + KD):
                        if n_y >= 3:
                            pe.wait_ge(y_added, c.next(y_added))
                        for kk in range(2):
                            ins = three(ps[:, Y_SETS[n_y % 3][0], :], w(s, kk * D + (n_y % KD) * P),
                                        (st[:, 0, 2 * half + kk, :], st[:, 1, 2 * half + kk, :]), kk == 0, kk == 1)
                        ins.then_inc(y_full, 1)
                pe.wait_ge(y_added, c.next(y_added, 3))
            mean_square()
            ffn(1, 0, 0, slot)

        @block.scalar
        def _(act):
            c = Count()
            fn = nc.scalar.activation

            def split_hi(s):
                act.wait_ge(raw_full[s], c.next(raw_full[s], 16))
                fn(wh[:, s, :], raw[:, s, :], ACT.Copy).then_inc(w_hi[s], 1)

            def ada_copy(n):
                act.wait_ge(ada_used, c.next(ada_used, n))
                flat = ada_rows[:].rearrange("p u e -> p (u e)")
                ins = fn(flat[:, 0:512], ps[:, 1, :], ACT.Copy)
                if n == 3:
                    ins = fn(ada_rows[:, 2, :], ps[:, 4, 0:256], ACT.Copy)
                ins.then_inc(ada_row, 1)

            def squares(m, wait_h=True):
                if wait_h:
                    act.wait_ge(y_added, c.next(y_added))
                if m >= 2:
                    act.wait_ge(sq_added, c.next(sq_added))
                fn(act_buf[:, m % 2, :], h[:, m, :], ACT.Square).then_inc(sq_done, 1)

            def norm(layer, k, n_y=None):
                if n_y is not None:
                    if n_y:
                        act.wait_ge(y_added, c.next(y_added, n_y))
                    for m in range(KD):
                        squares(m, False)
                c.next(sq_added, 2)
                act.wait_ge(ms_full, c.next(ms_full))
                fn(rstd[:, 0:S], ps[:, 6, :], ACT.Sqrt, bias=eps[:, 0:1], scale=1.0 / D)
                fn(rstd[:, S:T], ps[:, 7, 0:L], ACT.Sqrt, bias=eps[:, 0:1], scale=1.0 / D).then_inc(std_done, 1)
                shift = mod_col(layer, 3 * k)
                for m in range(KD):
                    act.wait_ge(prod_done, c.next(prod_done))
                    for i, (t0, n) in enumerate(STREAMS):
                        ins = fn(xnh[:, m, t0:t0 + n], act_buf[:, m % 2, t0:t0 + n], ACT.Identity, bias=shift[:, m, i:i + 1])
                    ins.then_inc(xn_hi, 1)

            def ffn(n_streams, slot, ada_per=0, gate_units=0, last=False):
                n_tok = (S, T)[n_streams - 1]

                def up(j, par, s, wait_buf=True, refill=True):
                    act.wait_ge(glu_full, c.next(glu_full))
                    if wait_buf:
                        act.wait_ge(hid_ready, c.next(hid_ready))
                    ins = fn(act_buf[:, j, 0:S], ps[:, 3 * j, :], ACT.Silu)
                    if n_streams == 2:
                        ins = fn(act_buf[:, j, S:T], ps[:, 3 * j + 2, 0:L], ACT.Silu)
                    ins.then_inc(silu_done, 1)
                    act.wait_ge(hid_done, c.next(hid_done))
                    fn(hidh[:, par, j, 0:n_tok], act_buf[:, j, 0:n_tok], ACT.Copy).then_inc(hid_hi, 1)
                    if refill:
                        split_hi(s)

                def down(s, refill=True, ada=False):
                    if ada:
                        ada_copy(ada_per)
                    act.wait_ge(y_full, c.next(y_full, KD))
                    if refill:
                        split_hi(s)

                s0, s1 = slot, 1 - slot
                up(0, 0, s0, wait_buf=False)
                up(1, 0, s1, wait_buf=False)
                for g in range(0, gate_units, 2):
                    ada_copy(2)
                if ada_per:
                    ada_copy(ada_per)
                loops = BLOCKS // 2 - (1 if last else 0)

                def body(refill=True):
                    up(0, 1, s0)
                    up(1, 1, s1)
                    down(s0, ada=bool(ada_per))
                    up(0, 0, s1)
                    up(1, 0, s0, refill=refill)
                    down(s1, refill=refill, ada=bool(ada_per))
                per = {glu_full: 4, hid_ready: 4, hid_done: 4, y_full: 16, raw_full[0]: 48, raw_full[1]: 48}
                if ada_per:
                    per[ada_used] = 2 * ada_per
                with c.loop(act, loops, per):
                    body()
                if last:
                    up(0, 1, s0)
                    up(1, 1, s1)
                    down(s0)
                    up(0, 0, s1)
                    up(1, 0, s0)
                    down(s1, refill=False)
                if last:
                    return
                act.wait_ge(hid_ready, c.next(hid_ready, 2))
                c.next(y_added, KD * (BLOCKS - 1))
                for m in range(KD):
                    squares(m)
                down(s0)
                return 1 - slot

            split_hi(0)
            split_hi(1)
            act.wait_ge(loaded, 48)
            act.wait_ge(dve_step, c.next(dve_step, 2))
            fn(c_act[:, :, 0:2], v("c").rearrange("p (k j) -> p k j", j=2), ACT.Silu).then_inc(setup_done, 1)
            fn(lg[:, 0, :], v("log1m"), ACT.Exp).then_inc(lg_step, 1)
            act.wait_ge(lg_step, c.next(lg_step, 2))
            fn(lg[:, 2, :], lg[:, 1, :], ACT.Ln).then_inc(lg_step, 1)
            c.next(lg_step)
            for g in range(0, ADA_FIRST - ADA_GATE, 2):
                ada_copy(2)
            norm(0, 0, 0)
            slot = ffn(2, 0, ADA_A, ADA_GATE)
            for g in range(0, ADA_MID, 3):
                ada_copy(min(3, ADA_MID - g))
            norm(0, 1)

            s0, s1 = slot, 1 - slot
            sets = ((0, 1), (2, 3), (4, 5))

            def square(n_item, wait_sq=True):
                act.wait_ge(item_full, c.next(item_full))
                if wait_sq:
                    act.wait_ge(item_ms, c.ahead(item_ms, 0))
                fn(sqb[:, 0:S], ps[:, sets[n_item % 3][0], :], ACT.Square)
                fn(sqb[:, S:T], ps[:, sets[n_item % 3][1], 0:L], ACT.Square).then_inc(item_sq, 1)

            def root(i, dim, n_ms=1):
                act.wait_ge(item_ms, c.next(item_ms, n_ms))
                fn(nrm[:, i, 0:S], ps[:, 6, :], ACT.Sqrt, bias=eps[:, 0:1], scale=1.0 / dim)
                fn(nrm[:, i, S:T], ps[:, 7, 0:L], ACT.Sqrt, bias=eps[:, 0:1], scale=1.0 / dim).then_inc(item_std, 1)

            def hi(dst, src, wait=item_v, rot=False):
                act.wait_ge(wait, c.next(wait))
                fn(dst, src, ACT.Copy).then_inc(item_hi, 1)

            square(0, False)
            c.next(item_ms)
            act.wait_ge(item_ms, c.ahead(item_ms, 0))
            square(1, False)
            split_hi(s0)
            c.next(item_ms)
            act.wait_ge(item_ms, c.ahead(item_ms, 0))
            square(2, False)
            root(0, Q_RANK)
            for k in range(3):
                hi(cqn[:, 0, k, :], nrm[:, (1, 2, 0)[k], :])
                if k == 0:
                    square(3, False)
                    split_hi(s1)
                if k == 1:
                    c.next(item_ms)
                    act.wait_ge(item_ms, c.ahead(item_ms, 0))
                    square(4, False)
            root(1, KV_RANK)
            hi(ckvn[:, 0, 0, :], nrm[:, 2, :])
            square(5, False)
            split_hi(s0)
            hi(ckvn[:, 0, 1, :], nrm[:, 1, :])
            root(2, ROPE)
            c.next(item_v)
            hi(krr[:, 0, :], nrm[:, 2, :], item_rot)
            slot = s1

            tiles = [(hh, q) for hh in range(2) for q in (4, 5, 0, 1, 2, 3)]
            scale = (NOPE + ROPE) ** -0.5

            def exponent(n, hh, q):
                act.wait_ge(max_done, c.next(max_done))
                b, e = n % 2, n % 2
                cols = (0, T) if q < 4 else (S, T)
                flat = ps[:, 2 * b:2 * b + 2, :].rearrange("p b t -> p (b t)")
                fn(nrm[:, e, cols[0]:cols[1]], flat[:, cols[0]:cols[1]], ACT.Exp, bias=row[:, 0, b:b + 1], scale=scale,
                   accum_out=row[:, 1, b:b + 1]).then_inc(exp_done, 1)

            def turned(n, hh, q):
                act.wait_ge(pt_full, c.next(pt_full))
                if q < 4:
                    fn(pt[0][:, 0:4, q * P:q * P + P], ps[:, 4, :].rearrange("p (k q) -> p k q", k=4), ACT.Copy)
                q0 = q * P if q < 4 else L + (q - 4) * P
                fn(pt[0][:, 4:6, q0:q0 + P], ps[:, 5, 0:256].rearrange("p (k q) -> p k q", k=2), ACT.Copy
                   ).then_inc(pt_hi, 1)

            def attended(hh, context):
                act.wait_ge(o_full, c.next(o_full))
                t0, n = STREAMS[context]
                fn(oo[0][:, hh, t0:t0 + n], ps[:, 6 + context, 0:n], ACT.Copy).then_inc(o_hi, 1)

            s0, s1 = slot, 1 - slot
            with c.loop(act, PAIRS, {item_full: 5, item_ms: 5, item_v: 5, item_rot: 1, v_full: 6, max_done: 12,
                                     pt_full: 12, o_full: 4, y_full: 16, raw_full[0]: 32, raw_full[1]: 32}):
                square(0)
                root(0, ROPE)
                square(1, False)
                c.next(item_v)
                hi(qrr[:, 0, :], nrm[:, 0, :], item_rot)
                root(1, NOPE)
                square(2, False)
                split_hi(s0)
                hi(qn[:, 0, 0, :], nrm[:, 1, :])
                root(2, NOPE)
                square(3, False)
                hi(qn[:, 0, 1, :], nrm[:, 2, :])
                root(0, NOPE)
                square(4, False)
                hi(kn[:, 0, 0, :], nrm[:, 0, :])

                def value(tc):
                    act.wait_ge(v_full, c.next(v_full))
                    fn(vv[0][:, tc, :], ps[:, 4 + tc % 2, 0:256], ACT.Copy).then_inc(v_hi, 1)
                value(0)
                value(1)
                value(2)
                root(1, NOPE)
                hi(kn[:, 0, 1, :], nrm[:, 1, :])
                for tc in range(3, 6):
                    value(tc)
                split_hi(s1)
                exponent(0, *tiles[0])
                for n, (hh, q) in enumerate(tiles):
                    if n + 1 < len(tiles):
                        exponent(n + 1, *tiles[n + 1])
                    if q == 1:
                        attended(hh, 1)
                    if q == 4 and hh == 1:
                        attended(0, 0)
                    turned(n, hh, q)
                attended(1, 0)
                for s in (s0, s1):
                    act.wait_ge(y_full, c.next(y_full, KD))
                    split_hi(s)
            norm(0, 2, 2 * KD * PAIRS)
            slot = ffn(2, slot, ADA_B)
            norm(1, 0)
            slot = ffn(2, slot)
            norm(1, 1)

            s0, s1 = slot, 1 - slot

            def part(wait, done, dst, src):
                act.wait_ge(wait, c.next(wait))
                fn(dst, src, ACT.Copy).then_inc(done, 1)

            with c.loop(act, RET_HEADS, {dec_done: 1, qk_full: 2, qk_val: 4, v_full: 12, sc_val: 6, o_full: 4, cen_done: 1,
                                         vsq_added: 4, var_full: 1, g_full: 4, g_val: 4, y_full: 16,
                                         raw_full[0]: 64, raw_full[1]: 64}):
                act.wait_ge(dec_done, c.next(dec_done))
                fn(dec_lat, dec_lat, ACT.Exp)
                fn(dec_ctx, dec_ctx, ACT.Exp)
                fn(rt_flat[:, 0:640], rt_flat[:, 0:640], ACT.Exp).then_inc(dec_exp, 1)
                act.wait_ge(qk_full, c.next(qk_full))
                split_hi(s0)
                for j in range(2):
                    part(qk_val, qk_hi, rq[:, 0, j, :], rt[:, j, :])
                act.wait_ge(qk_full, c.next(qk_full))
                split_hi(s1)
                fn(rk[:, 0, 0, S:T], ps[:, 4, 0:L], ACT.Copy)
                fn(rk[:, 0, 1, S:T], ps[:, 5, 0:L], ACT.Copy).then_inc(qk_hi, 1)
                for j in range(2):
                    part(qk_val, qk_hi, rk[:, 0, j, 0:S], rt[:, j, :])
                for tc in range(6):
                    part(v_full, v_hi, rv[:, 0, tc, :], ps[:, 6 + tc % 2, 0:256])
                split_hi(s0)
                for jc in range(6):
                    part(sc_val, sc_hi, st[:, 0, jc, :], rt[:, jc % 2, :])
                act.wait_ge(o_full, c.next(o_full, 2))
                for tc in range(6):
                    part(v_full, v_hi, rv[:, 0, tc, :], ps[:, tc % 2, 0:256])
                split_hi(s1)
                c.next(o_full, 2)
                act.wait_ge(cen_done, c.next(cen_done))
                for j in range(4):
                    if j >= 2:
                        act.wait_ge(vsq_added, c.next(vsq_added))
                    fn(rt[:, j % 2, :], dec[:, j, :], ACT.Square).then_inc(vsq_done, 1)
                c.next(vsq_added, 2)
                act.wait_ge(var_full, c.next(var_full))
                fn(rrs[:], ps[:, 1, :], ACT.Sqrt, bias=eps[:, 0:1], scale=1.0 / RET_DV).then_inc(rstd_done, 1)
                for j in range(4):
                    act.wait_ge(g_full, c.next(g_full))
                    fn(rt[:, 2, :], ps[:, 2 + j, :], ACT.Silu).then_inc(g_silu, 1)
                    if j in (1, 3):
                        split_hi((s0, s1)[j // 2])
                    part(g_val, g_hi, st[:, 0, j, :], dec[:, j, :])
                for s in (s0, s1):
                    act.wait_ge(y_full, c.next(y_full, KD))
                    split_hi(s)
            norm(1, 2, 2 * KD * RET_HEADS)
            ffn(1, slot, last=True)

        @block.vector
        def _(dve):
            c = Count()
            tt, ts, stt = nc.vector.tensor_tensor, nc.vector.tensor_scalar, nc.vector.scalar_tensor_tensor

            def split_lo(s):
                dve.wait_ge(w_hi[s], c.next(w_hi[s]))
                tt(wl[:, s, :], raw[:, s, :], wh[:, s, :].bitcast(F32), ALU.subtract).then_inc(w_ready[s], 1)

            def step(ins):
                ins.then_inc(dve_step, 1)
                dve.wait_ge(dve_step, c.next(dve_step))

            def ada_out(chunk, n):
                dve.wait_ge(ada_psum, c.next(ada_psum))
                b0 = _cols["ada_b"][0]
                at = slice(chunk, chunk + 2 * n) if isinstance(chunk, int) else bass.ds(chunk, 2 * n)
                bias = vec[:, b0:b0 + 2 * N_MOD * KD].rearrange("p (k j) -> p k j", j=1)[:, at, :]
                tt(mods[:, at, :], ps[:, 4, 256:256 + 4 * n].rearrange("p (k j) -> p k j", j=2),
                   bias.to_broadcast([P, 2 * n, 2]), ALU.add).then_inc(ada_evac, 1)

            def gate_coefs(layer, k):
                step(ts(coef[:, 1, :, :], mod_col(layer, 3 * k + 2), 0.5 if k != 1 else 1.0, None, ALU.mult))

            def coefs(layer, k):
                g0 = _cols["norm_g"][0] + (layer * 3 + k) * 2 * KD
                gain = vec[:, g0:g0 + 2 * KD].rearrange("p (k j) -> p k j", j=2)
                step(stt(out=coef[:, 0, :, :], in0=mod_col(layer, 3 * k + 1), scalar=1.0, in1=gain,
                         op0=ALU.add, op1=ALU.mult))

            def add_square(m):
                dve.wait_ge(sq_done, c.next(sq_done))
                if m == 0:
                    nc.vector.tensor_copy(ssum[:], act_buf[:, 0, :]).then_inc(sq_added, 1)
                else:
                    dve.wait_ge(sq_added, c.next(sq_added))
                    tt(ssum[:], ssum[:], act_buf[:, m % 2, :], ALU.add).then_inc(sq_added, 1)

            def norm(layer, k, sums=False, gate=True):
                if sums:
                    for m in range(KD):
                        add_square(m)
                c.next(sq_added)
                coefs(layer, k)
                if gate:
                    gate_coefs(layer, k)
                dve.wait_ge(std_done, c.next(std_done))
                step(nc.vector.reciprocal(rstd[:], rstd[:]))
                shift = mod_col(layer, 3 * k)
                for m in range(KD + 1):
                    if m < KD:
                        if m >= 2:
                            dve.wait_ge(xn_ready, c.next(xn_ready))
                        for i, (t0, n) in enumerate(STREAMS):
                            ins = stt(out=act_buf[:, m % 2, t0:t0 + n], in0=h[:, m, t0:t0 + n], scalar=coef[:, 0, m, i:i + 1],
                                      in1=rstd[:, t0:t0 + n], op0=ALU.mult, op1=ALU.mult)
                        ins.then_inc(prod_done, 1)
                    if m >= 1:
                        dve.wait_ge(xn_hi, c.next(xn_hi))
                        for i, (t0, n) in enumerate(STREAMS):
                            ins = stt(out=xnl[:, m - 1, t0:t0 + n], in0=act_buf[:, (m - 1) % 2, t0:t0 + n],
                                      scalar=shift[:, m - 1, i:i + 1], in1=xnh[:, m - 1, t0:t0 + n].bitcast(F32),
                                      op0=ALU.add, op1=ALU.subtract)
                        ins.then_inc(xn_ready, 1)
                c.next(xn_ready, 2)

            def add_y(m, n_streams, n_y=None):
                n_y = m if n_y is None else n_y
                dve.wait_ge(y_full, c.next(y_full))
                for i, (t0, n) in enumerate(STREAMS[:n_streams]):
                    bank = Y_SETS[n_y % 3][i]
                    ins = stt(out=h[:, m, t0:t0 + n], in0=ps[:, bank, 0:n], scalar=coef[:, 1, m, i:i + 1],
                              in1=h[:, m, t0:t0 + n], op0=ALU.mult, op1=ALU.add)
                ins.then_inc(y_added, 1)

            def ffn(n_streams, slot, ada_per, ada_first, gate_units=0, last=False):
                n_tok = (S, T)[n_streams - 1]

                def up(j, par, s=None):
                    dve.wait_ge(silu_done, c.next(silu_done))
                    ins = tt(act_buf[:, j, 0:S], act_buf[:, j, 0:S], ps[:, 3 * j + 1, :], ALU.mult)
                    if n_streams == 2:
                        ins = tt(act_buf[:, j, S:T], act_buf[:, j, S:T], ps[:, 3 * j + 2, L:2 * L], ALU.mult)
                    ins.then_inc(hid_done, 1)
                    dve.wait_ge(hid_hi, c.next(hid_hi))
                    tt(hidl[:, par, j, 0:n_tok], act_buf[:, j, 0:n_tok], hidh[:, par, j, 0:n_tok].bitcast(F32),
                       ALU.subtract).then_inc(hid_ready, 1)
                    if s is not None:
                        split_lo(s)

                def down(s, s_mid=None, square=False):
                    for m in range(KD):
                        add_y(m, n_streams)
                        if square and m:
                            add_square(m - 1)
                        if m == 3 and s_mid is not None:
                            split_lo(s_mid)
                    if square:
                        add_square(KD - 1)
                    if s is not None:
                        split_lo(s)

                s0, s1 = slot, 1 - slot
                up(0, 0, s0)
                up(1, 0, s1)
                if gate_units:
                    for g in range(0, gate_units, 2):
                        ada_out(2 * (ada_first - gate_units + g), 2)
                    dve.wait_ge(ada_evac, c.ahead(ada_evac, 2))
                    gate_coefs(0, 0)
                if ada_per:
                    ada_out(2 * ada_first, ada_per)
                per = {silu_done: 4, hid_hi: 4, w_hi[0]: 3, w_hi[1]: 3, y_full: 16}
                if ada_per:
                    per[ada_psum] = 2
                with c.loop(dve, BLOCKS // 2 - (1 if last else 0), per) as i:
                    up(0, 1, s0)
                    up(1, 1)
                    down(s0, s1)
                    if ada_per:
                        ada_out(i * (4 * ada_per) + 2 * (ada_first + ada_per), ada_per)
                    up(0, 0, s1)
                    up(1, 0)
                    down(s1, s0)
                    if ada_per:
                        ada_out(i * (4 * ada_per) + 2 * (ada_first + 2 * ada_per), ada_per)
                if last:
                    up(0, 1, s0)
                    up(1, 1)
                    down(s0, s1)
                    up(0, 0, s1)
                    up(1, 0)
                    down(None, s0)
                down(None if last else s0, square=not last)
                return 1 - slot

            step(nc.vector.memset(eps[:], EPS))
            step(nc.vector.memset(c_act[:], 0.0))
            split_lo(0)
            split_lo(1)
            dve.wait_ge(loaded, 48)
            dve.wait_ge(lg_step, c.next(lg_step))
            ts(lg[:, 1, :], lg[:, 0, :], -1.0, 1.0, ALU.mult, ALU.add).then_inc(lg_step, 1)
            dve.wait_ge(lg_step, c.next(lg_step, 2))
            step(ts(lg[:, 3, :], lg[:, 1, :], 1.0, None, ALU.is_equal))
            stt(out=lg[:, 4, :], in0=lg[:, 1, :], scalar=-1.0, in1=lg[:, 3, :], op0=ALU.add, op1=ALU.add)
            step(tt(lg[:, 2, :], lg[:, 2, :], lg[:, 3, :], ALU.add))
            step(nc.vector.reciprocal(lg[:, 4, :], lg[:, 4, :]))
            step(tt(lg[:, 2, :], lg[:, 2, :], lg[:, 4, :], ALU.mult))
            step(tt(lg[:, 2, :], lg[:, 2, :], lg[:, 0, :], ALU.mult))
            step(ts(lg[:, 1, :], lg[:, 2, :], -1.0, None, ALU.mult))
            for g in range(0, ADA_FIRST - ADA_GATE, 2):
                ada_out(2 * g, 2)
            dve.wait_ge(ada_evac, c.next(ada_evac, (ADA_FIRST - ADA_GATE) // 2))
            norm(0, 0, sums=True, gate=False)
            slot = ffn(2, 0, ADA_A, ADA_FIRST, ADA_GATE)
            c.next(ada_evac, ADA_GATE // 2 + BLOCKS)
            for g in range(0, ADA_MID, 3):
                ada_out(2 * (ADA_FIRST + ADA_A * BLOCKS + g), min(3, ADA_MID - g))
                c.next(ada_evac)
            dve.wait_ge(ada_evac, c.ahead(ada_evac, 0))
            norm(0, 1)

            s0, s1 = slot, 1 - slot
            sets = ((0, 1), (2, 3), (4, 5))
            gate_cols = {n: v(n) for n in ("q_norm", "kv_norm", "qg_nope", "qg_rope", "kg_nope", "kg_rope")}

            def inverse(i):
                dve.wait_ge(item_std, c.next(item_std))
                step(nc.vector.reciprocal(nrm[:, i, :], nrm[:, i, :]))

            def scaled(n_item, i_rms, i_out, gain):
                for i, (t0, n) in enumerate(STREAMS):
                    ins = stt(out=nrm[:, i_out, t0:t0 + n], in0=ps[:, sets[n_item % 3][i], 0:n], scalar=gain,
                              in1=nrm[:, i_rms, t0:t0 + n], op0=ALU.mult, op1=ALU.mult)
                ins.then_inc(item_v, 1)

            def lo(dst, hi_part, src):
                dve.wait_ge(item_hi, c.next(item_hi))
                tt(dst, src, hi_part.bitcast(F32), ALU.subtract).then_inc(item_ready, 1)

            def rotated(i):
                dve.wait_ge(item_swapped, c.next(item_swapped))
                tt(nrm[:, i, 0:S], nrm[:, i, 0:S], cs[:, 0, :], ALU.mult)
                step(tt(ps[:, 6, :], ps[:, 6, :], cs[:, 1, :], ALU.mult))
                tt(nrm[:, i, 0:S], nrm[:, i, 0:S], ps[:, 6, :], ALU.add).then_inc(item_rot, 1)

            inverse(0)
            g = gate_cols["q_norm"]
            for k, i_out in enumerate((1, 2, 0)):
                scaled(k, 0, i_out, g[:, k:k + 1])
                lo(cqn[:, 1, k, :], cqn[:, 0, k, :], nrm[:, i_out, :])
                if k == 1:
                    split_lo(s0)
            split_lo(s1)
            inverse(1)
            g = gate_cols["kv_norm"]
            for k, i_out in enumerate((2, 1)):
                scaled(3 + k, 1, i_out, g[:, k:k + 1])
                lo(ckvn[:, 1, k, :], ckvn[:, 0, k, :], nrm[:, i_out, :])
            split_lo(s0)
            inverse(2)
            scaled(5, 2, 2, gate_cols["kg_rope"])
            dve.wait_ge(tab_full, 16)
            rotated(2)
            lo(krr[:, 1, :], krr[:, 0, :], nrm[:, 2, :])
            slot = s1

            tiles = [(hh, q) for hh in range(2) for q in (4, 5, 0, 1, 2, 3)]
            scale = (NOPE + ROPE) ** -0.5

            def maximum(n, hh, q):
                dve.wait_ge(s_full, c.next(s_full))
                b = n % 2
                cols = (0, T) if q < 4 else (S, T)
                flat = ps[:, 2 * b:2 * b + 2, :].rearrange("p b t -> p (b t)")
                step(nc.vector.reduce_max(row[:, 3, b:b + 1], flat[:, cols[0]:cols[1]], AX_X))
                ts(row[:, 0, b:b + 1], row[:, 3, b:b + 1], -scale, None, ALU.mult).then_inc(max_done, 1)

            def probabilities(n, hh, q):
                dve.wait_ge(exp_done, c.next(exp_done))
                b = n % 2
                cols = (0, T) if q < 4 else (S, T)
                step(nc.vector.reciprocal(row[:, 2, b:b + 1], row[:, 1, b:b + 1]))
                ts(nrm[:, b, cols[0]:cols[1]], nrm[:, b, cols[0]:cols[1]], row[:, 2, b:b + 1], None, ALU.mult
                   ).then_inc(p_done, 1)

            def turned(n, hh, q):
                dve.wait_ge(pt_hi, c.next(pt_hi))
                if q < 4:
                    tt(pt[1][:, 0:4, q * P:q * P + P], ps[:, 4, :].rearrange("p (k q) -> p k q", k=4),
                       pt[0][:, 0:4, q * P:q * P + P].bitcast(F32), ALU.subtract)
                q0 = q * P if q < 4 else L + (q - 4) * P
                tt(pt[1][:, 4:6, q0:q0 + P], ps[:, 5, 0:256].rearrange("p (k q) -> p k q", k=2),
                   pt[0][:, 4:6, q0:q0 + P].bitcast(F32), ALU.subtract).then_inc(pt_ready, 1)

            def attended(hh, context):
                dve.wait_ge(o_hi, c.next(o_hi))
                t0, n = STREAMS[context]
                tt(oo[1][:, hh, t0:t0 + n], ps[:, 6 + context, 0:n], oo[0][:, hh, t0:t0 + n].bitcast(F32),
                   ALU.subtract).then_inc(o_ready, 1)

            s0, s1 = slot, 1 - slot
            with c.loop(dve, PAIRS, {item_std: 5, item_hi: 5, item_swapped: 1, v_hi: 6, s_full: 12, exp_done: 12,
                                     pt_hi: 12, o_hi: 4, y_full: 16, w_hi[0]: 2, w_hi[1]: 2, dve_step: 5 + 1 + 24}):
                inverse(0)
                scaled(0, 0, 0, gate_cols["qg_rope"])
                rotated(0)
                lo(qrr[:, 1, :], qrr[:, 0, :], nrm[:, 0, :])
                inverse(1)
                scaled(1, 1, 1, gate_cols["qg_nope"])
                lo(qn[:, 1, 0, :], qn[:, 0, 0, :], nrm[:, 1, :])
                inverse(2)
                scaled(2, 2, 2, gate_cols["qg_nope"])
                split_lo(s0)
                lo(qn[:, 1, 1, :], qn[:, 0, 1, :], nrm[:, 2, :])
                inverse(0)
                scaled(3, 0, 0, gate_cols["kg_nope"])
                lo(kn[:, 1, 0, :], kn[:, 0, 0, :], nrm[:, 0, :])

                def value(tc):
                    dve.wait_ge(v_hi, c.next(v_hi))
                    tt(vv[1][:, tc, :], ps[:, 4 + tc % 2, 0:256], vv[0][:, tc, :].bitcast(F32), ALU.subtract
                       ).then_inc(v_ready, 1)
                for tc in range(3):
                    value(tc)
                inverse(1)
                scaled(4, 1, 1, gate_cols["kg_nope"])
                lo(kn[:, 1, 1, :], kn[:, 0, 1, :], nrm[:, 1, :])
                for tc in range(3, 6):
                    value(tc)
                split_lo(s1)
                maximum(0, *tiles[0])
                for n, (hh, q) in enumerate(tiles):
                    if n + 1 < len(tiles):
                        maximum(n + 1, *tiles[n + 1])
                    probabilities(n, hh, q)
                    if q == 1:
                        attended(hh, 1)
                    if q == 4 and hh == 1:
                        attended(0, 0)
                    turned(n, hh, q)
                attended(1, 0)
                for n_y in range(2 * KD):
                    add_y(n_y % KD, 2, n_y)
                    if n_y == KD + 1:
                        split_lo(s0)
                split_lo(s1)
            norm(0, 2, sums=True)
            slot = ffn(2, slot, ADA_B, ADA_FIRST + ADA_A * BLOCKS + ADA_MID)
            dve.wait_ge(ada_evac, c.next(ada_evac, BLOCKS))
            norm(1, 0)
            slot = ffn(2, slot, 0, 0)
            norm(1, 1)

            s0, s1 = slot, 1 - slot
            dve.wait_ge(tab_full, 48)
            c.next(o_full, 4 * PAIRS)
            gn0 = _cols["gn"][0]
            with c.loop(dve, RET_HEADS, {dec_exp: 1, qk_full: 2, qk_hi: 5, v_hi: 12, qk_ready: 2, sc_ready: 6, sc_full: 6, sc_hi: 6, o_full: 4,
                                         mu_full: 1, vsq_done: 4, vsq_added: 4, rstd_done: 1, g_silu: 4, g_hi: 4, y_full: 16,
                                         w_hi[0]: 4, w_hi[1]: 4, dve_step: 18}) as i:
                lgf, nlgb = lg[:, 1, bass.ds(i, 1)], lg[:, 2, bass.ds(i + RET_HEADS, 1)]
                ts(dec_lat, dist[:], 0.0, lgf, ALU.max, ALU.mult)
                step(ts(rt_flat[:, 0:DIST_W], dist[:], 0.0, nlgb, ALU.min, ALU.mult))
                step(tt(dec_lat, dec_lat, rt_flat[:, 0:DIST_W], ALU.add))
                ts(dec_ctx, dist[:, 256:DIST_W], float(L), lgf, ALU.add, ALU.mult)
                ts(rt_flat[:, 0:640], dist[:, 256:DIST_W], -float(S), nlgb, ALU.add, ALU.mult).then_inc(dec_done, 1)
                dve.wait_ge(dec_exp, c.next(dec_exp))
                step(tt(dec_ctx, dec_ctx, rt_flat[:, 0:640], ALU.add))

                def rotate(b):
                    cos, sin = cr[:, 0, :], cr[:, 1, :]
                    tt(rt[:, 0, :], ps[:, b, :], cos, ALU.mult)
                    step(tt(rt[:, 2, :], ps[:, b + 1, :], sin, ALU.mult))
                    tt(rt[:, 0, :], rt[:, 0, :], rt[:, 2, :], ALU.subtract).then_inc(qk_val, 1)
                    step(tt(rt[:, 1, :], ps[:, b + 1, :], cos, ALU.mult))
                    step(tt(rt[:, 2, :], ps[:, b, :], sin, ALU.mult))
                    tt(rt[:, 1, :], rt[:, 1, :], rt[:, 2, :], ALU.add).then_inc(qk_val, 1)

                dve.wait_ge(qk_full, c.next(qk_full))
                rotate(0)
                for j in range(2):
                    dve.wait_ge(qk_hi, c.next(qk_hi))
                    ins = tt(rq[:, 1, j, :], rt[:, j, :], rq[:, 0, j, :].bitcast(F32), ALU.subtract)
                ins.then_inc(qk_ready, 1)
                split_lo(s0)
                dve.wait_ge(qk_full, c.next(qk_full))
                dve.wait_ge(qk_hi, c.next(qk_hi))
                for j in range(2):
                    tt(rk[:, 1, j, S:T], ps[:, 4 + j, 0:L], rk[:, 0, j, S:T].bitcast(F32), ALU.subtract)
                dve.wait_ge(qk_ready, c.next(qk_ready))
                rotate(2)
                for j in range(2):
                    dve.wait_ge(qk_hi, c.next(qk_hi))
                    ins = tt(rk[:, 1, j, 0:S], rt[:, j, :], rk[:, 0, j, 0:S].bitcast(F32), ALU.subtract)
                ins.then_inc(qk_ready, 1)
                split_lo(s1)

                def value(tc, bank):
                    dve.wait_ge(v_hi, c.next(v_hi))
                    tt(rv[:, 1, tc, :], ps[:, bank, 0:256], rv[:, 0, tc, :].bitcast(F32), ALU.subtract
                       ).then_inc(v_ready, 1)
                for tc in range(6):
                    value(tc, 6 + tc % 2)
                split_lo(s0)
                dve.wait_ge(qk_ready, c.next(qk_ready))
                for jc in range(7):
                    if jc < 6:
                        if jc >= 2:
                            dve.wait_ge(sc_ready, c.next(sc_ready))
                        dve.wait_ge(sc_full, c.next(sc_full))
                        table = dec_flat[:, 384 - P * jc:384 - P * jc + S] if jc < 4 else \
                            dec_ctx[:, P * (5 - jc):P * (5 - jc) + S]
                        stt(out=rt[:, jc % 2, :], in0=ps[:, jc % 4, :], scalar=RET_DK ** -0.5, in1=table,
                            op0=ALU.mult, op1=ALU.mult).then_inc(sc_val, 1)
                    if jc >= 1:
                        dve.wait_ge(sc_hi, c.next(sc_hi))
                        tt(st[:, 1, jc - 1, :], rt[:, (jc - 1) % 2, :], st[:, 0, jc - 1, :].bitcast(F32),
                           ALU.subtract).then_inc(sc_ready, 1)
                for tc in range(6):
                    value(tc, tc % 2)
                split_lo(s1)
                c.next(sc_ready, 2)
                dve.wait_ge(o_full, c.next(o_full, 4))
                step(nc.vector.tensor_copy(rrs[:], ps[:, 4, :]))
                step(tt(rrs[:], rrs[:], ps[:, 5, :], ALU.add))
                step(tt(rrs[:], rrs[:], ps[:, 6, :], ALU.add))
                tt(rrs[:], rrs[:], ps[:, 7, :], ALU.add).then_inc(osum_ready, 1)
                dve.wait_ge(mu_full, c.next(mu_full))
                step(ts(rt[:, 2, :], ps[:, 0, :], -1.0 / RET_DV, None, ALU.mult))
                for j in range(4):
                    ins = tt(dec[:, j, :], ps[:, 4 + j, :], rt[:, 2, :], ALU.add)
                ins.then_inc(cen_done, 1)
                for j in range(4):
                    dve.wait_ge(vsq_done, c.next(vsq_done))
                    if j == 0:
                        nc.vector.tensor_copy(rrs[:], rt[:, 0, :]).then_inc(vsq_added, 1)
                    else:
                        dve.wait_ge(vsq_added, c.next(vsq_added))
                        tt(rrs[:], rrs[:], rt[:, j % 2, :], ALU.add).then_inc(vsq_added, 1)
                c.next(vsq_added)
                dve.wait_ge(rstd_done, c.next(rstd_done))
                step(nc.vector.reciprocal(rrs[:], rrs[:]))
                for j in range(4):
                    step(stt(out=dec[:, j, :], in0=dec[:, j, :], scalar=vec[:, bass.ds(i * 4 + (gn0 + j), 1)],
                             in1=rrs[:], op0=ALU.mult, op1=ALU.mult))
                    dve.wait_ge(g_silu, c.next(g_silu))
                    tt(dec[:, j, :], dec[:, j, :], rt[:, 2, :], ALU.mult).then_inc(g_val, 1)
                    if j in (1, 3):
                        split_lo((s0, s1)[j // 2])
                    dve.wait_ge(g_hi, c.next(g_hi))
                    tt(st[:, 1, j, :], dec[:, j, :], st[:, 0, j, :].bitcast(F32), ALU.subtract).then_inc(g_ready, 1)
                for n_y in range(2 * KD):
                    add_y(n_y % KD, 1, n_y)
                    if n_y == KD + 1:
                        split_lo(s0)
                split_lo(s1)
            norm(1, 2, sums=True)
            ffn(1, slot, 0, 0, last=True)


def _chunks(w, n_out):
    i, o = w.shape
    return w.reshape(i // P, P, o // n_out, n_out).transpose(2, 1, 0, 3).reshape(o // n_out, P, -1)


def _rows(w, n_in):
    i, o = w.shape
    return w.reshape(i // (P * n_in), n_in, P, o).transpose(0, 2, 1, 3).reshape(i // (P * n_in), P, -1)


def _pad(u):
    full = np.zeros((u.shape[0], UNIT), u.dtype)
    full[:, :u.shape[1]] = u
    return full


def _ffn_units(w_in, w_out):
    a, b = _chunks(w_in[:, :D_FF], P), _chunks(w_in[:, D_FF:], P)
    up = np.concatenate([a.reshape(-1, P, KD, P), b.reshape(-1, P, KD, P)], 3).reshape(-1, P, UNIT)
    down = _rows(w_out, 2)
    order = [up[0], up[1]]
    for blk in range(1, BLOCKS):
        order += [up[2 * blk], up[2 * blk + 1], down[blk - 1]]
    return order + [down[BLOCKS - 1]]


def _mla_units(w_in, w_uq, w_ukv, w_o):
    w_in = np.concatenate([w_in, w_in[:, Q_RANK + KV_RANK:]], 1)
    order = list(_chunks(w_in, 256))
    uq = w_uq.reshape(Q_RANK, HEADS, NOPE + ROPE)
    ukv = w_ukv.reshape(KV_RANK, HEADS, NOPE + DV)
    for p in range(PAIRS):
        a, b = 2 * p, 2 * p + 1
        q = np.concatenate([uq[:, a, :NOPE], uq[:, b, :NOPE], uq[:, a, NOPE:], uq[:, b, NOPE:]], 1)
        kv = np.concatenate([ukv[:, a, :NOPE], ukv[:, b, :NOPE], ukv[:, a, NOPE:], ukv[:, b, NOPE:]], 1)
        order += [_pad(_rows(q, 3)[0]), _pad(_rows(kv, 2)[0])]
        order += [_pad(w_o[a * P:a * P + P]), _pad(w_o[b * P:b * P + P])]
    return order


def _ret_units(w_in, w_o):
    hdk, hdv = RET_HEADS * RET_DK, RET_HEADS * RET_DV
    u = _chunks(w_in, 256)
    q, k, val, gate = u[:4], u[4:8], u[8:16], u[16:24]
    o = _rows(w_o, 2)
    order = []
    for n in range(RET_HEADS):
        order += [q[n], k[n], val[2 * n], val[2 * n + 1], gate[2 * n], gate[2 * n + 1], o[2 * n], o[2 * n + 1]]
    return order


def _angles(pos, dim):
    inv = (np.float32(10000.0) ** (-np.arange(0, dim, 2, dtype=np.float32) / np.float32(dim))).astype(np.float32)
    return pos.astype(np.float32)[:, None] * inv[None, :]


def _tables():
    mats = np.zeros((P, 4 * P + 2), np.float32)
    mats[:, 0:P] = 1.0
    mats[:64, P:P + 64] = mats[64:, P + 64:2 * P] = 1.0
    for p in range(P):
        mats[p ^ 16, 2 * P + p] = 1.0
        mats[p, 3 * P + p] = 1.0
        if p % 32 < 2:
            mats[p, 4 * P + p % 32] = 1.0
    pos = np.arange(S)
    a_row, a_col = _angles(pos // 64, 32), _angles(pos % 64, 32)
    ang = np.concatenate([a_row, a_row, a_col, a_col], 1).T
    sign = np.where((np.arange(64) & 16) == 0, -1.0, 1.0).astype(np.float32)[:, None]
    rope = np.stack([np.cos(ang), np.sin(ang) * sign], 1)
    rope = np.concatenate([rope, rope], 0).astype(np.float32)
    ang = _angles(pos, RET_DK).T
    ret = np.stack([np.cos(ang), np.sin(ang)], 1).astype(np.float32)
    dist = (np.arange(DIST_W)[None, :] - 384 - np.arange(P)[:, None]).astype(np.float32)
    return mats, rope, ret, dist


def kernel(**inputs):
    import concourse.bacc as _bacc
    from concourse.bass_utils import run_bass_kernel_spmd as _run

    a = {k: np.asarray(t) for k, t in inputs.items()}
    units = []
    fi, fo = a["ffn_w_in"], a["ffn_w_out"]
    units += _ffn_units(fi[0, 0], fo[0, 0])
    units += _mla_units(a["mla_w_in"][0], a["mla_w_uq"][0], a["mla_w_ukv"][0], a["mla_w_o"][0])
    units += _ffn_units(fi[0, 1], fo[0, 1]) + _ffn_units(fi[1, 0], fo[1, 0])
    units += _ret_units(a["ret_w_in"][0], a["ret_w_o"][0])
    units += _ffn_units(fi[1, 1], fo[1, 1])
    weights = np.stack(units)
    assert weights.shape == (N_UNITS, P, UNIT)
    ada = np.concatenate([_chunks(a["ada_w"][i], 256) for i in range(2)])

    def col(x):
        return x.reshape(-1, P).T

    def twice(x):
        return np.repeat(col(x), 2, axis=1)
    c2 = np.stack([col(a["c"][0]), col(a["c_ctx"])], 2).reshape(P, -1)
    qg, kg = a["mla_q_gain"][0], a["mla_k_gain"][0]
    vecs = np.concatenate([
        c2, col(a["ada_b"]), twice(a["norm_g"]), col(a["mla_q_norm"][0]), col(a["mla_kv_norm"][0]),
        col(qg[:NOPE]), col(np.concatenate([qg[NOPE:]] * 2)), col(kg[:NOPE]), col(np.concatenate([kg[NOPE:]] * 2)),
        col(a["ret_gn_gain"][0]), np.broadcast_to(a["ret_log1m_gamma"][0].reshape(1, 8), (P, 8))], 1)
    assert vecs.shape == (P, N_VEC)
    x = np.concatenate([a["x"][0], a["ctx"][0]], 0).T.reshape(KD, P, T).transpose(1, 0, 2)
    mats, rope, ret, dist = _tables()
    arrays = {"weights": weights, "ada": ada, "vecs": vecs, "consts": mats, "x_in": x, "rope_mla": rope,
              "rope_ret": ret, "dist_in": dist}
    arrays = {k: np.ascontiguousarray(t) for k, t in arrays.items()}
    nc = _bacc.Bacc("TRN2", target_bir_lowering=False, num_devices=1)
    args = [nc.dram_tensor(k, t.shape, F32, kind="ExternalInput").ap() for k, t in arrays.items()]
    out = nc.dram_tensor("out", (KD, P, S), F32, kind="ExternalOutput").ap()
    build(nc, *args, out)
    r = _run(nc, [arrays], core_ids=[0])
    return np.ascontiguousarray(r.results[0]["out"].reshape(D, S).T)[None]
```

```python
from contextlib import ExitStack, contextmanager

import numpy as np
import concourse.bass as bass
from concourse import mybir

F32 = mybir.dt.float32
F32R = mybir.dt.float32r
ACT = mybir.ActivationFunctionType
ALU = mybir.AluOpType
AX_X = mybir.AxisListType.X

P = 128
D = 1024
KD = D // P
S, L = 512, 256
T = S + L
D_FF = P * ((8 * D + 3 * P - 1) // (3 * P))
BLOCKS = D_FF // (2 * P)
UNIT = 2048
N_MOD = 9
EPS = 1e-6
HEADS, NOPE, ROPE, DV = 8, 128, 64, 128
Q_RANK, KV_RANK = 384, 256
PAIRS = HEADS // 2
RET_HEADS, RET_DK, RET_DV = 4, 256, 512
FFN_UNITS = 3 * BLOCKS
MLA_PRE_UNITS, MLA_PAIR_UNITS, RET_UNITS = 3, 4, 8
N_UNITS = 4 * FFN_UNITS + MLA_PRE_UNITS + MLA_PAIR_UNITS * PAIRS + RET_UNITS * RET_HEADS
ADA_UNITS = 2 * N_MOD * D // 256
ADA_FIRST = 3 * D // 256
ADA_PER = 2
ADA_0 = ADA_FIRST
ADA_1 = ADA_0 + ADA_PER * (BLOCKS + 1)
ADA_2 = ADA_1 + ADA_PER * BLOCKS
assert ADA_2 + ADA_PER * (BLOCKS // 2 + 2) == ADA_UNITS
ADA_GATE = 4
Y_SETS = ((6, 7), (0, 2), (3, 5))
STREAMS = ((0, S), (S, L))

_cols = {}
_at = 0
for _name, _n in (("c", KD * 2), ("ada_b", 2 * N_MOD * KD), ("norm_g", 6 * KD * 2), ("q_norm", 3), ("kv_norm", 2),
                  ("qg_nope", 1), ("qg_rope", 1), ("kg_nope", 1), ("kg_rope", 1), ("gn", 16), ("log1m", 8)):
    _cols[_name] = (_at, _at + _n)
    _at += _n
N_VEC = _at
N_MATS = 2 * P + 74
DIST_W = 896


class Count:

    def __init__(self):
        self.n, self.i, self.per = {}, None, {}

    def ahead(self, sem, n):
        k = self.n.get(sem.name, 0) + n
        if self.i is None or not self.per.get(sem.name):
            return k
        return self.i * self.per[sem.name] + k

    def next(self, sem, n=1):
        v = self.ahead(sem, n)
        self.n[sem.name] = self.n.get(sem.name, 0) + n
        return v

    @contextmanager
    def loop(self, eng, times, per):
        before = dict(self.n)
        self.per = {s.name: v for s, v in per.items()}
        with eng.Fori(0, times) as i:
            self.i = i
            yield i
        took = {k: v - before.get(k, 0) for k, v in self.n.items() if v != before.get(k, 0)}
        assert took == self.per, f"an iteration takes {took}"
        for k, v in took.items():
            self.n[k] = before.get(k, 0) + v * times
        self.i, self.per = None, {}


def build(nc, weights, ada, vecs, consts, x_in, rope_mla, rope_ret, dist_in, out):
    with ExitStack() as ctx:
        def sb(name, shape, dt=F32, where=ctx):
            return where.enter_context(nc.sbuf_tensor(name, shape, dt))

        def sem(name):
            return ctx.enter_context(nc.semaphore(name))

        ps = ctx.enter_context(nc.psum_tensor("ps", [P, 8, 512], F32))

        h = sb("h", [P, KD, T])
        xnh = sb("xnh", [P, KD, T], F32R)
        xnl = sb("xnl", [P, KD, T], F32R)
        raw = sb("raw", [P, 2, UNIT])
        wh = sb("wh", [P, 2, UNIT], F32R)
        wl = sb("wl", [P, 2, UNIT], F32R)
        mats = sb("mats", [P, N_MATS])
        swap, ident = mats[:, 0:P], mats[:, P:2 * P]
        ones, ones64 = mats[:, 2 * P:2 * P + 32], mats[:, 2 * P + 32:2 * P + 64]
        pick = mats[:, 2 * P + 64:2 * P + 66]
        quarter = mats[:, 2 * P + 66:N_MATS]
        vec = sb("vec", [P, N_VEC])
        mods = sb("mods", [P, 2 * N_MOD * KD, 2])
        coef = sb("coef", [P, 2, KD, 2])
        c_act = sb("c_act", [P, KD, 32])
        lg = sb("lg", [P, 5, 8])
        row = sb("row", [P, 3, 2])
        eps = sb("eps", [P, 1])

        def v(name):
            a, b = _cols[name]
            return vec[:, a:b]

        ffn_mem = ExitStack()
        hidh = sb("hidh", [P, 2, 2, T], F32R, ffn_mem)
        hidl = sb("hidl", [P, 2, 2, T], F32R, ffn_mem)
        act_buf = sb("act_buf", [P, 2, T], F32, ffn_mem)
        ssum = sb("ssum", [P, T], F32, ffn_mem)
        rms = sb("rms", [P, T // 4], F32, ffn_mem)
        adaw = sb("adaw", [P, 2, UNIT], F32, ffn_mem)
        ada_rows = sb("ada_rows", [P, ADA_PER, 256], F32, ffn_mem)
        ffn_mem.close()
        mla_mem = ExitStack()
        cqn = sb("cqn", [P, 2, 3, T], F32R, mla_mem)
        ckvn = sb("ckvn", [P, 2, 2, T], F32R, mla_mem)
        krr = sb("krr", [P, 2, T], F32R, mla_mem)
        qrr = sb("qrr", [P, 2, T], F32R, mla_mem)
        qn = sb("qn", [P, 2, 2, T], F32R, mla_mem)
        kn = sb("kn", [P, 2, 2, T], F32R, mla_mem)
        cs = sb("cs", [P, 2, S], F32, mla_mem)
        sqb = sb("sqb", [P, T], F32, mla_mem)
        nrm = sb("nrm", [P, 3, T], F32, mla_mem)
        irms = sb("irms", [P, T // 4], F32, mla_mem)
        mla_mem.close()
        ret_mem = ExitStack()
        rq = sb("rq", [P, 2, 2, S], F32R, ret_mem)
        rk = sb("rk", [P, 2, 2, T], F32R, ret_mem)
        rv = sb("rv", [P, 2, 6, 256], F32R, ret_mem)
        st = sb("st", [P, 2, 6, S], F32R, ret_mem)
        cr = sb("cr", [P, 2, S], F32, ret_mem)
        dist = sb("dist", [P, DIST_W], F32, ret_mem)
        dec = sb("dec", [P, 4, S], F32, ret_mem)
        rt = sb("rt", [P, 3, S], F32, ret_mem)
        rrs = sb("rrs", [P, S], F32, ret_mem)
        ret_mem.close()
        dec_flat = dec[:].rearrange("p a t -> p (a t)")
        rt_flat = rt[:].rearrange("p a t -> p (a t)")
        dec_lat, dec_ctx = dec_flat[:, 0:DIST_W], dec_flat[:, DIST_W:DIST_W + 640]
        xf = [t[:].rearrange("p k t -> p (k t)") for t in (xnh, xnl)]
        pt = [t[:, 0:3072].rearrange("p (k q) -> p k q", k=6) for t in xf]
        vv = [t[:, 3072:4608].rearrange("p (k e) -> p k e", k=6) for t in xf]
        oo = [t[:, 4608:6144].rearrange("p (j t) -> p j t", j=2) for t in xf]

        loaded, x_loaded = sem("loaded"), sem("x_loaded")
        raw_full = [sem(f"raw_full{s}") for s in range(2)]
        w_hi = [sem(f"w_hi{s}") for s in range(2)]
        w_ready = [sem(f"w_ready{s}") for s in range(2)]
        ada_full = [sem(f"ada_full{s}") for s in range(2)]
        ada_used, ada_part, ada_row = sem("ada_used"), sem("ada_part"), sem("ada_row")
        ada_psum, ada_evac = sem("ada_psum"), sem("ada_evac")
        tab_full = sem("tab_full")
        dve_step = sem("dve_step")
        setup_done = sem("setup_done")
        sq_done, sq_added, ms_full, std_done = sem("sq_done"), sem("sq_added"), sem("ms_full"), sem("std_done")
        rms_ready, rms_full = sem("rms_ready"), sem("rms_full")
        prod_done, xn_hi, xn_ready = sem("prod_done"), sem("xn_hi"), sem("xn_ready")
        glu_full, silu_done, hid_done = sem("glu_full"), sem("silu_done"), sem("hid_done")
        hid_hi, hid_ready = sem("hid_hi"), sem("hid_ready")
        y_full, y_added = sem("y_full"), sem("y_added")
        item_full, item_sq, item_ms, item_std = sem("item_full"), sem("item_sq"), sem("item_ms"), sem("item_std")
        item_inv, item_rms = sem("item_inv"), sem("item_rms")
        item_v, item_swapped, item_rot = sem("item_v"), sem("item_swapped"), sem("item_rot")
        item_hi, item_ready = sem("item_hi"), sem("item_ready")
        v_full, v_hi, v_ready = sem("v_full"), sem("v_hi"), sem("v_ready")
        s_full, max_done, exp_done, p_done = sem("s_full"), sem("max_done"), sem("exp_done"), sem("p_done")
        pt_full, pt_hi, pt_ready = sem("pt_full"), sem("pt_hi"), sem("pt_ready")
        wo_used = sem("wo_used")
        o_full, o_hi, o_ready = sem("o_full"), sem("o_hi"), sem("o_ready")
        lg_ready, lg_step = sem("lg_ready"), sem("lg_step")
        dec_exp, dec_done = sem("dec_exp"), sem("dec_done")
        qk_full, qk_val, qk_hi, qk_ready = sem("qk_full"), sem("qk_val"), sem("qk_hi"), sem("qk_ready")
        sc_full, sc_val, sc_hi, sc_ready = sem("sc_full"), sem("sc_val"), sem("sc_hi"), sem("sc_ready")
        osum_ready, mu_full, cen_done = sem("osum_ready"), sem("mu_full"), sem("cen_done")
        vsq_done, vsq_added, var_full, rstd_done = sem("vsq_done"), sem("vsq_added"), sem("var_full"), sem("rstd_done")
        g_full, g_silu, g_val, g_hi, g_ready = sem("g_full"), sem("g_silu"), sem("g_val"), sem("g_hi"), sem("g_ready")
        stored = sem("stored")

        def two_tiles(bank):
            return ps[:, bank, :].rearrange("p (t e) -> p t e", t=2)

        def mod_col(layer, which):
            a = (layer * N_MOD + which) * KD
            return mods[:, a:a + KD, :]

        block = ctx.enter_context(nc.Block())

        @block.sync
        def _(sp):
            c = Count()
            sp.dma_start(vec[:], vecs).then_inc(loaded, 16)
            sp.dma_start(mats[:], consts).then_inc(loaded, 16)
            sp.dma_start(h[:], x_in).then_inc(x_loaded, 16)
            for s in range(2):
                sp.dma_start(raw[:, s, :], weights[s]).then_inc(raw_full[s], 16)
            with c.loop(sp, (N_UNITS - 2) // 2, {w_ready[0]: 1, w_ready[1]: 1}) as i:
                for s in range(2):
                    sp.wait_ge(w_ready[s], c.next(w_ready[s]))
                    sp.dma_start(raw[:, s, :], weights[bass.ds(i * 2 + (2 + s), 1)].rearrange("u p e -> (u p) e")
                                 ).then_inc(raw_full[s], 16)
            if N_UNITS % 2:
                sp.wait_ge(w_ready[0], c.next(w_ready[0]))
                sp.dma_start(raw[:, 0, :], weights[N_UNITS - 1]).then_inc(raw_full[0], 16)
            c.next(y_added, KD * (3 * BLOCKS + PAIRS + 2 * RET_HEADS + BLOCKS - 1))
            for m in range(KD):
                sp.wait_ge(y_added, c.next(y_added))
                sp.dma_start(out[m], h[:, m, 0:S]).then_inc(stored, 16)
            sp.wait_ge(stored, 16 * KD)

        @block.gpsimd
        def _(pool):
            c = Count()
            for s in range(2):
                pool.dma_start(adaw[:, s, :], ada[s]).then_inc(ada_full[s], 16)

            def ada_loop(first, times):
                with c.loop(pool, times, {ada_used: 2}) as i:
                    for j in range(2):
                        s = (first + j) % 2
                        pool.wait_ge(ada_used, c.next(ada_used))
                        pool.dma_start(adaw[:, s, :], ada[bass.ds(i * 2 + (first + j), 1)].rearrange("u p e -> (u p) e")
                                       ).then_inc(ada_full[s], 16)
            mid = ADA_1
            assert mid % 2 == 0 and ADA_UNITS % 2 == 0
            ada_loop(2, (mid - 2) // 2)
            c.next(ada_used, 2)
            c.next(xn_ready, KD)
            pool.wait_ge(xn_ready, c.next(xn_ready, KD))
            pool.dma_start(cs[:], rope_mla).then_inc(tab_full, 16)
            pool.wait_ge(xn_ready, c.next(xn_ready, KD))
            for s in range(2):
                pool.dma_start(adaw[:, s, :], ada[mid + s]).then_inc(ada_full[s], 16)
            ada_loop(mid + 2, (ADA_UNITS - mid - 2) // 2)
            pool.wait_ge(xn_ready, c.next(xn_ready, 2 * KD))
            pool.dma_start(cr[:], rope_ret).then_inc(tab_full, 16)
            pool.dma_start(dist[:], dist_in).then_inc(tab_full, 16)

        @block.tensor
        def _(pe):
            c = Count()
            mm = nc.tensor.matmul

            def three(dst, lhs, rhs, first, last, rows=slice(0, P)):
                mm(dst, lhs[1][rows], rhs[0][rows], start=first, stop=False)
                mm(dst, lhs[0][rows], rhs[1][rows], start=False, stop=False)
                return mm(dst, lhs[0][rows], rhs[0][rows], start=False, stop=last)

            def w(s, a, n=P):
                return wh[:, s, a:a + n], wl[:, s, a:a + n]

            def xn(k, a, n):
                return xnh[:, k, a:a + n], xnl[:, k, a:a + n]

            def ada_sums(first):
                for u in range(ADA_PER):
                    s = (first + u) % 2
                    pe.wait_ge(ada_full[s], c.next(ada_full[s], 16))
                    col = 256 * u
                    for k in range(KD):
                        j = 32 * (k % 4)
                        ins = mm(ps[j:j + 32, 1, col:col + 256], c_act[:, k, :],
                                 adaw[:, s, k * 256:k * 256 + 256], start=(k < 4), stop=(k >= 4))
                    ins.then_inc(ada_used, 1)

            def ada_turn():
                pe.wait_ge(ada_row, c.next(ada_row))
                for u in range(ADA_PER):
                    for j in range(2):
                        at = 256 + 4 * u + 2 * j
                        ins = mm(ps[:, 4, at:at + 2], ada_rows[:, u, j * P:j * P + P], pick, start=True, stop=True)
                ins.then_inc(ada_psum, 1)

            def quarter_sums(bank, at, sq, n_tok, first=True, last=True, mat=ones):
                n = n_tok // 4
                for g in range(4):
                    ins = mm(ps[32 * g:32 * g + 32, bank, at:at + n], mat, sq[:, g * n:g * n + n],
                             start=first, stop=last)
                return ins

            def spread(banks, inv, n_tok, halves=1):
                n, m = n_tok // 4, P // halves
                for i in range(halves):
                    for g in range(4):
                        col = 2 * g + i
                        for bank, t0, t1 in ((banks[0], 0, S), (banks[1], S, T)):
                            a, b = max(t0, g * n), min(t1, g * n + n)
                            if a < b:
                                ins = mm(ps[m * i:m * i + m, bank, a - t0:b - t0],
                                         quarter[:, col:col + 1].to_broadcast([P, m]), inv[:, a - g * n:b - g * n],
                                         start=True, stop=True)
                return ins

            def mean_square():
                pe.wait_ge(sq_added, c.next(sq_added, KD))
                quarter_sums(7, L, ssum, T).then_inc(ms_full, 1)
                pe.wait_ge(rms_ready, c.next(rms_ready))
                spread((6, 7), rms, T).then_inc(rms_full, 1)

            def ffn(n_streams, ada_halves, ada_first, slot, gate_units=0):
                streams = STREAMS[:n_streams]

                def up(j, s, first=False, wait_hid=True, y_left=0, wait_ada=False):
                    pe.wait_ge(w_ready[s], c.next(w_ready[s]))
                    if wait_hid:
                        pe.wait_ge(hid_done, c.next(hid_done))
                    if wait_ada:
                        pe.wait_ge(ada_evac, c.next(ada_evac))
                    groups = [(1, 3 * j + 1, 0, STREAMS[0]), (0, 3 * j, 0, STREAMS[0])] + \
                        [(0, 3 * j + 2, 0, STREAMS[1]), (1, 3 * j + 2, L, STREAMS[1])] * (n_streams - 1)
                    if first:
                        for k in range(KD):
                            pe.wait_ge(xn_ready, c.next(xn_ready))
                            for half, bank, col, (t0, n) in groups[:2]:
                                ins = three(ps[:, bank, col:col + n], w(s, k * 256 + half * P), xn(k, t0, n),
                                            k == 0, k == KD - 1)
                        groups = groups[2:]
                    for g, (half, bank, col, (t0, n)) in enumerate(groups):
                        if g == 1 and y_left:
                            pe.wait_ge(y_added, c.next(y_added, y_left))
                        for k in range(KD):
                            ins = three(ps[:, bank, col:col + n], w(s, k * 256 + half * P), xn(k, t0, n),
                                        k == 0, k == KD - 1)
                    ins.then_inc(glu_full, 1)

                def down(par, s, tail=False, ada_at=None):
                    pe.wait_ge(w_ready[s], c.next(w_ready[s]))
                    pe.wait_ge(hid_ready, c.next(hid_ready, 2))
                    for m in range(KD):
                        if m in (1, 2) and not tail:
                            pe.wait_ge(hid_done, c.ahead(hid_done, m))
                        if m >= 3:
                            pe.wait_ge(y_added, c.next(y_added))
                        for i, (t0, n) in enumerate(streams):
                            for kk in range(2):
                                ins = three(ps[:, Y_SETS[m % 3][i], 0:n], w(s, kk * D + m * P),
                                            (hidh[:, par, kk, t0:t0 + n], hidl[:, par, kk, t0:t0 + n]), kk == 0, kk == 1)
                        ins.then_inc(y_full, 1)
                        if m == 3 and ada_at is not None:
                            ada_sums(ada_at)
                    if ada_at is not None:
                        ada_turn()

                s0, s1 = slot, 1 - slot
                up(0, s0, first=True, wait_hid=False)
                up(1, s1, wait_hid=False)
                if ada_halves:
                    pe.wait_ge(hid_done, c.ahead(hid_done, 2))
                    for g in range(0, gate_units, ADA_PER):
                        ada_sums(ada_first - gate_units + g)
                        ada_turn()
                        pe.wait_ge(ada_evac, c.next(ada_evac))
                    ada_sums(ada_first)
                    ada_turn()
                    if ada_halves == 1:
                        pe.wait_ge(ada_evac, c.next(ada_evac))

                per = {w_ready[0]: 3, w_ready[1]: 3, hid_done: 4, y_added: 16, hid_ready: 4}
                if ada_halves:
                    per.update({ada_full[0]: 16 * ada_halves, ada_full[1]: 16 * ada_halves, ada_row: ada_halves,
                                ada_evac: ada_halves})
                with c.loop(pe, BLOCKS // 2, per):
                    up(0, s0)
                    up(1, s1, wait_ada=ada_halves == 2)
                    down(0, s0, ada_at=ada_first + ADA_PER if ada_halves else None)
                    up(0, s1, y_left=3)
                    up(1, s0, wait_ada=ada_halves > 0)
                    down(1, s1, ada_at=ada_first + 2 * ADA_PER if ada_halves == 2 else None)
                    pe.wait_ge(y_added, c.next(y_added, 3))
                down(0, s0, tail=True)
                pe.wait_ge(y_added, c.next(y_added, 3))
                c.next(hid_done, 2)
                if ada_halves == 2:
                    pe.wait_ge(ada_evac, c.next(ada_evac))
                return 1 - slot

            def ada_batch(first):
                ada_sums(first)
                ada_turn()
                pe.wait_ge(ada_evac, c.next(ada_evac))

            pe.wait_ge(loaded, 32)
            pe.wait_ge(setup_done, c.next(setup_done))
            for g in range(0, ADA_FIRST - ADA_GATE, ADA_PER):
                ada_batch(g)
            mean_square()
            slot = ffn(2, 2, ADA_0, 0, ADA_GATE)
            ada_batch(ADA_1 - ADA_PER)
            mean_square()

            sets = ((0, 1), (2, 3), (4, 5))

            def project(n_item, lhs, rhs, ks):
                for i, (t0, n) in enumerate(STREAMS):
                    for k in range(ks):
                        ins = three(ps[:, sets[n_item % 3][i], 0:n], lhs(k), rhs(k, t0, n), k == 0, k == ks - 1)
                ins.then_inc(item_full, 1)

            def item_sum(bank, at=L, first=True, last=True, mat=ones):
                pe.wait_ge(item_sq, c.next(item_sq))
                quarter_sums(bank, at, sqb, T, first, last, mat).then_inc(item_ms, 1)

            def item_spread(halves=1):
                pe.wait_ge(item_inv, c.next(item_inv))
                spread((6, 7), irms[:], T, halves).then_inc(item_rms, 1)

            def w_in(s, j):
                return lambda k: w(s, k * 256 + j * P)

            s0, s1 = slot, 1 - slot
            pe.wait_ge(w_ready[s0], c.next(w_ready[s0]))
            for k in range(KD):
                pe.wait_ge(xn_ready, c.next(xn_ready))
                for n_item in range(2):
                    for i, (t0, n) in enumerate(STREAMS):
                        ins = three(ps[:, sets[n_item][i], 0:n], w_in(s0, n_item)(k), xn(k, t0, n), k == 0, k == KD - 1)
                    if k == KD - 1:
                        ins.then_inc(item_full, 1)
            item_sum(6, 0, True, False)
            pe.wait_ge(w_ready[s1], c.next(w_ready[s1]))
            project(2, w_in(s1, 0), xn, KD)
            item_sum(6, 0, False, False)
            item_sum(6, 0, False, True)
            item_spread()
            project(3, w_in(s1, 1), xn, KD)
            pe.wait_ge(w_ready[s0], c.next(w_ready[s0]))
            project(4, w_in(s0, 0), xn, KD)
            item_sum(3, L, True, False)
            project(5, w_in(s0, 1), xn, KD)
            item_sum(3, L, False, True)
            pe.wait_ge(item_v, c.next(item_v, 3))
            item_spread()
            item_sum(5)
            pe.wait_ge(item_v, c.next(item_v, 2))
            item_spread()
            pe.wait_ge(item_v, c.next(item_v))
            mm(ps[:, 6, :], swap, nrm[:, 0, 0:S], start=True, stop=True).then_inc(item_swapped, 1)
            pe.wait_ge(item_ready, c.next(item_ready, 6))
            c.next(item_rot)
            slot = s1

            tiles = [(hh, q) for hh in range(2) for q in (4, 5, 0, 1, 2, 3)]

            def scores(n, hh, q):
                if n >= 2:
                    pe.wait_ge(exp_done, c.next(exp_done))
                b = 2 * (n % 2)
                qs = slice(q * P, q * P + P)
                for t0, n_key in (STREAMS if q < 4 else STREAMS[1:]):
                    bank = ps[:, b + (t0 > 0), 0:n_key]
                    ks = slice(t0, t0 + n_key)
                    half = slice(ROPE * hh, ROPE * hh + ROPE)
                    three(bank, (qn[:, 0, hh, qs], qn[:, 1, hh, qs]), (kn[:, 0, hh, ks], kn[:, 1, hh, ks]), True, False)
                    ins = three(bank, (qrr[:, 0, qs], qrr[:, 1, qs]), (krr[:, 0, ks], krr[:, 1, ks]), False, True, half)
                ins.then_inc(s_full, 1)

            def turn(n, hh, q):
                pe.wait_ge(p_done, c.next(p_done))
                if n >= 1:
                    pe.wait_ge(pt_ready, c.next(pt_ready))
                for kc in (range(6) if q < 4 else (4, 5)):
                    ins = mm(ps[:, 4 + kc // 4, (kc % 4) * P:(kc % 4) * P + P], nrm[:, n % 2, kc * P:kc * P + P],
                             nrm[:, 2, (n % 2) * P:(n % 2) * P + P], start=True, stop=True)
                ins.then_inc(pt_full, 1)

            def weigh(hh, part):
                keys = (4, 5) if part == 2 else range(6)
                q0, bank, at = ((0, 6, 0), (L, 6, L), (L, 7, 0))[part]
                for kc in keys:
                    ins = three(ps[:, bank, at:at + L], (vv[0][:, kc, hh * DV:hh * DV + DV], vv[1][:, kc, hh * DV:hh * DV + DV]),
                                (pt[0][:, kc, q0:q0 + L], pt[1][:, kc, q0:q0 + L]), kc == keys[0], kc == keys[-1])
                if part:
                    ins.then_inc(o_full, 1)

            s0, s1 = slot, 1 - slot
            with c.loop(pe, PAIRS, {w_ready[0]: 2, w_ready[1]: 2, item_v: 5, item_sq: 5, item_inv: 5,
                                    item_ready: 5, item_rot: 1, v_ready: 3, exp_done: 12, p_done: 12, pt_ready: 12, o_ready: 4,
                                    y_added: 8}):
                pe.wait_ge(w_ready[s0], c.next(w_ready[s0]))
                cq = lambda k, t0, n: (cqn[:, 0, k, t0:t0 + n], cqn[:, 1, k, t0:t0 + n])
                ckv = lambda k, t0, n: (ckvn[:, 0, k, t0:t0 + n], ckvn[:, 1, k, t0:t0 + n])

                project(0, lambda k: w(s0, k * 384 + 256), cq, 3)
                pe.wait_ge(y_added, c.ahead(y_added, 0))
                project(1, lambda k: w(s0, k * 384), cq, 3)
                item_sum(1, mat=ones64)
                project(2, lambda k: w(s0, k * 384 + 128), cq, 3)
                item_spread(halves=2)
                item_sum(3)
                pe.wait_ge(w_ready[s1], c.next(w_ready[s1]))
                pe.wait_ge(item_v, c.next(item_v))
                mm(ps[:, 6, :], swap, nrm[:, 0, 0:S], start=True, stop=True).then_inc(item_swapped, 1)
                project(3, lambda k: w(s1, k * 512), ckv, 2)
                pe.wait_ge(item_rot, c.next(item_rot))
                item_spread()
                item_sum(5)
                project(4, lambda k: w(s1, k * 512 + P), ckv, 2)
                pe.wait_ge(item_v, c.next(item_v))
                item_spread()
                item_sum(1)

                def value(t):
                    for tc in (2 * t, 2 * t + 1):
                        at = 256 * (tc % 2)
                        for k in range(2):
                            ins = three(ps[:, 4 + t % 2, at:at + 256], ckv(k, tc * P, P), w(s1, k * 512 + 256, 256),
                                        k == 0, k == 1)
                    ins.then_inc(v_full, 1)
                value(0)
                pe.wait_ge(item_v, c.next(item_v))
                item_spread()
                item_sum(3)
                value(1)
                pe.wait_ge(v_ready, c.next(v_ready))
                value(2)
                pe.wait_ge(item_v, c.next(item_v))
                item_spread()
                pe.wait_ge(item_ready, c.next(item_ready, 4))
                scores(0, *tiles[0])
                for n, (hh, q) in enumerate(tiles):
                    if n == 5:
                        pe.wait_ge(item_ready, c.next(item_ready))
                    if n + 1 < len(tiles):
                        scores(n + 1, *tiles[n + 1])
                    if n == 0:
                        pe.wait_ge(v_ready, c.next(v_ready, 2))
                        pe.wait_ge(item_v, c.next(item_v))
                    if q == 1:
                        weigh(hh, 2)
                    if q == 3:
                        weigh(hh, 0)
                    if q == 4 and hh == 1:
                        pe.wait_ge(pt_ready, c.ahead(pt_ready, 1))
                        weigh(0, 1)
                    turn(n, hh, q)
                    if q == 0 and hh == 1:
                        pe.wait_ge(o_ready, c.next(o_ready, 2))

                def project_out(m, kk):
                    if kk == 0 and m >= 3:
                        pe.wait_ge(y_added, c.next(y_added))
                    for i, (t0, n) in enumerate(STREAMS):
                        ins = three(ps[:, Y_SETS[(m + 1) % 3][i], 0:n], w((s0, s1)[kk], m * P),
                                    (oo[0][:, kk, t0:t0 + n], oo[1][:, kk, t0:t0 + n]), kk == 0, kk == 1)
                    if kk == 1:
                        ins.then_inc(y_full, 1)
                    return ins
                pe.wait_ge(w_ready[s0], c.next(w_ready[s0]))
                pe.wait_ge(exp_done, c.next(exp_done, 2))
                project_out(0, 0)
                pe.wait_ge(pt_ready, c.next(pt_ready))
                weigh(1, 1)
                project_out(1, 0)
                pe.wait_ge(w_ready[s1], c.next(w_ready[s1]))
                pe.wait_ge(o_ready, c.next(o_ready, 2))
                for m, kk in ((0, 1), (1, 1), (2, 0), (2, 1), (3, 0), (3, 1), (4, 0), (4, 1), (5, 0), (6, 0), (7, 0)):
                    ins = project_out(m, kk)
                ins.then_inc(wo_used, 1)
                for m in (5, 6, 7):
                    project_out(m, 1)
                pe.wait_ge(y_added, c.next(y_added, 2))
                c.next(y_added)
            mean_square()
            slot = ffn(2, 2, ADA_1, slot)
            mean_square()
            slot = ffn(2, 1, ADA_2, slot)
            ada_batch(ADA_UNITS - ADA_PER)
            mean_square()

            s0, s1 = slot, 1 - slot

            def values(s, bank, t):
                for tc in (2 * t, 2 * t + 1):
                    at = 256 * (tc % 2)
                    for k in range(KD):
                        ins = three(ps[:, bank, at:at + 256], xn(k, tc * P, P), w(s, k * 256, 256), k == 0, k == KD - 1)
                ins.then_inc(v_full, 1)

            def outputs(half):
                for j in range(2):
                    for jc in range(6):
                        ins = three(ps[:, 4 + 2 * half + j, :], (rv[:, 0, jc, j * P:j * P + P], rv[:, 1, jc, j * P:j * P + P]),
                                    (st[:, 0, jc, :], st[:, 1, jc, :]), jc == 0, jc == 5)
                    ins.then_inc(o_full, 1)

            xn_before = c.n[xn_ready.name]
            with c.loop(pe, RET_HEADS, {w_ready[0]: 4, w_ready[1]: 4, v_ready: 6, qk_ready: 2, sc_ready: 6,
                                        osum_ready: 1, cen_done: 1, vsq_added: 4, rms_ready: 1, g_ready: 4, y_added: 16}):
                pe.wait_ge(w_ready[s0], c.next(w_ready[s0]))
                for k in range(KD):
                    pe.wait_ge(xn_ready, xn_before + k + 1)
                    for j in range(2):
                        ins = three(ps[:, j, :], w(s0, k * 256 + j * P), xn(k, 0, S), k == 0, k == KD - 1)
                ins.then_inc(qk_full, 1)
                pe.wait_ge(w_ready[s1], c.next(w_ready[s1]))
                for i, (t0, n) in enumerate(STREAMS):
                    for j in range(2):
                        for k in range(KD):
                            ins = three(ps[:, 2 + 2 * i + j, 0:n], w(s1, k * 256 + j * P), xn(k, t0, n), k == 0, k == KD - 1)
                ins.then_inc(qk_full, 1)
                pe.wait_ge(w_ready[s0], c.next(w_ready[s0]))
                values(s0, 6, 0)
                values(s0, 7, 1)
                pe.wait_ge(v_ready, c.next(v_ready))
                values(s0, 6, 2)
                pe.wait_ge(v_ready, c.next(v_ready, 2))
                pe.wait_ge(qk_ready, c.next(qk_ready, 2))
                for jc in range(6):
                    if jc >= 4:
                        pe.wait_ge(sc_ready, c.next(sc_ready))
                    for k in range(2):
                        ins = three(ps[:, jc % 4, :], (rk[:, 0, k, jc * P:jc * P + P], rk[:, 1, k, jc * P:jc * P + P]),
                                    (rq[:, 0, k, :], rq[:, 1, k, :]), k == 0, k == 1)
                    ins.then_inc(sc_full, 1)
                pe.wait_ge(w_ready[s1], c.next(w_ready[s1]))
                pe.wait_ge(sc_ready, c.next(sc_ready))
                values(s1, 2, 0)
                pe.wait_ge(sc_ready, c.next(sc_ready, 3))
                outputs(0)
                values(s1, 3, 1)
                pe.wait_ge(v_ready, c.next(v_ready))
                values(s1, 2, 2)
                pe.wait_ge(v_ready, c.next(v_ready, 2))
                outputs(1)
                pe.wait_ge(w_ready[s0], c.next(w_ready[s0]))

                def gate(j, s, bank):
                    for k in range(KD):
                        ins = three(ps[:, bank, :], w(s, k * 256 + (j % 2) * P), xn(k, 0, S), k == 0, k == KD - 1)
                    ins.then_inc(g_full, 1)
                gate(0, s0, 2)
                pe.wait_ge(osum_ready, c.next(osum_ready))
                mm(ps[:, 0, :], ones[:, 0:1].to_broadcast([P, P]), rrs[:], start=True, stop=True).then_inc(mu_full, 1)
                gate(1, s0, 3)
                pe.wait_ge(vsq_added, c.next(vsq_added, 4))
                quarter_sums(1, 0, rrs, S).then_inc(var_full, 1)
                pe.wait_ge(w_ready[s1], c.next(w_ready[s1]))
                pe.wait_ge(cen_done, c.next(cen_done))
                gate(2, s1, 4)
                pe.wait_ge(rms_ready, c.next(rms_ready))
                spread((1, None), rrs, S).then_inc(rms_full, 1)
                gate(3, s1, 5)
                for half, s in enumerate((s0, s1)):
                    pe.wait_ge(g_ready, c.next(g_ready, 2))
                    pe.wait_ge(w_ready[s], c.next(w_ready[s]))
                    for n_y in range(KD * half, KD * half + KD):
                        if n_y >= 3:
                            pe.wait_ge(y_added, c.next(y_added))
                        for kk in range(2):
                            ins = three(ps[:, Y_SETS[n_y % 3][0], :], w(s, kk * D + (n_y % KD) * P),
                                        (st[:, 0, 2 * half + kk, :], st[:, 1, 2 * half + kk, :]), kk == 0, kk == 1)
                        ins.then_inc(y_full, 1)
                pe.wait_ge(y_added, c.next(y_added, 3))
            c.next(xn_ready, KD)
            mean_square()
            ffn(1, 0, 0, slot)

        @block.scalar
        def _(act):
            c = Count()
            fn = nc.scalar.activation

            def split_hi(s, n=UNIT):
                act.wait_ge(raw_full[s], c.next(raw_full[s], 16))
                fn(wh[:, s, 0:n], raw[:, s, 0:n], ACT.Copy).then_inc(w_hi[s], 1)

            def ada_copy():
                act.wait_ge(ada_used, c.next(ada_used, ADA_PER))
                fn(ada_rows[:].rearrange("p u e -> p (u e)"), ps[:, 1, :], ACT.Copy).then_inc(ada_row, 1)

            def squares(m, wait_h=True):
                if wait_h:
                    act.wait_ge(y_added, c.next(y_added))
                if m >= 2:
                    act.wait_ge(sq_added, c.next(sq_added))
                fn(act_buf[:, m % 2, :], h[:, m, :], ACT.Square).then_inc(sq_done, 1)

            def norm(layer, k, n_y=None):
                if n_y is not None:
                    c.next(y_added, n_y - KD)
                    for m in range(KD):
                        squares(m)
                c.next(sq_added, 2)
                act.wait_ge(ms_full, c.next(ms_full))
                fn(rms[:], ps[:, 7, L:L + T // 4], ACT.Sqrt, bias=eps[:, 0:1], scale=1.0 / D).then_inc(std_done, 1)
                shift = mod_col(layer, 3 * k)
                for m in range(KD):
                    act.wait_ge(prod_done, c.next(prod_done))
                    for i, (t0, n) in enumerate(STREAMS):
                        ins = fn(xnh[:, m, t0:t0 + n], act_buf[:, m % 2, t0:t0 + n], ACT.Identity, bias=shift[:, m, i:i + 1])
                    ins.then_inc(xn_hi, 1)

            def ffn(n_streams, slot, ada_halves=0, gate_units=0, last=False):
                n_tok = (S, T)[n_streams - 1]

                def up(j, par, s, wait_buf=True, refill=True):
                    act.wait_ge(glu_full, c.next(glu_full))
                    if wait_buf:
                        act.wait_ge(hid_ready, c.next(hid_ready))
                    ins = fn(act_buf[:, j, 0:S], ps[:, 3 * j, :], ACT.Silu)
                    if n_streams == 2:
                        ins = fn(act_buf[:, j, S:T], ps[:, 3 * j + 2, 0:L], ACT.Silu)
                    ins.then_inc(silu_done, 1)
                    act.wait_ge(hid_done, c.next(hid_done))
                    fn(hidh[:, par, j, 0:n_tok], act_buf[:, j, 0:n_tok], ACT.Copy).then_inc(hid_hi, 1)
                    if refill:
                        split_hi(s)

                def down(s, refill=True, ada=False):
                    if ada:
                        ada_copy()
                    act.wait_ge(y_full, c.next(y_full, KD))
                    if refill:
                        split_hi(s)

                s0, s1 = slot, 1 - slot
                up(0, 0, s0, wait_buf=False)
                up(1, 0, s1, wait_buf=False)
                for g in range(0, gate_units, ADA_PER):
                    ada_copy()
                if ada_halves:
                    ada_copy()
                loops = BLOCKS // 2 - (1 if last else 0)

                def body(refill=True):
                    up(0, 1, s0)
                    up(1, 1, s1)
                    down(s0, ada=ada_halves > 0)
                    up(0, 0, s1)
                    up(1, 0, s0, refill=refill)
                    down(s1, refill=refill, ada=ada_halves == 2)
                per = {glu_full: 4, hid_ready: 4, hid_done: 4, y_full: 16, raw_full[0]: 48, raw_full[1]: 48}
                if ada_halves:
                    per[ada_used] = ADA_PER * ada_halves
                with c.loop(act, loops, per):
                    body()
                if last:
                    up(0, 1, s0)
                    up(1, 1, s1)
                    down(s0)
                    up(0, 0, s1)
                    up(1, 0, s0)
                    down(s1, refill=False)
                if last:
                    return
                act.wait_ge(hid_ready, c.next(hid_ready, 2))
                c.next(y_added, KD * (BLOCKS - 1))
                for m in range(KD):
                    squares(m)
                down(s0)
                return 1 - slot

            act.wait_ge(loaded, 32)
            act.wait_ge(dve_step, c.next(dve_step, 2))
            fn(c_act[:, :, 0:2], v("c").rearrange("p (k j) -> p k j", j=2), ACT.Silu).then_inc(setup_done, 1)
            fn(lg[:, 0, :], v("log1m"), ACT.Exp).then_inc(lg_step, 1)
            act.wait_ge(lg_step, c.next(lg_step, 2))
            fn(lg[:, 2, :], lg[:, 1, :], ACT.Ln).then_inc(lg_step, 1)
            c.next(lg_step)
            for g in range(0, ADA_FIRST - ADA_GATE, ADA_PER):
                ada_copy()
                if g == 0:
                    act.wait_ge(x_loaded, 16)
                for m in (g, g + 1):
                    squares(m, False)
                if g == 2:
                    split_hi(0)
                if g == 4:
                    split_hi(1)
            norm(0, 0)
            slot = ffn(2, 0, 2, ADA_GATE)
            ada_copy()
            norm(0, 1)

            s0, s1 = slot, 1 - slot
            sets = ((0, 1), (2, 3), (4, 5))

            def square(n_item, row, n_ready=0):
                act.wait_ge(item_full, c.next(item_full))
                if n_ready:
                    act.wait_ge(item_ready, c.next(item_ready, n_ready))
                if c.n.get(item_ms.name):
                    act.wait_ge(item_ms, c.ahead(item_ms, 0))
                fn(nrm[:, row, 0:S], ps[:, sets[n_item % 3][0], :], ACT.Copy)
                fn(nrm[:, row, S:T], ps[:, sets[n_item % 3][1], 0:L], ACT.Copy)
                fn(sqb[:, 0:S], ps[:, sets[n_item % 3][0], :], ACT.Square)
                fn(sqb[:, S:T], ps[:, sets[n_item % 3][1], 0:L], ACT.Square).then_inc(item_sq, 1)

            def root(dim, bank, at=L, n_ms=1):
                act.wait_ge(item_ms, c.next(item_ms, n_ms))
                fn(irms[:], ps[:, bank, at:at + T // 4], ACT.Sqrt, bias=eps[:, 0:1], scale=1.0 / dim
                   ).then_inc(item_std, 1)

            def hi(dst, src, wait=item_v):
                act.wait_ge(wait, c.next(wait))
                fn(dst, src, ACT.Copy).then_inc(item_hi, 1)

            square(0, 1)
            c.next(item_ms)
            square(1, 2)
            split_hi(s0)
            c.next(item_ms)
            square(2, 0)
            root(Q_RANK, 6, 0)
            for k in range(3):
                hi(cqn[:, 0, k, :], nrm[:, (1, 2, 0)[k], :])
                if k == 0:
                    square(3, 1, 1)
                    split_hi(s1)
                if k == 1:
                    c.next(item_ms)
                    square(4, 2, 1)
            root(KV_RANK, 3)
            square(5, 0, 1)
            split_hi(s0)
            hi(ckvn[:, 0, 0, :], nrm[:, 1, :])
            hi(ckvn[:, 0, 1, :], nrm[:, 2, :])
            root(2 * ROPE, 5)
            c.next(item_v)
            hi(krr[:, 0, :], nrm[:, 0, :], item_rot)
            act.wait_ge(item_ready, c.next(item_ready, 3))
            slot = s1

            tiles = [(hh, q) for hh in range(2) for q in (4, 5, 0, 1, 2, 3)]

            def exponent(n, hh, q):
                act.wait_ge(max_done, c.next(max_done))
                b, e = n % 2, n % 2
                cols = (0, T) if q < 4 else (S, T)
                flat = ps[:, 2 * b:2 * b + 2, :].rearrange("p b t -> p (b t)")
                fn(nrm[:, e, cols[0]:cols[1]], flat[:, cols[0]:cols[1]], ACT.Exp, bias=row[:, 0, b:b + 1],
                   accum_out=row[:, 1, b:b + 1]).then_inc(exp_done, 1)

            def turned(n, hh, q):
                act.wait_ge(pt_full, c.next(pt_full))
                if q < 4:
                    fn(pt[0][:, 0:4, q * P:q * P + P], ps[:, 4, :].rearrange("p (k q) -> p k q", k=4), ACT.Copy)
                q0 = q * P if q < 4 else L + (q - 4) * P
                fn(pt[0][:, 4:6, q0:q0 + P], ps[:, 5, 0:256].rearrange("p (k q) -> p k q", k=2), ACT.Copy
                   ).then_inc(pt_hi, 1)

            def attended(hh, context):
                act.wait_ge(o_full, c.next(o_full))
                t0, n = STREAMS[context]
                fn(oo[0][:, hh, t0:t0 + n], ps[:, 6 + context, 0:n], ACT.Copy).then_inc(o_hi, 1)

            s0, s1 = slot, 1 - slot
            with c.loop(act, PAIRS, {item_full: 5, item_ms: 5, item_v: 5, item_ready: 5, item_rot: 1, v_full: 3, max_done: 12,
                                     pt_full: 12, o_full: 4, wo_used: 1, y_full: 8, raw_full[0]: 32, raw_full[1]: 32}):
                square(0, 0)
                root(ROPE, 1)
                square(1, 1)
                root(NOPE, 3)
                square(2, 2)
                split_hi(s0, 1024)
                c.next(item_v)
                hi(qrr[:, 0, :], nrm[:, 0, :], item_rot)
                root(NOPE, 5)
                hi(qn[:, 0, 0, :], nrm[:, 1, :])
                square(3, 0, 1)
                root(NOPE, 1)
                hi(qn[:, 0, 1, :], nrm[:, 2, :])
                square(4, 1, 1)

                def value(t):
                    act.wait_ge(v_full, c.next(v_full))
                    fn(vv[0][:, 2 * t:2 * t + 2, :], two_tiles(4 + t % 2), ACT.Copy).then_inc(v_hi, 1)
                value(0)
                root(NOPE, 3)
                value(1)
                hi(kn[:, 0, 0, :], nrm[:, 0, :])
                value(2)
                exponent(0, *tiles[0])
                hi(kn[:, 0, 1, :], nrm[:, 1, :])
                c.next(item_ready, 3)
                for n, (hh, q) in enumerate(tiles):
                    if n + 1 < len(tiles):
                        exponent(n + 1, *tiles[n + 1])
                    if q == 1:
                        attended(hh, 1)
                    if q == 4 and hh == 1:
                        attended(0, 0)
                    turned(n, hh, q)
                    if n == 2:
                        split_hi(s1, 1024)
                attended(1, 0)
                act.wait_ge(wo_used, c.next(wo_used))
                split_hi(s0)
                act.wait_ge(y_full, c.next(y_full, KD))
                split_hi(s1)
            norm(0, 2, KD * PAIRS)
            slot = ffn(2, slot, 2)
            norm(1, 0)
            slot = ffn(2, slot, 1)
            ada_copy()
            norm(1, 1)

            s0, s1 = slot, 1 - slot

            def part(wait, done, dst, src):
                act.wait_ge(wait, c.next(wait))
                fn(dst, src, ACT.Copy).then_inc(done, 1)

            with c.loop(act, RET_HEADS, {dec_done: 1, qk_full: 2, qk_val: 4, v_full: 6, sc_val: 6, o_full: 4, cen_done: 1,
                                         vsq_added: 4, var_full: 1, g_full: 4, g_val: 4, y_full: 16,
                                         raw_full[0]: 64, raw_full[1]: 64}):
                act.wait_ge(dec_done, c.next(dec_done))
                fn(dec_lat, dec_lat, ACT.Exp)
                fn(dec_ctx, dec_ctx, ACT.Exp)
                fn(rt_flat[:, 0:640], rt_flat[:, 0:640], ACT.Exp).then_inc(dec_exp, 1)
                act.wait_ge(qk_full, c.next(qk_full))
                split_hi(s0)
                for j in range(2):
                    part(qk_val, qk_hi, rq[:, 0, j, :], rt[:, j, :])
                act.wait_ge(qk_full, c.next(qk_full))
                split_hi(s1)
                fn(rk[:, 0, 0, S:T], ps[:, 4, 0:L], ACT.Copy)
                fn(rk[:, 0, 1, S:T], ps[:, 5, 0:L], ACT.Copy).then_inc(qk_hi, 1)
                for j in range(2):
                    part(qk_val, qk_hi, rk[:, 0, j, 0:S], rt[:, j, :])
                for t in range(3):
                    part(v_full, v_hi, rv[:, 0, 2 * t:2 * t + 2, :], two_tiles(6 + t % 2))
                split_hi(s0)
                for jc in range(6):
                    part(sc_val, sc_hi, st[:, 0, jc, :], rt[:, jc % 2, :])
                act.wait_ge(o_full, c.next(o_full, 2))
                for t in range(3):
                    part(v_full, v_hi, rv[:, 0, 2 * t:2 * t + 2, :], two_tiles(2 + t % 2))
                split_hi(s1)
                c.next(o_full, 2)
                act.wait_ge(cen_done, c.next(cen_done))
                for j in range(4):
                    if j >= 2:
                        act.wait_ge(vsq_added, c.next(vsq_added))
                    fn(rt[:, j % 2, :], dec[:, j, :], ACT.Square).then_inc(vsq_done, 1)
                c.next(vsq_added, 2)
                act.wait_ge(var_full, c.next(var_full))
                fn(rrs[:, 0:P], ps[:, 1, 0:P], ACT.Sqrt, bias=eps[:, 0:1], scale=1.0 / RET_DV).then_inc(rstd_done, 1)
                for j in range(4):
                    act.wait_ge(g_full, c.next(g_full))
                    fn(rt[:, 2, :], ps[:, 2 + j, :], ACT.Silu).then_inc(g_silu, 1)
                    if j in (1, 3):
                        split_hi((s0, s1)[j // 2])
                    part(g_val, g_hi, st[:, 0, j, :], dec[:, j, :])
                for s in (s0, s1):
                    act.wait_ge(y_full, c.next(y_full, KD))
                    split_hi(s)
            norm(1, 2, 2 * KD * RET_HEADS)
            ffn(1, slot, last=True)

        @block.vector
        def _(dve):
            c = Count()
            tt, ts, stt = nc.vector.tensor_tensor, nc.vector.tensor_scalar, nc.vector.scalar_tensor_tensor

            def split_lo(s, n=UNIT):
                dve.wait_ge(w_hi[s], c.next(w_hi[s]))
                tt(wl[:, s, 0:n], raw[:, s, 0:n], wh[:, s, 0:n].bitcast(F32), ALU.subtract).then_inc(w_ready[s], 1)

            def step(ins):
                ins.then_inc(dve_step, 1)
                dve.wait_ge(dve_step, c.next(dve_step))

            def ada_out(chunk, n=ADA_PER):
                dve.wait_ge(ada_psum, c.next(ada_psum))
                b0 = _cols["ada_b"][0]
                at = slice(chunk, chunk + 2 * n) if isinstance(chunk, int) else bass.ds(chunk, 2 * n)
                bias = vec[:, b0:b0 + 2 * N_MOD * KD].rearrange("p (k j) -> p k j", j=1)[:, at, :]
                tt(mods[:, at, :], ps[:, 4, 256:256 + 4 * n].rearrange("p (k j) -> p k j", j=2),
                   bias.to_broadcast([P, 2 * n, 2]), ALU.add).then_inc(ada_evac, 1)

            def gate_coefs(layer, k):
                step(ts(coef[:, 1, :, :], mod_col(layer, 3 * k + 2), 0.5 if k != 1 else 1.0, None, ALU.mult))

            def coefs(layer, k):
                g0 = _cols["norm_g"][0] + (layer * 3 + k) * 2 * KD
                gain = vec[:, g0:g0 + 2 * KD].rearrange("p (k j) -> p k j", j=2)
                step(stt(out=coef[:, 0, :, :], in0=mod_col(layer, 3 * k + 1), scalar=1.0, in1=gain,
                         op0=ALU.add, op1=ALU.mult))

            def add_square(m):
                dve.wait_ge(sq_done, c.next(sq_done))
                if m == 0:
                    nc.vector.tensor_copy(ssum[:], act_buf[:, 0, :]).then_inc(sq_added, 1)
                else:
                    dve.wait_ge(sq_added, c.next(sq_added))
                    tt(ssum[:], ssum[:], act_buf[:, m % 2, :], ALU.add).then_inc(sq_added, 1)

            def norm(layer, k, sums=False, gate=True):
                if sums:
                    for m in range(KD):
                        add_square(m)
                c.next(sq_added)
                coefs(layer, k)
                if gate:
                    gate_coefs(layer, k)
                dve.wait_ge(std_done, c.next(std_done))
                nc.vector.reciprocal(rms[:], rms[:]).then_inc(rms_ready, 1)
                dve.wait_ge(rms_full, c.next(rms_full))
                shift = mod_col(layer, 3 * k)
                for m in range(KD + 1):
                    if m < KD:
                        if m >= 2:
                            dve.wait_ge(xn_ready, c.next(xn_ready))
                        for i, (t0, n) in enumerate(STREAMS):
                            ins = stt(out=act_buf[:, m % 2, t0:t0 + n], in0=h[:, m, t0:t0 + n], scalar=coef[:, 0, m, i:i + 1],
                                      in1=ps[:, 6 + i, 0:n], op0=ALU.mult, op1=ALU.mult)
                        ins.then_inc(prod_done, 1)
                    if m >= 1:
                        dve.wait_ge(xn_hi, c.next(xn_hi))
                        for i, (t0, n) in enumerate(STREAMS):
                            ins = stt(out=xnl[:, m - 1, t0:t0 + n], in0=act_buf[:, (m - 1) % 2, t0:t0 + n],
                                      scalar=shift[:, m - 1, i:i + 1], in1=xnh[:, m - 1, t0:t0 + n].bitcast(F32),
                                      op0=ALU.add, op1=ALU.subtract)
                        ins.then_inc(xn_ready, 1)
                c.next(xn_ready, 2)

            def add_y(m, n_streams, n_y=None):
                n_y = m if n_y is None else n_y
                dve.wait_ge(y_full, c.next(y_full))
                for i, (t0, n) in enumerate(STREAMS[:n_streams]):
                    bank = Y_SETS[n_y % 3][i]
                    ins = stt(out=h[:, m, t0:t0 + n], in0=ps[:, bank, 0:n], scalar=coef[:, 1, m, i:i + 1],
                              in1=h[:, m, t0:t0 + n], op0=ALU.mult, op1=ALU.add)
                ins.then_inc(y_added, 1)

            def ffn(n_streams, slot, ada_halves=0, ada_first=0, gate_units=0, last=False):
                n_tok = (S, T)[n_streams - 1]

                def up(j, par, s=None):
                    dve.wait_ge(silu_done, c.next(silu_done))
                    ins = tt(act_buf[:, j, 0:S], act_buf[:, j, 0:S], ps[:, 3 * j + 1, :], ALU.mult)
                    if n_streams == 2:
                        ins = tt(act_buf[:, j, S:T], act_buf[:, j, S:T], ps[:, 3 * j + 2, L:2 * L], ALU.mult)
                    ins.then_inc(hid_done, 1)
                    dve.wait_ge(hid_hi, c.next(hid_hi))
                    tt(hidl[:, par, j, 0:n_tok], act_buf[:, j, 0:n_tok], hidh[:, par, j, 0:n_tok].bitcast(F32),
                       ALU.subtract).then_inc(hid_ready, 1)
                    if s is not None:
                        split_lo(s)

                def down(s, s_mid=None, square=False):
                    for m in range(KD):
                        add_y(m, n_streams)
                        if square and m:
                            add_square(m - 1)
                        if m == 3 and s_mid is not None:
                            split_lo(s_mid)
                    if square:
                        add_square(KD - 1)
                    if s is not None:
                        split_lo(s)

                s0, s1 = slot, 1 - slot
                up(0, 0, s0)
                up(1, 0, s1)
                for g in range(0, gate_units, ADA_PER):
                    ada_out(2 * (ada_first - gate_units + g))
                if gate_units:
                    dve.wait_ge(ada_evac, c.ahead(ada_evac, gate_units // ADA_PER))
                    gate_coefs(0, 0)
                if ada_halves:
                    ada_out(2 * ada_first)
                per = {silu_done: 4, hid_hi: 4, w_hi[0]: 3, w_hi[1]: 3, y_full: 16}
                if ada_halves:
                    per[ada_psum] = ada_halves
                stride = 2 * ADA_PER * ada_halves
                with c.loop(dve, BLOCKS // 2 - (1 if last else 0), per) as i:
                    up(0, 1, s0)
                    up(1, 1)
                    down(s0, s1)
                    if ada_halves:
                        ada_out(i * stride + 2 * (ada_first + ADA_PER))
                    up(0, 0, s1)
                    up(1, 0)
                    down(s1, s0)
                    if ada_halves == 2:
                        ada_out(i * stride + 2 * (ada_first + 2 * ADA_PER))
                if last:
                    up(0, 1, s0)
                    up(1, 1)
                    down(s0, s1)
                    up(0, 0, s1)
                    up(1, 0)
                    down(None, s0)
                down(None if last else s0, square=not last)
                return 1 - slot

            step(nc.vector.memset(eps[:], EPS))
            step(nc.vector.memset(c_act[:], 0.0))
            dve.wait_ge(loaded, 32)
            a, b = _cols["qg_nope"][0], _cols["qg_rope"][1]
            step(ts(vec[:, a:b], vec[:, a:b], (NOPE + ROPE) ** -0.5, None, ALU.mult))
            dve.wait_ge(lg_step, c.next(lg_step))
            ts(lg[:, 1, :], lg[:, 0, :], -1.0, 1.0, ALU.mult, ALU.add).then_inc(lg_step, 1)
            dve.wait_ge(lg_step, c.next(lg_step, 2))
            step(ts(lg[:, 3, :], lg[:, 1, :], 1.0, None, ALU.is_equal))
            stt(out=lg[:, 4, :], in0=lg[:, 1, :], scalar=-1.0, in1=lg[:, 3, :], op0=ALU.add, op1=ALU.add)
            step(tt(lg[:, 2, :], lg[:, 2, :], lg[:, 3, :], ALU.add))
            step(nc.vector.reciprocal(lg[:, 4, :], lg[:, 4, :]))
            step(tt(lg[:, 2, :], lg[:, 2, :], lg[:, 4, :], ALU.mult))
            step(tt(lg[:, 2, :], lg[:, 2, :], lg[:, 0, :], ALU.mult))
            step(ts(lg[:, 1, :], lg[:, 2, :], -1.0, None, ALU.mult))
            assert ADA_FIRST - ADA_GATE == KD
            for g in range(0, ADA_FIRST - ADA_GATE, ADA_PER):
                ada_out(2 * g)
                for m in (g, g + 1):
                    add_square(m)
                if g == 2:
                    split_lo(0)
                if g == 4:
                    split_lo(1)
            dve.wait_ge(ada_evac, c.next(ada_evac, (ADA_FIRST - ADA_GATE) // ADA_PER))
            norm(0, 0, gate=False)
            slot = ffn(2, 0, 2, ADA_0, ADA_GATE)
            ada_out(2 * (ADA_1 - ADA_PER))
            dve.wait_ge(ada_evac, c.next(ada_evac, ADA_GATE // ADA_PER + BLOCKS + 1))
            norm(0, 1)

            s0, s1 = slot, 1 - slot
            sets = ((0, 1), (2, 3), (4, 5))
            gate_cols = {n: v(n) for n in ("q_norm", "kv_norm", "qg_nope", "qg_rope", "kg_nope", "kg_rope")}

            def inverse():
                dve.wait_ge(item_std, c.next(item_std))
                nc.vector.reciprocal(irms[:], irms[:]).then_inc(item_inv, 1)

            def scaled(row, gain, spread=True):
                if spread:
                    dve.wait_ge(item_rms, c.next(item_rms))
                for i, (t0, n) in enumerate(STREAMS):
                    ins = stt(out=nrm[:, row, t0:t0 + n], in0=nrm[:, row, t0:t0 + n], scalar=gain,
                              in1=ps[:, 6 + i, 0:n], op0=ALU.mult, op1=ALU.mult)
                ins.then_inc(item_v, 1)

            def lo(dst, hi_part, src):
                dve.wait_ge(item_hi, c.next(item_hi))
                tt(dst, src, hi_part.bitcast(F32), ALU.subtract).then_inc(item_ready, 1)

            def rotated(i):
                dve.wait_ge(item_swapped, c.next(item_swapped))
                tt(nrm[:, i, 0:S], nrm[:, i, 0:S], cs[:, 0, :], ALU.mult)
                step(tt(ps[:, 6, :], ps[:, 6, :], cs[:, 1, :], ALU.mult))
                tt(nrm[:, i, 0:S], nrm[:, i, 0:S], ps[:, 6, :], ALU.add).then_inc(item_rot, 1)

            split_lo(s0)
            inverse()
            g = gate_cols["q_norm"]
            for k, i_out in enumerate((1, 2, 0)):
                scaled(i_out, g[:, k:k + 1], k == 0)
                if k:
                    lo(cqn[:, 1, k - 1, :], cqn[:, 0, k - 1, :], nrm[:, k, :])
            split_lo(s1)
            lo(cqn[:, 1, 2, :], cqn[:, 0, 2, :], nrm[:, 0, :])
            inverse()
            g = gate_cols["kv_norm"]
            for k, i_out in enumerate((1, 2)):
                scaled(i_out, g[:, k:k + 1], k == 0)
                lo(ckvn[:, 1, k, :], ckvn[:, 0, k, :], nrm[:, i_out, :])
            split_lo(s0)
            inverse()
            scaled(0, gate_cols["kg_rope"])
            dve.wait_ge(tab_full, 16)
            rotated(0)
            lo(krr[:, 1, :], krr[:, 0, :], nrm[:, 0, :])
            slot = s1

            tiles = [(hh, q) for hh in range(2) for q in (4, 5, 0, 1, 2, 3)]

            def maximum(n, hh, q):
                dve.wait_ge(s_full, c.next(s_full))
                b = n % 2
                cols = (0, T) if q < 4 else (S, T)
                flat = ps[:, 2 * b:2 * b + 2, :].rearrange("p b t -> p (b t)")
                nc.vector.tensor_reduce(row[:, 0, b:b + 1], flat[:, cols[0]:cols[1]], AX_X, ALU.max, negate=True
                                        ).then_inc(max_done, 1)

            def diagonal(n, hh, q):
                dve.wait_ge(exp_done, c.next(exp_done))
                b = n % 2
                step(nc.vector.reciprocal(row[:, 2, b:b + 1], row[:, 1, b:b + 1]))
                ts(nrm[:, 2, b * P:b * P + P], ident, row[:, 2, b:b + 1], None, ALU.mult).then_inc(p_done, 1)

            def turned(n, hh, q):
                dve.wait_ge(pt_hi, c.next(pt_hi))
                if q < 4:
                    tt(pt[1][:, 0:4, q * P:q * P + P], ps[:, 4, :].rearrange("p (k q) -> p k q", k=4),
                       pt[0][:, 0:4, q * P:q * P + P].bitcast(F32), ALU.subtract)
                q0 = q * P if q < 4 else L + (q - 4) * P
                tt(pt[1][:, 4:6, q0:q0 + P], ps[:, 5, 0:256].rearrange("p (k q) -> p k q", k=2),
                   pt[0][:, 4:6, q0:q0 + P].bitcast(F32), ALU.subtract).then_inc(pt_ready, 1)

            def attended(hh, context):
                dve.wait_ge(o_hi, c.next(o_hi))
                t0, n = STREAMS[context]
                tt(oo[1][:, hh, t0:t0 + n], ps[:, 6 + context, 0:n], oo[0][:, hh, t0:t0 + n].bitcast(F32),
                   ALU.subtract).then_inc(o_ready, 1)

            s0, s1 = slot, 1 - slot
            with c.loop(dve, PAIRS, {item_std: 5, item_hi: 5, item_swapped: 1, v_hi: 3, s_full: 12, exp_done: 12,
                                     pt_hi: 12, o_hi: 4, y_full: 8, w_hi[0]: 2, w_hi[1]: 2, item_rms: 5,
                                     dve_step: 1 + 12}):
                inverse()
                scaled(0, gate_cols["qg_rope"])
                inverse()
                rotated(0)
                lo(qrr[:, 1, :], qrr[:, 0, :], nrm[:, 0, :])
                scaled(1, gate_cols["qg_nope"])
                inverse()
                lo(qn[:, 1, 0, :], qn[:, 0, 0, :], nrm[:, 1, :])
                scaled(2, gate_cols["qg_nope"])
                inverse()
                lo(qn[:, 1, 1, :], qn[:, 0, 1, :], nrm[:, 2, :])

                def value(t):
                    dve.wait_ge(v_hi, c.next(v_hi))
                    tt(vv[1][:, 2 * t:2 * t + 2, :], two_tiles(4 + t % 2), vv[0][:, 2 * t:2 * t + 2, :].bitcast(F32),
                       ALU.subtract).then_inc(v_ready, 1)
                value(0)
                scaled(0, gate_cols["kg_nope"])
                inverse()
                value(1)
                lo(kn[:, 1, 0, :], kn[:, 0, 0, :], nrm[:, 0, :])
                scaled(1, gate_cols["kg_nope"])
                maximum(0, *tiles[0])
                value(2)
                for n, (hh, q) in enumerate(tiles):
                    diagonal(n, hh, q)
                    if n == 0:
                        lo(kn[:, 1, 1, :], kn[:, 0, 1, :], nrm[:, 1, :])
                    if n + 1 < len(tiles):
                        maximum(n + 1, *tiles[n + 1])
                    if n == 2:
                        split_lo(s0, 1024)
                    if n == 4:
                        split_lo(s1, 1024)
                    if q == 1:
                        attended(hh, 1)
                    if q == 4 and hh == 1:
                        attended(0, 0)
                    turned(n, hh, q)
                attended(1, 0)
                for m in range(KD):
                    if m == 7:
                        split_lo(s0)
                    add_y(m, 2, m + 1)
                split_lo(s1)
            norm(0, 2, sums=True)
            slot = ffn(2, slot, 2, ADA_1)
            dve.wait_ge(ada_evac, c.next(ada_evac, BLOCKS))
            norm(1, 0)
            slot = ffn(2, slot, 1, ADA_2)
            ada_out(2 * (ADA_UNITS - ADA_PER))
            dve.wait_ge(ada_evac, c.next(ada_evac, BLOCKS // 2 + 2))
            norm(1, 1)

            s0, s1 = slot, 1 - slot
            dve.wait_ge(tab_full, 48)
            c.next(o_full, 4 * PAIRS)
            gn0 = _cols["gn"][0]
            with c.loop(dve, RET_HEADS, {dec_exp: 1, qk_full: 2, qk_hi: 5, v_hi: 6, qk_ready: 2, sc_ready: 6, sc_full: 6, sc_hi: 6, o_full: 4,
                                         mu_full: 1, vsq_done: 4, vsq_added: 4, rstd_done: 1, rms_full: 1, g_silu: 4, g_hi: 4, y_full: 16,
                                         w_hi[0]: 4, w_hi[1]: 4, dve_step: 17}) as i:
                lgf, nlgb = lg[:, 1, bass.ds(i, 1)], lg[:, 2, bass.ds(i + RET_HEADS, 1)]
                ts(dec_lat, dist[:], 0.0, lgf, ALU.max, ALU.mult)
                step(ts(rt_flat[:, 0:DIST_W], dist[:], 0.0, nlgb, ALU.min, ALU.mult))
                step(tt(dec_lat, dec_lat, rt_flat[:, 0:DIST_W], ALU.add))
                ts(dec_ctx, dist[:, 256:DIST_W], float(L), lgf, ALU.add, ALU.mult)
                ts(rt_flat[:, 0:640], dist[:, 256:DIST_W], -float(S), nlgb, ALU.add, ALU.mult).then_inc(dec_done, 1)
                dve.wait_ge(dec_exp, c.next(dec_exp))
                step(tt(dec_ctx, dec_ctx, rt_flat[:, 0:640], ALU.add))

                def rotate(b):
                    cos, sin = cr[:, 0, :], cr[:, 1, :]
                    tt(rt[:, 0, :], ps[:, b, :], cos, ALU.mult)
                    step(tt(rt[:, 2, :], ps[:, b + 1, :], sin, ALU.mult))
                    tt(rt[:, 0, :], rt[:, 0, :], rt[:, 2, :], ALU.subtract).then_inc(qk_val, 1)
                    step(tt(rt[:, 1, :], ps[:, b + 1, :], cos, ALU.mult))
                    step(tt(rt[:, 2, :], ps[:, b, :], sin, ALU.mult))
                    tt(rt[:, 1, :], rt[:, 1, :], rt[:, 2, :], ALU.add).then_inc(qk_val, 1)

                dve.wait_ge(qk_full, c.next(qk_full))
                rotate(0)
                for j in range(2):
                    dve.wait_ge(qk_hi, c.next(qk_hi))
                    ins = tt(rq[:, 1, j, :], rt[:, j, :], rq[:, 0, j, :].bitcast(F32), ALU.subtract)
                ins.then_inc(qk_ready, 1)
                split_lo(s0)
                dve.wait_ge(qk_full, c.next(qk_full))
                dve.wait_ge(qk_hi, c.next(qk_hi))
                for j in range(2):
                    tt(rk[:, 1, j, S:T], ps[:, 4 + j, 0:L], rk[:, 0, j, S:T].bitcast(F32), ALU.subtract)
                dve.wait_ge(qk_ready, c.next(qk_ready))
                rotate(2)
                for j in range(2):
                    dve.wait_ge(qk_hi, c.next(qk_hi))
                    ins = tt(rk[:, 1, j, 0:S], rt[:, j, :], rk[:, 0, j, 0:S].bitcast(F32), ALU.subtract)
                ins.then_inc(qk_ready, 1)
                split_lo(s1)

                def value(t, bank):
                    dve.wait_ge(v_hi, c.next(v_hi))
                    tt(rv[:, 1, 2 * t:2 * t + 2, :], two_tiles(bank), rv[:, 0, 2 * t:2 * t + 2, :].bitcast(F32),
                       ALU.subtract).then_inc(v_ready, 1)
                for t in range(3):
                    value(t, 6 + t % 2)
                split_lo(s0)
                dve.wait_ge(qk_ready, c.next(qk_ready))
                for jc in range(7):
                    if jc < 6:
                        if jc >= 2:
                            dve.wait_ge(sc_ready, c.next(sc_ready))
                        dve.wait_ge(sc_full, c.next(sc_full))
                        table = dec_flat[:, 384 - P * jc:384 - P * jc + S] if jc < 4 else \
                            dec_ctx[:, P * (5 - jc):P * (5 - jc) + S]
                        stt(out=rt[:, jc % 2, :], in0=ps[:, jc % 4, :], scalar=RET_DK ** -0.5, in1=table,
                            op0=ALU.mult, op1=ALU.mult).then_inc(sc_val, 1)
                    if jc >= 1:
                        dve.wait_ge(sc_hi, c.next(sc_hi))
                        tt(st[:, 1, jc - 1, :], rt[:, (jc - 1) % 2, :], st[:, 0, jc - 1, :].bitcast(F32),
                           ALU.subtract).then_inc(sc_ready, 1)
                for t in range(3):
                    value(t, 2 + t % 2)
                split_lo(s1)
                c.next(sc_ready, 2)
                dve.wait_ge(o_full, c.next(o_full, 4))
                step(nc.vector.tensor_copy(rrs[:], ps[:, 4, :]))
                step(tt(rrs[:], rrs[:], ps[:, 5, :], ALU.add))
                step(tt(rrs[:], rrs[:], ps[:, 6, :], ALU.add))
                tt(rrs[:], rrs[:], ps[:, 7, :], ALU.add).then_inc(osum_ready, 1)
                dve.wait_ge(mu_full, c.next(mu_full))
                step(ts(rt[:, 2, :], ps[:, 0, :], -1.0 / RET_DV, None, ALU.mult))
                for j in range(4):
                    ins = tt(dec[:, j, :], ps[:, 4 + j, :], rt[:, 2, :], ALU.add)
                ins.then_inc(cen_done, 1)
                for j in range(4):
                    dve.wait_ge(vsq_done, c.next(vsq_done))
                    if j == 0:
                        nc.vector.tensor_copy(rrs[:], rt[:, 0, :]).then_inc(vsq_added, 1)
                    else:
                        dve.wait_ge(vsq_added, c.next(vsq_added))
                        tt(rrs[:], rrs[:], rt[:, j % 2, :], ALU.add).then_inc(vsq_added, 1)
                c.next(vsq_added)
                dve.wait_ge(rstd_done, c.next(rstd_done))
                nc.vector.reciprocal(rrs[:, 0:P], rrs[:, 0:P]).then_inc(rms_ready, 1)
                dve.wait_ge(rms_full, c.next(rms_full))
                for j in range(4):
                    step(stt(out=dec[:, j, :], in0=dec[:, j, :], scalar=vec[:, bass.ds(i * 4 + (gn0 + j), 1)],
                             in1=ps[:, 1, :], op0=ALU.mult, op1=ALU.mult))
                    dve.wait_ge(g_silu, c.next(g_silu))
                    tt(dec[:, j, :], dec[:, j, :], rt[:, 2, :], ALU.mult).then_inc(g_val, 1)
                    if j in (1, 3):
                        split_lo((s0, s1)[j // 2])
                    dve.wait_ge(g_hi, c.next(g_hi))
                    tt(st[:, 1, j, :], dec[:, j, :], st[:, 0, j, :].bitcast(F32), ALU.subtract).then_inc(g_ready, 1)
                for n_y in range(2 * KD):
                    add_y(n_y % KD, 1, n_y)
                    if n_y == KD + 1:
                        split_lo(s0)
                split_lo(s1)
            norm(1, 2, sums=True)
            ffn(1, slot, last=True)


def _chunks(w, n_out):
    i, o = w.shape
    return w.reshape(i // P, P, o // n_out, n_out).transpose(2, 1, 0, 3).reshape(o // n_out, P, -1)


def _rows(w, n_in):
    i, o = w.shape
    return w.reshape(i // (P * n_in), n_in, P, o).transpose(0, 2, 1, 3).reshape(i // (P * n_in), P, -1)


def _pad(u):
    full = np.zeros((u.shape[0], UNIT), u.dtype)
    full[:, :u.shape[1]] = u
    return full


def _ffn_units(w_in, w_out):
    a, b = _chunks(w_in[:, :D_FF], P), _chunks(w_in[:, D_FF:], P)
    up = np.concatenate([a.reshape(-1, P, KD, P), b.reshape(-1, P, KD, P)], 3).reshape(-1, P, UNIT)
    down = _rows(w_out, 2)
    order = [up[0], up[1]]
    for blk in range(1, BLOCKS):
        order += [up[2 * blk], up[2 * blk + 1], down[blk - 1]]
    return order + [down[BLOCKS - 1]]


def _mla_units(w_in, w_uq, w_ukv, w_o):
    w_in = np.concatenate([w_in, w_in[:, Q_RANK + KV_RANK:]], 1)
    order = list(_chunks(w_in, 256))
    uq = w_uq.reshape(Q_RANK, HEADS, NOPE + ROPE)
    ukv = w_ukv.reshape(KV_RANK, HEADS, NOPE + DV)
    for p in range(PAIRS):
        a, b = 2 * p, 2 * p + 1
        q = np.concatenate([uq[:, a, :NOPE], uq[:, b, :NOPE], uq[:, a, NOPE:], uq[:, b, NOPE:]], 1)
        kv = np.concatenate([ukv[:, a, :NOPE], ukv[:, b, :NOPE], ukv[:, a, NOPE:], ukv[:, b, NOPE:]], 1)
        order += [_pad(_rows(q, 3)[0]), _pad(_rows(kv, 2)[0])]
        order += [_pad(w_o[a * P:a * P + P]), _pad(w_o[b * P:b * P + P])]
    return order


def _ret_units(w_in, w_o):
    hdk, hdv = RET_HEADS * RET_DK, RET_HEADS * RET_DV
    u = _chunks(w_in, 256)
    q, k, val, gate = u[:4], u[4:8], u[8:16], u[16:24]
    o = _rows(w_o, 2)
    order = []
    for n in range(RET_HEADS):
        order += [q[n], k[n], val[2 * n], val[2 * n + 1], gate[2 * n], gate[2 * n + 1], o[2 * n], o[2 * n + 1]]
    return order


def _angles(pos, dim):
    inv = (np.float32(10000.0) ** (-np.arange(0, dim, 2, dtype=np.float32) / np.float32(dim))).astype(np.float32)
    return pos.astype(np.float32)[:, None] * inv[None, :]


def _tables():
    mats = np.zeros((P, N_MATS), np.float32)
    mats[:, 2 * P:2 * P + 32] = 1.0
    mats[:64, 2 * P + 32:2 * P + 48] = mats[64:, 2 * P + 48:2 * P + 64] = 1.0
    for p in range(P):
        mats[p ^ 16, p] = 1.0
        mats[p, P + p] = 1.0
        if p % 32 < 2:
            mats[p, 2 * P + 64 + p % 32] = 1.0
        if p % 16 == 0:
            mats[p, 2 * P + 66 + p // 16] = 1.0
    pos = np.arange(S)
    a_row, a_col = _angles(pos // 64, 32), _angles(pos % 64, 32)
    ang = np.concatenate([a_row, a_row, a_col, a_col], 1).T
    sign = np.where((np.arange(64) & 16) == 0, -1.0, 1.0).astype(np.float32)[:, None]
    rope = np.stack([np.cos(ang), np.sin(ang) * sign], 1)
    rope = np.concatenate([rope, rope], 0).astype(np.float32)
    ang = _angles(pos, RET_DK).T
    ret = np.stack([np.cos(ang), np.sin(ang)], 1).astype(np.float32)
    dist = (np.arange(DIST_W)[None, :] - 384 - np.arange(P)[:, None]).astype(np.float32)
    return mats, rope, ret, dist


def kernel(**inputs):
    import concourse.bacc as _bacc
    from concourse.bass_utils import run_bass_kernel_spmd as _run

    a = {k: np.asarray(t) for k, t in inputs.items()}
    units = []
    fi, fo = a["ffn_w_in"], a["ffn_w_out"]
    units += _ffn_units(fi[0, 0], fo[0, 0])
    units += _mla_units(a["mla_w_in"][0], a["mla_w_uq"][0], a["mla_w_ukv"][0], a["mla_w_o"][0])
    units += _ffn_units(fi[0, 1], fo[0, 1]) + _ffn_units(fi[1, 0], fo[1, 0])
    units += _ret_units(a["ret_w_in"][0], a["ret_w_o"][0])
    units += _ffn_units(fi[1, 1], fo[1, 1])
    weights = np.stack(units)
    assert weights.shape == (N_UNITS, P, UNIT)
    ada = np.concatenate([_chunks(a["ada_w"][i], 256) for i in range(2)])

    def col(x):
        return x.reshape(-1, P).T

    def twice(x):
        return np.repeat(col(x), 2, axis=1)
    c2 = np.stack([col(a["c"][0]), col(a["c_ctx"])], 2).reshape(P, -1)
    qg, kg = a["mla_q_gain"][0], a["mla_k_gain"][0]
    vecs = np.concatenate([
        c2, col(a["ada_b"]), twice(a["norm_g"]), col(a["mla_q_norm"][0]), col(a["mla_kv_norm"][0]),
        col(qg[:NOPE]), col(np.concatenate([qg[NOPE:]] * 2)), col(kg[:NOPE]), col(np.concatenate([kg[NOPE:]] * 2)),
        col(a["ret_gn_gain"][0]), np.broadcast_to(a["ret_log1m_gamma"][0].reshape(1, 8), (P, 8))], 1)
    assert vecs.shape == (P, N_VEC)
    x = np.concatenate([a["x"][0], a["ctx"][0]], 0).T.reshape(KD, P, T).transpose(1, 0, 2)
    mats, rope, ret, dist = _tables()
    arrays = {"weights": weights, "ada": ada, "vecs": vecs, "consts": mats, "x_in": x, "rope_mla": rope,
              "rope_ret": ret, "dist_in": dist}
    arrays = {k: np.ascontiguousarray(t) for k, t in arrays.items()}
    nc = _bacc.Bacc("TRN2", target_bir_lowering=False, num_devices=1)
    args = [nc.dram_tensor(k, t.shape, F32, kind="ExternalInput").ap() for k, t in arrays.items()]
    out = nc.dram_tensor("out", (KD, P, S), F32, kind="ExternalOutput").ap()
    build(nc, *args, out)
    r = _run(nc, [arrays], core_ids=[0])
    return np.ascontiguousarray(r.results[0]["out"].reshape(D, S).T)[None]
```
